# Optimizing a Trainium2 kernel written in Bass

```python
import jax, jax.numpy as jnp
from jax import lax
import numpy as np

D_MODEL = 1024
BATCH = 1
SEQ = 512
DEPTH = 2

GRID_W = 64
CTX_LEN = 256
N_MIXERS = 2
GLA_HEADS = 4
GLA_DK = D_MODEL // 2
GLA_DV = D_MODEL
GLA_HEAD_K = GLA_DK // GLA_HEADS
GLA_HEAD_V = GLA_DV // GLA_HEADS
GLA_GATE_RANK = 16
GLA_TAU = 16.0
GLA_CHUNK = 64
LRU_WIDTH = D_MODEL
LRU_BLOCKS = 4
LRU_BLOCK = LRU_WIDTH // LRU_BLOCKS
LRU_C = 8.0
CONV_W = 4
CONV_LEFT = 2
FFN_HIDDEN = -(-8 * D_MODEL // (3 * 256)) * 256
EPS = 1e-6

kernel_name = "hybrid_gla_rglru_prefix_dit"

def rmsnorm(x, g):
    xf = x.astype(jnp.float32)
    y = xf * lax.rsqrt(jnp.mean(xf * xf, axis=-1, keepdims=True) + EPS)
    return (y * g.astype(jnp.float32)).astype(x.dtype)

def swiglu(h, w1, w3, w2):
    return (jax.nn.silu(h @ w1) * (h @ w3)) @ w2

def _heads(t, n):
    B, L, F = t.shape
    return t.reshape(B, L, n, F // n).transpose(0, 2, 1, 3)

def _flip_if(t, rev, axis):
    return jnp.flip(t, axis=axis) if rev else t

def gla_chunked(q, k, v, log_a, s0):
    B, H, L, dk = q.shape
    dv = v.shape[-1]
    C = GLA_CHUNK
    N = L // C
    q = q.reshape(B, H, N, C, dk)
    k = k.reshape(B, H, N, C, dk)
    v = v.reshape(B, H, N, C, dv)
    b = jnp.cumsum(log_a.reshape(B, H, N, C, dk), axis=3)
    b_last = b[:, :, :, -1:, :]
    q_dec = q * jnp.exp(b)
    k_inv = k * jnp.exp(-b)
    k_to_end = k * jnp.exp(b_last - b)
    mask = jnp.tril(jnp.ones((C, C), dtype=bool))
    att = jnp.where(mask, jnp.einsum('bhnik,bhnjk->bhnij', q_dec, k_inv), 0.0)
    o_intra = jnp.einsum('bhnij,bhnjv->bhniv', att, v)
    u = jnp.einsum('bhnck,bhncv->bhnkv', k_to_end, v)
    decay = jnp.exp(b_last[:, :, :, 0, :])

    def step(s, inp):
        d, uu = inp
        return d[..., None] * s + uu, s

    s_final, s_prev = lax.scan(step, s0, (jnp.moveaxis(decay, 2, 0), jnp.moveaxis(u, 2, 0)))
    s_prev = jnp.moveaxis(s_prev, 0, 2)
    o_inter = jnp.einsum('bhnck,bhnkv->bhncv', q_dec, s_prev)
    return (o_intra + o_inter).reshape(B, H, L, dv), s_final

def gla_mixer(h_c, h_l, w_in, gw1, gw2, gb, hn_g, w_out, need_ctx):
    f32 = jnp.float32
    B = h_l.shape[0]

    def project(h):
        z = h @ w_in
        q, k, v, g = jnp.split(z, [GLA_DK, 2 * GLA_DK, 2 * GLA_DK + GLA_DV], axis=-1)
        q = _heads(q, GLA_HEADS).astype(f32) * (GLA_HEAD_K ** -0.5)
        return q, _heads(k, GLA_HEADS).astype(f32), _heads(v, GLA_HEADS).astype(f32), g

    def log_gate(h, d):
        z = (h @ gw1[d]) @ gw2[d] + gb[d]
        return _heads(jax.nn.log_sigmoid(z.astype(f32)) / GLA_TAU, GLA_HEADS)

    qc, kc, vc, gc = project(h_c)
    ql, kl, vl, gl = project(h_l)
    s0 = jnp.zeros((B, GLA_HEADS, GLA_HEAD_K, GLA_HEAD_V), f32)
    outs_c, outs_l = [], []
    for d in range(2):
        rev = d == 1
        oc, s_ctx = gla_chunked(_flip_if(qc, rev, 2), _flip_if(kc, rev, 2), _flip_if(vc, rev, 2),
                                _flip_if(log_gate(h_c, d), rev, 2), s0)
        ol, _ = gla_chunked(_flip_if(ql, rev, 2), _flip_if(kl, rev, 2), _flip_if(vl, rev, 2),
                            _flip_if(log_gate(h_l, d), rev, 2), s_ctx)
        outs_c.append(_flip_if(oc, rev, 2))
        outs_l.append(_flip_if(ol, rev, 2))

    def finish(o, g, h):
        Bh, H, L, dv = o.shape
        o = rmsnorm(o, hn_g).transpose(0, 2, 1, 3).reshape(Bh, L, H * dv)
        return ((o * jax.nn.silu(g.astype(f32))) @ w_out).astype(h.dtype)

    y_l = finish(outs_l[0] + outs_l[1], gl, h_l)
    y_c = finish(outs_c[0] + outs_c[1], gc, h_c) if need_ctx else None
    return y_c, y_l

def conv_centred(u, w, b):
    L = u.shape[1]
    up = jnp.pad(u, ((0, 0), (CONV_LEFT, CONV_W - 1 - CONV_LEFT), (0, 0)))
    y = b
    for j in range(CONV_W):
        y = y + up[:, j:j + L, :] * w[j]
    return y

def rglru_coeffs(u, wa, ba, wx, bx, lam):
    B, L, W = u.shape
    ub = u.reshape(B, L, LRU_BLOCKS, LRU_BLOCK)
    r = jax.nn.sigmoid(jnp.einsum('blgi,gij->blgj', ub, wa).reshape(B, L, W) + ba)
    i = jax.nn.sigmoid(jnp.einsum('blgi,gij->blgj', ub, wx).reshape(B, L, W) + bx)
    log_a = -LRU_C * r * jax.nn.softplus(-lam.astype(jnp.float32))
    a = jnp.exp(log_a)
    return a, jnp.sqrt(-jnp.expm1(2.0 * log_a)) * (i * u)

def linear_scan(a, b, h0):
    b = b.at[:, 0].add(a[:, 0] * h0)

    def comb(left, right):
        a1, b1 = left
        a2, b2 = right
        return a1 * a2, a2 * b1 + b2

    _, h = lax.associative_scan(comb, (a, b), axis=1)
    return h

def rglru_mixer(h_c, h_l, w_in, conv_w, conv_b, ga_w, ga_b, gx_w, gx_b, lam, w_out, need_ctx):
    f32 = jnp.float32
    B = h_l.shape[0]

    def branches(h):
        z = h @ w_in
        y, u = jnp.split(z, 2, axis=-1)
        return jax.nn.gelu(y.astype(f32)), conv_centred(u, conv_w, conv_b).astype(f32)

    yc, uc = branches(h_c)
    yl, ul = branches(h_l)
    h0 = jnp.zeros((B, LRU_WIDTH), f32)
    hs_c, hs_l = [], []
    for d in range(2):
        rev = d == 1
        a, b = rglru_coeffs(_flip_if(uc, rev, 1), ga_w[d], ga_b[d], gx_w[d], gx_b[d], lam[d])
        hc = linear_scan(a, b, h0)
        a, b = rglru_coeffs(_flip_if(ul, rev, 1), ga_w[d], ga_b[d], gx_w[d], gx_b[d], lam[d])
        hl = linear_scan(a, b, hc[:, -1])
        hs_c.append(_flip_if(hc, rev, 1))
        hs_l.append(_flip_if(hl, rev, 1))
    y_l = (((hs_l[0] + hs_l[1]) * yl) @ w_out).astype(h_l.dtype)
    y_c = (((hs_c[0] + hs_c[1]) * yc) @ w_out).astype(h_c.dtype) if need_ctx else None
    return y_c, y_l

def setup_inputs(seed: int = 0) -> dict:
    key = jax.random.key(seed)
    ks = list(jax.random.split(key, 32))
    n_gla = (DEPTH + 1) // 2
    n_lru = DEPTH // 2
    D = D_MODEL
    nrm = lambda k, shape, s: jax.random.normal(k, shape, jnp.float32) * s
    u_a = jax.random.uniform(ks[21], (n_lru, 2, LRU_WIDTH), jnp.float32, 0.9, 0.999)
    s_root = u_a ** (1.0 / LRU_C)
    return {
        'x': nrm(ks[0], (BATCH, SEQ, D), 1.0),
        'c': nrm(ks[1], (BATCH, D), 1.0),
        'ctx': nrm(ks[2], (BATCH, CTX_LEN, D), 1.0),
        'c_ctx': nrm(ks[3], (D,), 1.0),
        'norm_mix_g': 1.0 + nrm(ks[4], (DEPTH, D), 0.1),
        'norm_ffn_g': 1.0 + nrm(ks[5], (DEPTH, D), 0.1),
        'w_mod': nrm(ks[6], (DEPTH, D, 6 * D), D ** -0.5),
        'b_mod': nrm(ks[7], (DEPTH, 6 * D), 0.02),
        'gla_w_in': nrm(ks[8], (n_gla, D, 2 * GLA_DK + 2 * GLA_DV), D ** -0.5),
        'gla_gate_w1': nrm(ks[9], (n_gla, 2, D, GLA_GATE_RANK), D ** -0.5),
        'gla_gate_w2': nrm(ks[10], (n_gla, 2, GLA_GATE_RANK, GLA_DK), GLA_GATE_RANK ** -0.5),
        'gla_gate_b': nrm(ks[11], (n_gla, 2, GLA_DK), 0.5),
        'gla_head_norm_g': 1.0 + nrm(ks[12], (n_gla, GLA_HEAD_V), 0.1),
        'gla_w_out': nrm(ks[13], (n_gla, GLA_DV, D), GLA_DV ** -0.5),
        'lru_w_in': nrm(ks[14], (n_lru, D, 2 * LRU_WIDTH), D ** -0.5),
        'lru_conv_w': nrm(ks[15], (n_lru, CONV_W, LRU_WIDTH), CONV_W ** -0.5),
        'lru_conv_b': nrm(ks[16], (n_lru, LRU_WIDTH), 0.02),
        'lru_gate_a_w': nrm(ks[17], (n_lru, 2, LRU_BLOCKS, LRU_BLOCK, LRU_BLOCK), LRU_BLOCK ** -0.5),
        'lru_gate_a_b': nrm(ks[18], (n_lru, 2, LRU_WIDTH), 0.1),
        'lru_gate_x_w': nrm(ks[19], (n_lru, 2, LRU_BLOCKS, LRU_BLOCK, LRU_BLOCK), LRU_BLOCK ** -0.5),
        'lru_gate_x_b': nrm(ks[20], (n_lru, 2, LRU_WIDTH), 0.1),
        'lru_lambda': jnp.log(s_root) - jnp.log1p(-s_root),
        'lru_w_out': nrm(ks[22], (n_lru, LRU_WIDTH, D), LRU_WIDTH ** -0.5),
        'ffn_w1': nrm(ks[23], (DEPTH, D, FFN_HIDDEN), D ** -0.5),
        'ffn_w3': nrm(ks[24], (DEPTH, D, FFN_HIDDEN), D ** -0.5),
        'ffn_w2': nrm(ks[25], (DEPTH, FFN_HIDDEN, D), FFN_HIDDEN ** -0.5),
        'final_norm_g': 1.0 + nrm(ks[26], (D,), 0.1),
    }

def reference(x, c, ctx, c_ctx, norm_mix_g, norm_ffn_g, w_mod, b_mod,
              gla_w_in, gla_gate_w1, gla_gate_w2, gla_gate_b, gla_head_norm_g, gla_w_out,
              lru_w_in, lru_conv_w, lru_conv_b, lru_gate_a_w, lru_gate_a_b, lru_gate_x_w,
              lru_gate_x_b, lru_lambda, lru_w_out, ffn_w1, ffn_w3, ffn_w2, final_norm_g):
    B, S, D = x.shape
    rows = S // GRID_W

    def to_col(t):
        return t.reshape(B, rows, GRID_W, D).transpose(0, 2, 1, 3).reshape(B, S, D)

    def from_col(t):
        return t.reshape(B, GRID_W, rows, D).transpose(0, 2, 1, 3).reshape(B, S, D)

    h_ctx = ctx
    for i in range(DEPTH):
        last = i == DEPTH - 1
        j = i // N_MIXERS
        m_l = (jax.nn.silu(c) @ w_mod[i] + b_mod[i])[:, None, :]
        m_c = (jax.nn.silu(c_ctx) @ w_mod[i] + b_mod[i])[None, None, :]
        sh1, sc1, g1, sh2, sc2, g2 = jnp.split(m_l, 6, axis=-1)
        csh1, csc1, cg1, csh2, csc2, cg2 = jnp.split(m_c, 6, axis=-1)
        a_l = rmsnorm(x, norm_mix_g[i]) * (1.0 + sc1) + sh1
        a_c = rmsnorm(h_ctx, norm_mix_g[i]) * (1.0 + csc1) + csh1
        if i % N_MIXERS == 0:
            y_c, y_l = gla_mixer(a_c, a_l, gla_w_in[j], gla_gate_w1[j], gla_gate_w2[j], gla_gate_b[j],
                                 gla_head_norm_g[j], gla_w_out[j], not last)
        else:
            y_c, y_lc = rglru_mixer(a_c, to_col(a_l), lru_w_in[j], lru_conv_w[j], lru_conv_b[j],
                                    lru_gate_a_w[j], lru_gate_a_b[j], lru_gate_x_w[j], lru_gate_x_b[j],
                                    lru_lambda[j], lru_w_out[j], not last)
            y_l = from_col(y_lc)
        x = x + g1 * y_l
        f_l = rmsnorm(x, norm_ffn_g[i]) * (1.0 + sc2) + sh2
        x = x + g2 * swiglu(f_l, ffn_w1[i], ffn_w3[i], ffn_w2[i])
        if not last:
            h_ctx = h_ctx + cg1 * y_c
            f_c = rmsnorm(h_ctx, norm_ffn_g[i]) * (1.0 + csc2) + csh2
            h_ctx = h_ctx + cg2 * swiglu(f_c, ffn_w1[i], ffn_w3[i], ffn_w2[i])
    return rmsnorm(x, final_norm_g)


_drawn_inputs = setup_inputs


def setup_inputs(seed=0):
    import zlib

    import numpy as np

    out = dict(_drawn_inputs(seed))
    spreads = {}
    factors = {'lru_gate_a_b': 4.921}
    for name, (base, spread) in spreads.items():
        noise = np.random.default_rng([zlib.crc32(name.encode()), seed]).standard_normal(out[name].shape)
        drawn = base * np.exp(spread * noise) if base else spread * noise
        out[name] = __import__('jax').numpy.asarray(drawn.astype(out[name].dtype))
    for name, factor in factors.items():
        out[name] = (out[name] * factor).astype(out[name].dtype)
    return out
```

```python
from contextlib import ExitStack, contextmanager

import concourse.bass as bass
from concourse import mybir

P = 128
F32 = mybir.dt.float32
F32R = mybir.dt.float32r
BF16 = mybir.dt.bfloat16
I32 = mybir.dt.int32
ALU = mybir.AluOpType
ACT = mybir.ActivationFunctionType

LAT, CTX = 512, 256
TOK = LAT + CTX
D = 1024
KT = D // P
HEADS = 4
CHUNK = 64
NCH = TOK // CHUNK
TT = TOK // P
TAU = 16.0
RANK = 16
EPS = 1e-6
GRID_W = 64
ROWS = LAT // GRID_W
FFN = 2816
FT = FFN // P
FFN_PARTS = [(0, 8), (8, 8), (16, 6)]
CONV_W = 4
LRU_C = 8.0
DK_SCALE = float(P) ** -0.5
BOTH = [(0, 0, LAT), (1, LAT, CTX)]
ONLY_LAT = [(0, 0, LAT)]

Q_TURN = 0
Q_STAT = [[4, 58], [0, 0]]
Q_T = 5
Q_HEAD = 6
PER_HEAD = 10
Q_NORM = Q_HEAD + HEADS * PER_HEAD
Q_G = Q_NORM + HEADS
Q_OUT0 = Q_G + 4
Q_STAT[0][1] = Q_OUT0 + 4
Q_FFN0 = Q_STAT[0][1] + 1
FFN_DUOS = sum(n + 4 for _, n in FFN_PARTS)
Q_STAT[1][0] = Q_FFN0 + FFN_DUOS
Q_LRU = Q_STAT[1][0] + 1
PER_BLOCK = 6
Q_OUT1 = Q_LRU + 4 * PER_BLOCK
Q_STAT[1][1] = Q_OUT1 + 4
Q_FFN1 = Q_STAT[1][1] + 1
Q_FINAL = Q_FFN1 + FFN_DUOS

C_GATE1 = 0
C_HEAD = 1
C_G = C_HEAD + 2 * HEADS
C_OUT0 = C_G + 4
C_FFN0 = C_OUT0 + 4
C_LRU = C_FFN0 + FFN_DUOS
C_OUT1 = C_LRU + 12
C_FFN1 = C_OUT1 + 4
CHUNKS = C_FFN1 + FFN_DUOS
assert (CHUNKS - 1) % 2 == 0

SEC_FIRST = [1, 0]
SEC_HEAD = 2
V_BMOD, V_NMIX, V_NFFN = 0, 96, 112
V_C, V_GB, V_HN, V_CW, V_CB, V_BA, V_BX, V_LAM, V_END = 0, 16, 24, 26, 58, 66, 82, 98, 114


class Steps:

    def __init__(self, eng, sem):
        self.eng, self.sem, self.base, self.k, self.i, self.per = eng, sem, 0, 0, 0, 0

    def mark(self, ins):
        ins.then_inc(self.sem, 1)
        self.k += 1

    def wait(self):
        self.eng.wait_ge(self.sem, self.base + self.i * self.per + self.k)

    def link(self, ins):
        self.mark(ins)
        self.wait()

    @contextmanager
    def loop(self, n, per):
        self.base, self.k, self.per = self.base + self.k, 0, per
        with self.eng.Fori(0, n) as i:
            self.i = i
            yield i
        assert self.k == per, (self.k, per)
        self.base, self.k, self.i, self.per = self.base + n * per, 0, 0, 0


def build(nc, x, c, ctx_in, c_ctx, norm_mix_g, norm_ffn_g, w_mod, b_mod, gla_w_in, gla_gate_w1, gla_gate_w2,
          gla_gate_b, gla_head_norm_g, gla_w_out, lru_w_in, lru_conv_w, lru_conv_b, lru_gate_a_w, lru_gate_a_b,
          lru_gate_x_w, lru_gate_x_b, lru_lambda, lru_w_out, ffn_w1, ffn_w3, ffn_w2, final_norm_g, out):
    es = ExitStack()
    with es:
        at = [-(-nc.sbuf_base // 64) * 64]

        def region(nbytes):
            start = at[0]
            at[0] += -(-nbytes // 32) * 32
            assert at[0] <= nc.sbuf_usable_end, at[0]
            return start

        def place(name, shape, dt, offset):
            return nc.alloc_sbuf_tensor_at(name, shape, dt, offset=offset)

        KB = 1024
        X_AT, A_AT, H_AT = region(24 * KB), region(48 * KB), region(48 * KB)
        W_AT, M_AT, T_AT = region(48 * KB), region(8 * KB), region(24 * KB)

        def small(name, shape, dt=F32):
            n = 2 if dt == BF16 else 4
            for s in shape[1:]:
                n *= s
            return place(name, shape, dt, region(n))

        xres = place("xres", [P, KT, TOK], F32, X_AT)
        a_hi = place("a_hi", [P, KT, TOK], F32R, A_AT)
        a_lo = place("a_lo", [P, KT, TOK], F32R, A_AT + 24 * KB)
        h_hi = place("h_hi", [P, 8, TOK], F32R, H_AT)
        h_lo = place("h_lo", [P, 8, TOK], F32R, H_AT + 24 * KB)
        raw = [place(f"raw{b}", [P, 8, 256], F32, W_AT + 8 * KB * b) for b in range(2)]
        w_hi = [place(f"w_hi{b}", [P, 8, 256], F32R, W_AT + 8 * KB * (2 + b)) for b in range(2)]
        w_lo = [place(f"w_lo{b}", [P, 8, 256], F32R, W_AT + 8 * KB * (4 + b)) for b in range(2)]
        mod_ring = [place(f"mod_ring{b}", [P, 8, P], F32, M_AT + 4 * KB * b) for b in range(2)]
        mod_first = [place("mod_first0", [P, 8, D], F32, H_AT), place("mod_first1", [P, 8, D], F32, A_AT)]
        vec_rows = place("vec_rows", [P, 2, P], F32, A_AT + 32 * KB)
        x_rows = place("x_rows", [P, TT, D], F32, T_AT)
        sq = [place(f"sq{b}", [P, TOK], F32, T_AT + 3 * KB * b) for b in range(2)]
        sqsum = place("sqsum", [P, TOK], F32, T_AT + 6 * KB)
        rinv = place("rinv", [P, TOK], F32, T_AT + 9 * KB)
        normed = [place(f"normed{b}", [P, TOK], F32, T_AT + 12 * KB + 3 * KB * b) for b in range(2)]
        o_all = place("o_all", [P, 8, TOK], F32, H_AT)
        t_low = place("t_low", [64, TOK], F32, H_AT + 18 * KB)
        gate2 = place("gate2", [64, 2, P], F32, H_AT + 22 * KB)
        states = place("states", [P, 22, 256], F32, H_AT + 24 * KB)
        k_end = place("k_end", [P, 2, TOK], F32, H_AT + (24 + 16) * KB)
        q_dec = place("q_dec", [P, 2, TOK], F32, T_AT)
        k_inv = place("k_inv", [P, 2, TOK], F32, T_AT + 6 * KB)
        att = place("att", [P, 12, P], F32, T_AT + 6 * KB)
        zg = place("zg", [P, 2, TOK], F32, T_AT + 12 * KB)
        k_tok = place("k_tok", [P, 12, P], F32, T_AT + 12 * KB)
        bcum = place("bcum", [P, 2, TOK], F32, T_AT + 18 * KB)
        v_tok = place("v_tok", [P, TT, 256], F32, T_AT + 18 * KB)
        o_sq = [place(f"o_sq{b}", [P, 2, TOK], F32, T_AT + 6 * KB * b) for b in range(2)]
        o_sum = [place(f"o_sum{b}", [P, TOK], F32, T_AT + 12 * KB + 3 * KB * b) for b in range(2)]
        silu_g = [place(f"silu_g{b}", [P, 2, TOK], F32, T_AT + 18 * KB - 6 * KB * b) for b in range(2)]
        o_rinv = place("o_rinv", [P, HEADS, TOK], F32, H_AT + 24 * KB)
        gate = place("gate", [P, 2, TOK], F32, T_AT)
        hid = place("hid", [P, 2, TOK], F32, T_AT + 6 * KB)
        GAP = 2
        UW = LAT + GAP + CTX
        lru_o = place("lru_o", [P, 8, LAT], F32, H_AT)
        lru_y = place("lru_y", [P, 2, LAT], F32, H_AT + 16 * KB)
        gates_r = place("gates_r", [P, 4, 2, TOK], F32, H_AT + 20 * KB)
        U_AT = H_AT + 44 * KB
        u_hi = place("u_hi", [P, 2, TOK], F32R, T_AT)
        u_lo = place("u_lo", [P, 2, TOK], F32R, T_AT + 6 * KB)
        scan_h = [place(f"scan_h{b}", [P, 2, TOK], F32, T_AT + 6 * KB * b) for b in range(2)]
        u_pad = place("u_pad", [P, 2, UW + 4], F32, T_AT + 12 * KB)
        UP_END = T_AT + 12 * KB + 2 * 4 * (UW + 4)
        u_conv = place("u_conv", [P, 2, UW], F32, -(-UP_END // 32) * 32)
        assert UP_END + 32 + 8 * UW <= T_AT + 24 * KB + 1024
        final_g = place("final_g", [P, D], F32, M_AT)
        y_rows = [place(f"y_rows{b}", [P, D], F32, T_AT + 4 * KB * b) for b in range(4)]
        y_junk = place("y_junk", [P, D], F32, T_AT + 16 * KB)
        region(512)

        ident = small("ident", [P, P])
        ones = small("ones", [P, P])
        mask = small("mask", [P, 2, P])
        resets = small("resets", [P, NCH, CHUNK], BF16)
        vec = small("vec", [P, 2, P])
        cs = small("cs", [P, KT, 2])
        mod = small("mod", [P, 2 * 6, KT, 2])
        gain = small("gain", [P, 4, KT, 2])
        decay = small("decay", [P, 2, NCH])
        lru_c = small("lru_c", [P, 2, 16])
        lw = small("lw", [P, 4, 16])
        eps = small("eps", [P, 1])
        zero = small("zero", [P, 1])
        ysum = small("ysum", [P, 3, 4])

        duo_psum = [es.enter_context(nc.psum_tensor(f"duo{b}", [P, 3, 512], F32)) for b in range(2)]
        vec_psum = es.enter_context(nc.psum_tensor("vec_psum", [P, 512], F32))
        mod_psum = es.enter_context(nc.psum_tensor("mod_psum", [P, 512], F32))

        def sem(name):
            return es.enter_context(nc.semaphore(name))

        consts_made, pads_made = sem("consts_made"), sem("pads_made")
        vec_loaded, x_loaded = sem("vec_loaded"), sem("x_loaded")
        first_loaded = [sem(f"first_loaded{b}") for b in range(2)]
        vec_turned, vec_ready, cs_ready = sem("vec_turned"), sem("vec_ready"), sem("cs_ready")
        raw_loaded = [sem(f"raw_loaded{b}") for b in range(2)]
        hi_ready, lo_ready = sem("hi_ready"), sem("lo_ready")
        mod_loaded = [sem(f"mod_loaded{b}") for b in range(2)]
        mod_used, mod_ready = sem("mod_used"), sem("mod_ready")
        gate2_zeroed, gate2_loaded, gates_loaded = sem("gate2_zeroed"), sem("gate2_loaded"), sem("gates_loaded")
        duo_done = sem("duo_done")
        duo_moved = [sem(f"duo_moved{b}") for b in range(2)]
        act_step, dve_step = sem("act_step"), sem("dve_step")
        squared, summed, scaled, hi_split, a_ready = (sem("squared"), sem("summed"), sem("scaled"),
                                                      sem("hi_split"), sem("a_ready"))
        z_logged, cum_ready, exps_ready = sem("z_logged"), sem("cum_ready"), sem("exps_ready")
        o_squared, o_summed, rinv_ready, gated = (sem("o_squared"), sem("o_summed"), sem("rinv_ready"),
                                                  sem("gated"))
        hid_ready = sem("hid_ready")
        conv_done, u_ready, sig_done, tanh_done, a_sq, factor, root, scanned, lruc_ready = (
            sem("conv_done"), sem("u_ready"), sem("sig_done"), sem("tanh_done"), sem("a_sq"), sem("factor"),
            sem("root"), sem("scanned"), sem("lruc_ready"))
        u_rounded = sem("u_rounded")
        y_rooted, final_g_loaded, stored = sem("y_rooted"), sem("final_g_loaded"), sem("stored")
        l_exp, l_w = sem("l_exp"), sem("l_w")

        def duo(q):
            return duo_psum[q % 2]

        def state_psum(q, s):
            if s < 4:
                return duo(par(q))[:, s % 2, (s // 2) * 256:(s // 2) * 256 + 256]
            return duo(par(q))[:, 2, 0:256] if s == 4 else vec_psum[:, 0:256]

        def half(i):
            if isinstance(i, tuple):
                base, per, reg = i
                assert per % 2 == 0
                return base // 2 + (per // 2) * reg
            return i // 2

        def whole(i):
            return i[0] + i[1] * i[2] if isinstance(i, tuple) else i

        def plus(i, k):
            return (i[0] + k, i[1], i[2]) if isinstance(i, tuple) else i + k

        def par(i):
            return (i[0] if isinstance(i, tuple) else i) % 2

        def wait_done(eng, q):
            eng.wait_ge(duo_done, whole(q) + 1)

        def wait_moved(eng, q):
            eng.wait_ge(duo_moved[par(q)], half(q) + 1)

        def moved(ins, q):
            ins.then_inc(duo_moved[par(q)], 1)

        A_READY = {key: KT * n for key, n in A_ORDER.items()}
        block = es.enter_context(nc.Block())

        @block.sync
        def _(sp):
            def raw_free(ch):
                n = whole(ch)
                if isinstance(ch, tuple) or ch >= 2:
                    sp.wait_ge(lo_ready, n if isinstance(ch, tuple) and ch[0] == 1 else n - 1)

            def load(ch, first, second):
                raw_free(ch)
                for dst, src in (first, second):
                    sp.dma_start(dst, src).then_inc(raw_loaded[par(ch)], 16)

            def columns(ch, w, col, rows=8):
                r = raw[par(ch)]
                v = w.rearrange("(k p) n -> p k n", p=P)
                m = rows // 2
                load(ch, (r[:, 0:m], v[:, 0:m, bass.ds(col, 256)]), (r[:, m:rows], v[:, m:rows, bass.ds(col, 256)]))

            def mod_pieces(u, layer, col):
                v = w_mod[layer].rearrange("(k p) n -> p k n", p=P)
                for p in range(8):
                    sp.wait_ge(mod_used, whole(u) + p + 1)
                    sp.dma_start(mod_ring[p % 2][:], v[:, :, bass.ds(col + p * P, P)]).then_inc(mod_loaded[p % 2], 16)

            def rows(dst, src):
                sp.dma_start(dst, src).then_inc(vec_loaded, 16)

            r0, r1 = vec_rows[:, 0], vec_rows[:, 1]
            rows(r0[V_BMOD:V_BMOD + 96], b_mod.rearrange("l (m p) -> (l m) p", p=P))
            rows(r0[V_NMIX:V_NMIX + 16], norm_mix_g.rearrange("l (m p) -> (l m) p", p=P))
            rows(r0[V_NFFN:V_NFFN + 16], norm_ffn_g.rearrange("l (m p) -> (l m) p", p=P))
            rows(r1[V_C:V_C + 8], c.rearrange("b (m p) -> (b m) p", p=P))
            rows(r1[V_C + 8:V_C + 16], c_ctx.rearrange("(m p) -> m p", p=P))
            rows(r1[V_GB:V_GB + 8], gla_gate_b.rearrange("j d (m p) -> (j d m) p", p=P))
            rows(r1[V_HN:V_HN + 2], gla_head_norm_g.rearrange("j (m p) -> (j m) p", p=P))
            rows(r1[V_CW:V_CW + 32], lru_conv_w.rearrange("j w (m p) -> (j w m) p", p=P))
            rows(r1[V_CB:V_CB + 8], lru_conv_b.rearrange("j (m p) -> (j m) p", p=P))
            rows(r1[V_BA:V_BA + 16], lru_gate_a_b.rearrange("j d (m p) -> (j d m) p", p=P))
            rows(r1[V_BX:V_BX + 16], lru_gate_x_b.rearrange("j d (m p) -> (j d m) p", p=P))
            rows(r1[V_LAM:V_LAM + 16], lru_lambda.rearrange("j d (m p) -> (j d m) p", p=P))
            sp.dma_start(x_rows[:, 0:4], x[0].rearrange("(t p) n -> p t n", p=P)).then_inc(x_loaded, 16)
            sp.dma_start(x_rows[:, 4:6], ctx_in[0].rearrange("(t p) n -> p t n", p=P)).then_inc(x_loaded, 16)
            for b, sec in enumerate(SEC_FIRST):
                sp.dma_start(mod_first[b][:], w_mod[0].rearrange("(k p) n -> p k n", p=P)[:, :, sec * D:(sec + 1) * D]
                             ).then_inc(first_loaded[b], 16)
            sp.wait_ge(pads_made, 1)
            g1 = gla_gate_w1[0].rearrange("d (k p) r -> d p k r", p=P)
            load(C_GATE1, (raw[0][:, :, 0:RANK], g1[0]), (raw[0][:, :, 32:32 + RANK], g1[1]))
            qk = gla_w_in[0, :, 0:2 * LAT].rearrange("(k p) (s n) -> p k s n", p=P, s=2)
            sp.wait_ge(gate2_zeroed, 1)
            with sp.Fori(0, HEADS) as h:
                ch = (C_HEAD, 2, h)
                r = raw[par(ch)]
                load(ch, (r[:, :, 0:P], qk[:, :, 0, bass.ds(h * P, P)]), (r[:, :, P:2 * P], qk[:, :, 1, bass.ds(h * P, P)]))
                columns(plus(ch, 1), gla_w_in[0], 2 * LAT + 256 * h)
                sp.wait_ge(duo_done, Q_HEAD - 5 + PER_HEAD * h)
                for d in range(2):
                    sp.dma_start(gate2[32 * d:32 * d + RANK, d], gla_gate_w2[0, d, :, bass.ds(h * P, P)]
                                 ).then_inc(gate2_loaded, 16)
                mod_pieces((0, 8, h), 0, 2 * D + D * h)
            with sp.Fori(0, 2) as i:
                for b in range(2):
                    columns((C_G + b, 2, i), gla_w_in[0], 2 * LAT + D + 512 * i + 256 * b)

            def out_loads(c0, w):
                with sp.Fori(0, 2) as i:
                    for b in range(2):
                        columns((c0 + b, 2, i), w, 512 * i + 256 * b)

            def ffn_loads(layer):
                ch = C_FFN0 if layer == 0 else C_FFN1
                for part, (first, n) in enumerate(FFN_PARTS):
                    with sp.Fori(0, n // 2) as i:
                        columns((ch, 2, i), ffn_w1[layer], first * P + 256 * i)
                        columns((ch + 1, 2, i), ffn_w3[layer], first * P + 256 * i)
                        if layer == 0 and part == 0:
                            mod_pieces((8 * HEADS, 8, i), 1, D * i)
                    ch += n
                    w2 = ffn_w2[layer, first * P:(first + n) * P]
                    with sp.Fori(0, 2) as i:
                        for b in range(2):
                            columns((ch + b, 2, i), w2, 512 * i + 256 * b, rows=n)
                    ch += 4

            out_loads(C_OUT0, gla_w_out[0])
            ffn_loads(0)
            ga = lru_gate_a_w[0].rearrange("d g (k p) j -> d g p k j", p=P)
            gx = lru_gate_x_w[0].rearrange("d g (k p) j -> d g p k j", p=P)
            with sp.Fori(0, 2) as i:
                for b in range(2):
                    ch = (C_LRU + 3 * b, 6, i)
                    columns(ch, lru_w_in[0], D + 512 * i + 256 * b)
                    columns(plus(ch, 1), lru_w_in[0], (2 * i + b) * 256)
                    if b == 0:
                        mod_pieces((8 * HEADS + 32, 8, i), 1, 4 * D + D * i)
                    r = raw[par(plus(ch, 2))]
                    raw_free(plus(ch, 2))
                    for n, w in enumerate((ga, gx)):
                        for d in range(2):
                            sp.dma_start(r[:, 4 * n + 2 * d:4 * n + 2 * d + 2],
                                         w[d, bass.ds(2 * i + b, 1)].rearrange("o p k j -> (o p) k j")
                                         ).then_inc((raw_loaded[par(plus(ch, 2))], gates_loaded)[n], 16)
            out_loads(C_OUT1, lru_w_out[0])
            ffn_loads(1)
            sp.wait_ge(mod_used, 2 + 8 * 10)
            sp.dma_start(final_g[:], final_norm_g.partition_broadcast(P)).then_inc(final_g_loaded, 16)
            y_dram = out[0].rearrange("(t p) n -> t p n", p=P)
            for t in range(4):
                wait_moved(sp, Q_FINAL + t)
                sp.dma_start(y_dram[t], y_rows[t][:]).then_inc(stored, 16)
            sp.wait_ge(stored, 64)

        @block.gpsimd
        def _(pool):
            pool.memset(raw[0][:, :, 0:P], 0.0).then_inc(pads_made, 1)
            pool.memset(ident[:], 0.0)
            pool.memset(ones[:], 1.0)
            pool.memset(mask[:], 1.0)
            pool.memset(resets[:], 1.0)
            pool.memset(zero[:], 0.0)
            pool.memset(eps[:], EPS).then_inc(pads_made, 1)
            pool.wait_ge(pads_made, 2)
            pool.memset(resets[:, :, 0:1], 0.0)
            pool.affine_select(out=ident[:], in_=ident[:], compare_op=ALU.not_equal, fill=1.0, base=0,
                               pattern=[[-1, P]], channel_multiplier=1)
            pool.affine_select(out=mask[:, 0], in_=mask[:, 0], compare_op=ALU.is_ge, fill=0.0, base=0,
                               pattern=[[1, P]], channel_multiplier=-1)
            pool.affine_select(out=mask[:, 1], in_=mask[:, 1], compare_op=ALU.is_ge, fill=0.0, base=0,
                               pattern=[[-1, P]], channel_multiplier=1).then_inc(pads_made, 1)
            pool.wait_ge(pads_made, 3)
            pool.memset(mask[0:CHUNK, 0, CHUNK:P], 0.0)
            pool.memset(mask[CHUNK:P, 1, 0:CHUNK], 0.0).then_inc(consts_made, 1)

            def low(ch, cols=256):
                b = par(ch)
                pool.wait_ge(hi_ready, whole(ch) + 1)
                pool.tensor_tensor(w_lo[b][:, :, 0:cols], raw[b][:, :, 0:cols],
                                   w_hi[b][:, :, 0:cols].bitcast(F32), ALU.subtract).then_inc(lo_ready, 1)

            low(C_GATE1, P)
            with pool.Fori(0, (CHUNKS - 1) // 2) as i:
                for b in range(2):
                    low((1 + b, 2, i))

        @block.tensor
        def _(pe):
            def duo_wait(q):
                if isinstance(q, tuple) or q >= 2:
                    pe.wait_ge(duo_moved[par(q)], half(q))

            def chunk_wait(ch):
                pe.wait_ge(hi_ready, whole(ch) + 1)
                pe.wait_ge(lo_ready, whole(ch) + 1)

            def tile_out(ps, t, part, n):
                return ps[:, t, 0:n] if part == 0 else ps[:, 2, t * CTX:t * CTX + n]

            def tile_pair(ch, q, parts, act_hi, act_lo, rows=8, ready=None, pieces=None, cols=(0, 1), k0=0):
                chunk_wait(ch)
                duo_wait(q)
                ps, hi, lo = duo(par(q)), w_hi[par(ch)], w_lo[par(ch)]
                for t in cols:
                    for k in range(rows):
                        if ready is not None and t == cols[0]:
                            ready(k)
                        if pieces is not None and k % 2 == 0 and t * 4 + k // 2 < 8:
                            pieces(t * 4 + k // 2)
                        first, last = k == 0, k == rows - 1
                        wh, wl = hi[:, k0 + k, t * P:(t + 1) * P], lo[:, k0 + k, t * P:(t + 1) * P]
                        for part, s, n in parts:
                            pe.matmul(tile_out(ps, t, part, n), wh, act_hi[:, k, s:s + n], start=first, stop=False,
                                      skip_group_check=True)
                        for part, s, n in parts:
                            pe.matmul(tile_out(ps, t, part, n), wh, act_lo[:, k, s:s + n], start=False, stop=False,
                                      skip_group_check=True)
                        for part, s, n in parts:
                            mm = pe.matmul(tile_out(ps, t, part, n), wl, act_hi[:, k, s:s + n], start=False,
                                           stop=last, skip_group_check=True)
                return mm

            def a_wait(key):
                return lambda k: pe.wait_ge(a_ready, A_READY[key] + k + 1)

            def mod_piece(u, p):
                if p == 0:
                    pe.wait_ge(mod_ready, whole(section_of(u)))
                pe.wait_ge(mod_loaded[p % 2], 16 * (half(plus(u, p)) + 1))
                for k in range(KT):
                    mm = pe.matmul(mod_psum[:, 2 * p:2 * p + 2], mod_ring[p % 2][:, k], cs[:, k], start=k == 0,
                                   stop=k == KT - 1, skip_group_check=True)
                mm.then_inc(mod_used, 1)

            def section_of(u):
                return (2 + u[0] // 8, 1, u[2])

            def rms_sum(q, parts, src, ready, n):
                pe.wait_ge(ready, n)
                duo_wait(q)
                for part, s, w in parts:
                    mm = pe.matmul(tile_out(duo(q), 0, part, w), ones[:], src[:, s:s + w], start=True, stop=True)
                mm.then_inc(duo_done, 1)

            pe.wait_ge(consts_made, 1)
            pe.wait_ge(vec_loaded, 16 * 12)
            pe.transpose(vec_psum[:, 0:P], vec_rows[:, 0], ident[:])
            pe.transpose(vec_psum[:, P:P + V_END], vec_rows[0:V_END, 1], ident[0:V_END, 0:V_END]).then_inc(vec_turned, 1)
            pe.wait_ge(x_loaded, 32)
            for i in range(4):
                q = Q_TURN + i
                duo_wait(q)
                for t in range(2):
                    f = 2 * i + t
                    for tau in range(TT):
                        dst = (duo(q)[:, t, tau * P:(tau + 1) * P] if tau < 4
                               else duo(q)[:, 2, t * CTX + (tau - 4) * P:t * CTX + (tau - 3) * P])
                        mm = pe.transpose(dst, x_rows[:, tau, f * P:(f + 1) * P], ident[:])
                mm.then_inc(duo_done, 1)
            pe.wait_ge(cs_ready, 1)
            for b in range(2):
                pe.wait_ge(first_loaded[b], 16)
                if b:
                    pe.wait_ge(mod_ready, 1)
                for m in range(8):
                    for k in range(KT):
                        mm = pe.matmul(mod_psum[:, 2 * m:2 * m + 2], mod_first[b][:, k, m * P:(m + 1) * P], cs[:, k],
                                       start=k == 0, stop=k == KT - 1, skip_group_check=True)
                mm.then_inc(mod_used, 1)
            rms_sum(Q_STAT[0][0], BOTH, sqsum, summed, 8)

            tile_pair(C_GATE1, Q_T, BOTH, a_hi, a_lo, ready=a_wait(("prep", 0, 0)), cols=(0,)).then_inc(duo_done, 1)
            wait_moved(pe, Q_T)
            with pe.Fori(0, HEADS) as h:
                q0 = (Q_HEAD, PER_HEAD, h)
                pe.wait_ge(gate2_loaded, 32 * h + 32)
                duo_wait(q0)
                for d in range(2):
                    for part, s, n in BOTH:
                        mm = pe.matmul(tile_out(duo(par(q0)), d, part, n), gate2[:, d], t_low[:, s:s + n], start=True, stop=True,
                                       skip_group_check=True)
                mm.then_inc(duo_done, 1)
                ch = (C_HEAD, 2, h)
                tile_pair(ch, plus(q0, 1), BOTH, a_hi, a_lo,
                          pieces=lambda p: mod_piece((0, 8, h), p)).then_inc(duo_done, 1)
                chv, qv = plus(ch, 1), plus(q0, 2)
                chunk_wait(chv)
                duo_wait(qv)
                hi, lo = w_hi[par(chv)], w_lo[par(chv)]
                for tau in range(TT):
                    dst = duo(par(qv))[:, tau // 2, (tau % 2) * 256:(tau % 2) * 256 + 256]
                    for k in range(KT):
                        ah, al = a_hi[:, k, tau * P:(tau + 1) * P], a_lo[:, k, tau * P:(tau + 1) * P]
                        pe.matmul(dst, ah, hi[:, k], start=k == 0, stop=False, skip_group_check=True)
                        pe.matmul(dst, ah, lo[:, k], start=False, stop=False, skip_group_check=True)
                        mm = pe.matmul(dst, al, hi[:, k], start=False, stop=k == KT - 1, skip_group_check=True)
                mm.then_inc(duo_done, 1)
                wait_moved(pe, plus(q0, 1))
                qt = plus(q0, 3)
                duo_wait(qt)
                for j in range(12):
                    d, tau = j // 6, j % 6
                    mm = pe.transpose(duo(par(qt))[:, j // 4, (j % 4) * P:(j % 4 + 1) * P],
                                      k_end[:, d, tau * P:(tau + 1) * P], ident[:])
                mm.then_inc(duo_done, 1)
                qa = plus(q0, 4)
                duo_wait(qa)
                for j in range(12):
                    d, tau = j // 6, j % 6
                    mm = pe.matmul(duo(par(qa))[:, j // 4, (j % 4) * P:(j % 4 + 1) * P],
                                   k_inv[:, d, tau * P:(tau + 1) * P], q_dec[:, d, tau * P:(tau + 1) * P],
                                   start=True, stop=True, skip_group_check=True)
                mm.then_inc(duo_done, 1)
                wait_moved(pe, qt)
                wait_moved(pe, qv)
                for g, (d, chunks) in enumerate(STATE_GROUPS):
                    qu = plus(q0, 5 + g)
                    duo_wait(qu)
                    for s, n in enumerate(chunks):
                        r = CHUNK * (n % 2)
                        mm = pe.matmul(state_psum(qu, s),
                                       k_tok[r:r + CHUNK, d * 6 + n // 2], v_tok[r:r + CHUNK, n // 2],
                                       start=True, stop=True, skip_group_check=True)
                    mm.then_inc(duo_done, 1)
                for g in range(4):
                    wait_moved(pe, plus(q0, 5 + g)) if g >= 2 else None
                wait_moved(pe, qa)
                qo = plus(q0, 9)
                duo_wait(qo)
                for tau in range(TT):
                    for v in range(2):
                        c0 = (tau % 2) * 256 + v * P
                        dst = duo(par(qo))[:, tau // 2, c0:c0 + P]
                        pe.matmul(dst, v_tok[:, tau, v * P:(v + 1) * P], att[:, tau], start=True, stop=False,
                                  skip_group_check=True)
                        mm = pe.matmul(dst, v_tok[:, tau, v * P:(v + 1) * P], att[:, 6 + tau], start=False,
                                       stop=False, skip_group_check=True)
                        for n in (2 * tau, 2 * tau + 1):
                            for d in range(2):
                                s = STATE_BEFORE[d][n]
                                if s is not None:
                                    mm = pe.matmul(duo(par(qo))[:, tau // 2, c0 + CHUNK * (n % 2):c0 + CHUNK * (n % 2) + CHUNK],
                                                   states[:, s, v * P:(v + 1) * P],
                                                   q_dec[:, d, n * CHUNK:(n + 1) * CHUNK], start=False,
                                                   stop=n % 2 == 1 and d == 1, skip_group_check=True)
                mm.then_inc(duo_done, 1)

            for h in range(HEADS):
                rms_sum(Q_NORM + h, BOTH, o_sum[h % 2], o_summed, h + 1)
            with pe.Fori(0, 2) as i:
                for b in range(2):
                    tile_pair((C_G + b, 2, i), (Q_G + b, 2, i), BOTH, a_hi, a_lo).then_inc(duo_done, 1)

            def project_out(layer, parts):
                c0, q0 = (C_OUT0, Q_OUT0) if layer == 0 else (C_OUT1, Q_OUT1)
                with pe.Fori(0, 2) as i:
                    for b in range(2):
                        tile_pair((c0 + b, 2, i), (q0 + b, 2, i), parts, a_hi, a_lo,
                                  ready=a_wait(("out", layer)) if b == 0 else None).then_inc(duo_done, 1)

            def ffn(layer, parts):
                ch, q = (C_FFN0, Q_FFN0) if layer == 0 else (C_FFN1, Q_FFN1)
                rms_sum(Q_STAT[layer][1], parts, sqsum, summed, 8 * (2 * layer + 2))
                hb = 0 if layer == 0 else FT // 2
                for part, (first, n) in enumerate(FFN_PARTS):
                    with pe.Fori(0, n // 2) as i:
                        piece = (lambda p: mod_piece((8 * HEADS, 8, i), p)) if layer == 0 and part == 0 else None
                        tile_pair((ch, 2, i), (q, 2, i), parts, a_hi, a_lo, ready=a_wait(("prep", layer, 1)),
                                  pieces=piece).then_inc(duo_done, 1)
                        tile_pair((ch + 1, 2, i), (q + 1, 2, i), parts, a_hi, a_lo).then_inc(duo_done, 1)
                    ch, q, hb = ch + n, q + n, hb + n // 2
                    with pe.Fori(0, 2) as i:
                        for b in range(2):
                            rd = (lambda k: pe.wait_ge(hid_ready, hb - n // 2 + k // 2 + 1) if k % 2 == 0 else None)
                            tile_pair((ch + b, 2, i), (q + b, 2, i), parts, h_hi, h_lo, rows=n,
                                      ready=rd if b == 0 else None).then_inc(duo_done, 1)
                    ch, q = ch + 4, q + 4

            project_out(0, BOTH)
            ffn(0, BOTH)
            rms_sum(Q_STAT[1][0], BOTH, sqsum, summed, 24)
            with pe.Fori(0, 2) as i:
                for b in range(2):
                    q0, ch = (Q_LRU + 6 * b, 12, i), (C_LRU + 3 * b, 6, i)
                    tile_pair(ch, q0, BOTH, a_hi, a_lo, ready=a_wait(("prep", 1, 0)) if b == 0 else None,
                              pieces=(lambda p: mod_piece((8 * HEADS + 32, 8, i), p)) if b == 0 else None
                              ).then_inc(duo_done, 1)
                    tile_pair(plus(ch, 1), plus(q0, 1), ONLY_LAT, a_hi, a_lo).then_inc(duo_done, 1)
                    pe.wait_ge(u_ready, 2 * i + b + 1)
                    for gi in range(4):
                        tile_pair(plus(ch, 2), plus(q0, 2 + gi), BOTH, u_hi, u_lo, rows=2, k0=2 * gi
                                  ).then_inc(duo_done, 1)
            project_out(1, ONLY_LAT)
            ffn(1, ONLY_LAT)
            wait_moved(pe, Q_FINAL - 2)
            wait_moved(pe, Q_FINAL - 1)
            for t in range(4):
                q = Q_FINAL + t
                duo_wait(q)
                for f in range(KT):
                    mm = pe.transpose(duo(q)[:, f // 4, (f % 4) * P:(f % 4 + 1) * P], xres[:, f, t * P:(t + 1) * P],
                                      ident[:])
                mm.then_inc(duo_done, 1)

        @block.scalar
        def _(act):
            steps = Steps(act, act_step)

            def high(ch, q_before, cols=256):
                if not isinstance(ch, tuple) and ch >= CHUNKS:
                    return
                b = par(ch)
                act.wait_ge(raw_loaded[b], 32 * (half(ch) + 1))
                if q_before is not None:
                    wait_done(act, q_before)
                act.activation(w_hi[b][:, :, 0:cols], raw[b][:, :, 0:cols], ACT.Copy).then_inc(hi_ready, 1)

            def part_psum(q, part):
                ps = duo(par(q))
                return ps[:, 0:2, :] if part == 0 else ps[:, 2, :].rearrange("p (t n) -> p t n", t=2)

            def tile_psum(q, t, part):
                ps = duo(par(q))
                return ps[:, t, :] if part == 0 else ps[:, 2, t * CTX:(t + 1) * CTX]

            def prep(layer, which, parts, q_resid):
                n = 2 * layer + which
                width = parts[-1][1] + parts[-1][2]
                for m in range(KT):
                    if q_resid is not None:
                        wait_moved(act, q_resid + m // 2)
                    if m >= 2:
                        act.wait_ge(summed, 8 * n + m - 1)
                    act.activation(sq[m % 2][:, 0:width], xres[:, m, 0:width], ACT.Square).then_inc(squared, 1)
                q = Q_STAT[layer][which]
                wait_done(act, q)
                for part, s, w in parts:
                    ins = act.activation(rinv[:, s:s + w], tile_psum(q, 0, part), ACT.Sqrt, bias=eps[:, 0:1],
                                         scale=1.0 / D)
                    if part == parts[-1][0]:
                        moved(ins, q)
                sec = 6 * layer + 3 * which
                if n == 0:
                    act.wait_ge(mod_ready, 2)
                for m in range(KT):
                    act.wait_ge(scaled, 8 * n + m + 1)
                    for part, s, w in parts:
                        dst, src = a_hi[:, m, s:s + w], normed[m % 2][:, s:s + w]
                        if part == 0 and (layer, which) == (1, 0):
                            dst = dst.rearrange("p (c r) -> p r c", r=ROWS)
                            src = src.rearrange("p (r c) -> p r c", r=ROWS)
                        ins = act.activation(dst, src, ACT.Identity, bias=mod[:, sec, m, part:part + 1])
                    ins.then_inc(hi_split, 1)

            act.wait_ge(vec_ready, 1)
            act.activation(cs[:].rearrange("p k v -> p v k"), vec[:, 1, V_C:V_C + 16].rearrange("p (v k) -> p v k", v=2),
                           ACT.Silu).then_inc(cs_ready, 1)
            act.wait_ge(l_w, 1)
            act.activation(lw[:, 0], lw[:, 3], ACT.Exp, scale=-1.0).then_inc(l_exp, 1)
            for i in (1, 3):
                q = Q_TURN + i
                wait_done(act, q)
                steps.mark(act.activation(xres[:, 2 * i:2 * i + 2, 0:LAT], part_psum(q, 0), ACT.Copy))
                moved(act.activation(xres[:, 2 * i:2 * i + 2, LAT:TOK], part_psum(q, 1), ACT.Copy), q)
            for i in range(4):
                wait_moved(act, Q_TURN + i)
            high(0, None, P)
            high(1, None)
            prep(0, 0, BOTH, None)

            act.preload_act_table_set("natural_log_exp_and_others")
            wait_done(act, Q_T)
            steps.mark(act.activation(t_low[:, 0:LAT], duo(Q_T)[0:64, 0, :], ACT.Copy))
            moved(act.activation(t_low[:, LAT:TOK], duo(Q_T)[0:64, 2, 0:CTX], ACT.Copy), Q_T)
            high(2, Q_T)
            with steps.loop(HEADS, 10) as h:
                q0 = (Q_HEAD, PER_HEAD, h)
                wait_done(act, q0)
                for d in range(2):
                    for part, s, n in BOTH:
                        ins = act.activation(zg[:, d, s:s + n], tile_psum(q0, d, part), ACT.Identity,
                                             bias=vec[:, 1, bass.ds(V_GB + 4 * d + h, 1)])
                        if d == 1 and part == 1:
                            moved(ins, q0)
                        else:
                            steps.mark(ins)
                wait_moved(act, q0)
                steps.link(act.activation(bcum[:], zg[:], ACT.Abs))
                steps.link(act.activation(bcum[:], bcum[:], ACT.Exp, scale=-1.0))
                act.activation(bcum[:], bcum[:], ACT.Ln, bias=1.0).then_inc(z_logged, 1)
                act.wait_ge(cum_ready, h + 1)
                steps.mark(act.activation(q_dec[:], bcum[:], ACT.Exp, scale=1.0 / TAU))
                steps.mark(act.activation(k_inv[:], bcum[:], ACT.Exp, scale=-1.0 / TAU))
                steps.mark(act.activation(k_end[:], zg[:], ACT.Exp, scale=1.0 / TAU))
                steps.mark(act.activation(decay[:, 0], bcum[:, 0, CHUNK - 1::CHUNK], ACT.Exp, scale=1.0 / TAU))
                act.activation(decay[:, 1], bcum[:, 1, 0::CHUNK], ACT.Exp, scale=1.0 / TAU).then_inc(exps_ready, 1)
                ch = (C_HEAD, 2, h)
                high(plus(ch, 2), plus(q0, 1))
                act.wait_ge(exps_ready, h + 1)
                wait_done(act, plus(q0, 2))
                moved(act.activation(v_tok[:].rearrange("p t n -> p (t n)"),
                                     duo(par(q0))[:].rearrange("p b n -> p (b n)"), ACT.Copy), plus(q0, 2))
                high(plus(ch, 3), plus(q0, 2))
                wait_done(act, plus(q0, 3))
                moved(act.activation(k_tok[:].rearrange("p t n -> p (t n)"),
                                     duo(par(plus(q0, 3)))[:].rearrange("p b n -> p (b n)"), ACT.Copy), plus(q0, 3))
                qo = plus(q0, 9)
                wait_done(act, qo)
                src = duo(par(qo))[:].rearrange("p b (t v n) -> p v (b t) n", t=2, v=2)
                steps.mark(act.activation(o_all[:, bass.ds(2 * h, 1)].rearrange("p o (t n) -> p (o t) n", n=P), src[:, 0],
                                          ACT.Copy))
                moved(act.activation(o_all[:, bass.ds(2 * h + 1, 1)].rearrange("p o (t n) -> p (o t) n", n=P), src[:, 1],
                                     ACT.Copy), qo)
            wait_moved(act, Q_HEAD + HEADS * PER_HEAD - 1)
            for h in range(HEADS):
                if h >= 2:
                    act.wait_ge(o_summed, h - 1)
                act.activation(o_sq[h % 2][:], o_all[:, 2 * h:2 * h + 2], ACT.Square).then_inc(o_squared, 1)
            for h in range(HEADS):
                wait_done(act, Q_NORM + h)
                for part, s, n in BOTH:
                    ins = act.activation(o_rinv[:, h, s:s + n], tile_psum(Q_NORM + h, 0, part), ACT.Sqrt,
                                         bias=eps[:, 0:1], scale=1.0 / 256)
                    if part:
                        moved(ins, Q_NORM + h)
            for h in range(HEADS):
                q = Q_G + h
                wait_done(act, q)
                if h >= 2:
                    act.wait_ge(gated, h - 1)
                act.activation(silu_g[h % 2][:, :, 0:LAT], part_psum(q, 0), ACT.Silu)
                moved(act.activation(silu_g[h % 2][:, :, LAT:TOK], part_psum(q, 1), ACT.Silu), q)
                high(C_G + h + 2, q)

            def split_out(layer, parts):
                src = o_all if layer == 0 else lru_o
                width = parts[-1][1] + parts[-1][2]
                last = Q_OUT0 - 1 if layer == 0 else Q_OUT1 - 1
                wait_done(act, last)
                if layer == 0:
                    act.wait_ge(gated, 4)
                else:
                    act.wait_ge(scanned, 5)
                for m in range(KT):
                    act.activation(a_hi[:, m, 0:width], src[:, m, 0:width], ACT.Copy).then_inc(hi_split, 1)
                c0, q0 = (C_OUT0, Q_OUT0) if layer == 0 else (C_OUT1, Q_OUT1)
                with act.Fori(0, 2) as i:
                    for b in range(2):
                        high((c0 + 2 + b, 2, i), (q0 + b, 2, i))

            def ffn(layer, parts):
                ch, q = (C_FFN0, Q_FFN0) if layer == 0 else (C_FFN1, Q_FFN1)
                for part, (first, n) in enumerate(FFN_PARTS):
                    with act.Fori(0, n // 2) as i:
                        wait_done(act, (q, 2, i))
                        act.wait_ge(duo_moved[(q + 1) % 2], half((q + 1, 2, i)))
                        for k, s, w in parts:
                            ins = act.activation(gate[:, :, s:s + w], part_psum(q, k), ACT.Silu)
                            if k == parts[-1][0]:
                                moved(ins, q)
                        high((ch + 2, 2, i), (q, 2, i))
                        high((ch + 3, 2, i), (q + 1, 2, i))
                    ch, q = ch + n, q + n
                    last = layer == 1 and part == len(FFN_PARTS) - 1
                    if last:
                        for b in range(2):
                            high(ch + 2 + b, q + b)
                    else:
                        with act.Fori(0, 2) as i:
                            for b in range(2):
                                high((ch + 2 + b, 2, i), (q + b, 2, i))
                    ch, q = ch + 4, q + 4

            split_out(0, BOTH)
            prep(0, 1, BOTH, Q_OUT0)
            ffn(0, BOTH)
            prep(1, 0, BOTH, Q_FFN0 + FFN_DUOS - 4)
            with steps.loop(2, 44) as i:
                for b in range(2):
                    q0, ch, n = (Q_LRU + 6 * b, 12, i), (C_LRU + 3 * b, 6, i), 2 * i + b
                    wait_done(act, q0)
                    steps.mark(act.activation(u_pad[:, :, 2:2 + LAT], part_psum(q0, 0), ACT.Copy))
                    moved(act.activation(u_pad[:, :, 2 + LAT + GAP:2 + UW], part_psum(q0, 1), ACT.Copy), q0)
                    act.wait_ge(gates_loaded, 32 * n + 32)
                    high(plus(ch, 2), q0)
                    act.wait_ge(conv_done, n + 1)
                    act.wait_ge(scanned, n + 1)
                    steps.mark(act.activation(u_hi[:, :, 0:LAT], u_conv[:, :, 0:LAT], ACT.Copy))
                    act.activation(u_hi[:, :, LAT:TOK], u_conv[:, :, LAT + GAP:UW], ACT.Copy).then_inc(u_rounded, 1)
                    wait_done(act, plus(q0, 1))
                    moved(act.activation(lru_y[:], part_psum(plus(q0, 1), 0), ACT.Gelu_apprx_tanh), plus(q0, 1))
                    high(plus(ch, 3), plus(q0, 1))
                    for gi in range(4):
                        q = plus(q0, 2 + gi)
                        col = (V_BA if gi < 2 else V_BX) + 8 * (gi % 2)
                        wait_done(act, q)
                        for t in range(2):
                            for part, s, w in BOTH:
                                ins = act.activation(gates_r[:, gi, t, s:s + w], tile_psum(q, t, part), ACT.Sigmoid,
                                                     bias=vec[:, 1, bass.ds(col + 2 * n + t, 1)])
                                if t == 1 and part == 1:
                                    moved(ins, q)
                                else:
                                    steps.mark(ins)
                    wait_moved(act, plus(q0, 4))
                    wait_moved(act, plus(q0, 5))
                    act.wait_ge(lruc_ready, 1)
                    for d in range(2):
                        for t in range(2):
                            steps.mark(act.activation(scan_h[d][:, t], gates_r[:, d, t], ACT.Tanh,
                                                      scale=lru_c[:, 0, bass.ds(8 * d + 2 * n + t, 1)]))
                    steps.wait()
                    for d in range(2):
                        for t in range(2):
                            steps.mark(act.activation(gates_r[:, d, t], gates_r[:, d, t], ACT.Exp,
                                                      scale=lru_c[:, 1, bass.ds(8 * d + 2 * n + t, 1)]))
                    steps.wait()
                    for d in range(2):
                        act.wait_ge(factor, 3 * n + 1 + d)
                        act.activation(u_conv[:, :, 0:TOK], gates_r[:, d], ACT.Square).then_inc(a_sq, 1)
                    for d in range(2):
                        act.wait_ge(factor, 3 * n + 2 + d)
                        act.activation(scan_h[d][:], scan_h[d][:], ACT.Sqrt).then_inc(root, 1)
                    high(plus(ch, 4), plus(q0, 5))
            split_out(1, ONLY_LAT)
            prep(1, 1, ONLY_LAT, Q_OUT1)
            ffn(1, ONLY_LAT)
            for t in range(4):
                q = Q_FINAL + t
                wait_done(act, q)
                steps.link(act.activation(y_junk[:], duo(q)[:, 0:2, :].rearrange("p b n -> p (b n)"), ACT.Square,
                                          accum_out=ysum[:, 0, t:t + 1]))
                act.activation(ysum[:, 1, t:t + 1], ysum[:, 0, t:t + 1], ACT.Sqrt, bias=eps[:, 0:1], scale=1.0 / D
                               ).then_inc(y_rooted, 1)

        @block.vector
        def _(dve):
            steps = Steps(dve, dve_step)

            def part_psum(q, part):
                ps = duo(par(q))
                return ps[:, 0:2, :] if part == 0 else ps[:, 2, :].rearrange("p (t n) -> p t n", t=2)

            def tile_psum(q, t, part):
                ps = duo(par(q))
                return ps[:, t, :] if part == 0 else ps[:, 2, t * CTX:(t + 1) * CTX]

            def section(s, row):
                dve.wait_ge(mod_used, 8 * whole(s) - 6 if isinstance(s, tuple) else (s + 1 if s < 2 else 8 * s - 6))
                r = whole(row)
                dve.tensor_tensor(mod[:, bass.ds(r, 1)].rearrange("p o m v -> p (o m) v"),
                                  mod_psum[:, 0:16].rearrange("p (m v) -> p m v", v=2),
                                  vec[:, 0, bass.ds(V_BMOD + 8 * r, 8)].unsqueeze(2).broadcast_to([P, 8, 2]),
                                  ALU.add).then_inc(mod_ready, 1)

            def prep(layer, which, parts):
                n = 2 * layer + which
                width = parts[-1][1] + parts[-1][2]
                g = vec[:, 0, (V_NMIX if which == 0 else V_NFFN) + 8 * layer:][:, 0:8]
                sec = 6 * layer + 3 * which
                dve.wait_ge(mod_ready, [1, 6, 10, 12][n])
                steps.link(dve.scalar_tensor_tensor(out=gain[:, n], in0=mod[:, sec + 1], scalar=1.0,
                                                    in1=g.unsqueeze(2).broadcast_to([P, 8, 2]), op0=ALU.add,
                                                    op1=ALU.mult))
                for m in range(KT):
                    dve.wait_ge(squared, 8 * n + m + 1)
                    if m == 0:
                        ins = dve.tensor_copy(sqsum[:, 0:width], sq[0][:, 0:width])
                    else:
                        dve.wait_ge(summed, 8 * n + m)
                        ins = dve.tensor_tensor(sqsum[:, 0:width], sqsum[:, 0:width], sq[m % 2][:, 0:width], ALU.add)
                    ins.then_inc(summed, 1)
                if n == 0:
                    section(1, SEC_FIRST[1])
                wait_moved(dve, Q_STAT[layer][which])
                steps.link(dve.reciprocal(rinv[:, 0:width], rinv[:, 0:width]))
                if n == 0:
                    dve.wait_ge(mod_ready, 2)

                def scale(m):
                    if m >= 2:
                        dve.wait_ge(hi_split, HI_SPLIT[n] + m - 1)
                    for part, s, w in parts:
                        ins = dve.scalar_tensor_tensor(out=normed[m % 2][:, s:s + w], in0=xres[:, m, s:s + w],
                                                       scalar=gain[:, n, m, part:part + 1], in1=rinv[:, s:s + w],
                                                       op0=ALU.mult, op1=ALU.mult)
                    ins.then_inc(scaled, 1)

                scale(0)
                for m in range(KT):
                    if m + 1 < KT:
                        if m >= 1:
                            dve.wait_ge(a_ready, 8 * A_ORDER[("prep", layer, which)] + m)
                        scale(m + 1)
                    dve.wait_ge(hi_split, HI_SPLIT[n] + m + 1)
                    for part, s, w in parts:
                        dst, hi, src = a_lo[:, m, s:s + w], a_hi[:, m, s:s + w], normed[m % 2][:, s:s + w]
                        if part == 0 and (layer, which) == (1, 0):
                            dst = dst.rearrange("p (c r) -> p r c", r=ROWS)
                            hi = hi.rearrange("p (c r) -> p r c", r=ROWS)
                            src = src.rearrange("p (r c) -> p r c", r=ROWS)
                        ins = dve.scalar_tensor_tensor(out=dst, in0=src, scalar=mod[:, sec, m, part:part + 1],
                                                       in1=hi.bitcast(F32), op0=ALU.add, op1=ALU.subtract)
                    ins.then_inc(a_ready, 1)

            dve.wait_ge(vec_turned, 1)
            steps.mark(dve.tensor_copy(vec[:, 0], vec_psum[:, 0:P]))
            dve.tensor_copy(vec[:, 1, 0:V_END], vec_psum[:, P:P + V_END]).then_inc(vec_ready, 1)
            dve.wait_ge(vec_ready, 1)
            steps.wait()
            lam = vec[:, 1, V_LAM:V_LAM + 16]
            steps.link(dve.tensor_scalar(lw[:, 1], lam, -1.0, 0.0, ALU.mult, ALU.max))
            steps.link(dve.tensor_scalar(lw[:, 2], lam, 0.0, None, ALU.max))
            dve.tensor_tensor(lw[:, 3], lw[:, 1], lw[:, 2], ALU.add).then_inc(l_w, 1)
            for i in (0, 2):
                q = Q_TURN + i
                wait_done(dve, q)
                steps.mark(dve.tensor_copy(xres[:, 2 * i:2 * i + 2, 0:LAT], part_psum(q, 0)))
                moved(dve.tensor_copy(xres[:, 2 * i:2 * i + 2, LAT:TOK], part_psum(q, 1)), q)
            dve.wait_ge(l_exp, 1)
            steps.link(dve.tensor_scalar(lw[:, 2], lw[:, 0], 2.0, None, ALU.add))
            steps.link(dve.reciprocal(lw[:, 2], lw[:, 2]))
            steps.link(dve.tensor_tensor(lw[:, 0], lw[:, 0], lw[:, 2], ALU.mult))
            steps.link(dve.tensor_tensor(lw[:, 2], lw[:, 0], lw[:, 0], ALU.mult))
            steps.link(dve.tensor_scalar(lw[:, 3], lw[:, 2], 1.0 / 15, 1.0 / 13, ALU.mult, ALU.add))
            for odd in (11, 9, 7, 5, 3, 1):
                steps.link(dve.tensor_tensor(lw[:, 3], lw[:, 3], lw[:, 2], ALU.mult))
                steps.link(dve.tensor_scalar(lw[:, 3], lw[:, 3], 1.0 / odd, None, ALU.add))
            steps.link(dve.tensor_tensor(lw[:, 3], lw[:, 3], lw[:, 0], ALU.mult))
            steps.link(dve.scalar_tensor_tensor(out=lw[:, 0], in0=lw[:, 3], scalar=2.0, in1=lw[:, 1], op0=ALU.mult,
                                                op1=ALU.add))
            steps.mark(dve.tensor_scalar(lru_c[:, 0], lw[:, 0], LRU_C, None, ALU.mult))
            dve.tensor_scalar(lru_c[:, 1], lw[:, 0], -LRU_C, None, ALU.mult).then_inc(lruc_ready, 1)
            section(0, SEC_FIRST[0])
            dve.memset(gate2[:], 0.0).then_inc(gate2_zeroed, 1)
            dve.wait_ge(mod_ready, 1)
            for i in range(4):
                wait_moved(dve, Q_TURN + i)
            prep(0, 0, BOTH)

            dve.wait_ge(consts_made, 1)
            reset_row = resets[:].rearrange("p n c -> p (n c)")
            with steps.loop(HEADS, 30) as h:
                q0 = (Q_HEAD, PER_HEAD, h)
                dve.wait_ge(z_logged, h + 1)
                steps.link(dve.scalar_tensor_tensor(out=zg[:], in0=zg[:], scalar=0.0, in1=bcum[:], op0=ALU.min,
                                                    op1=ALU.subtract))
                steps.mark(dve.tensor_tensor_scan(bcum[:, 0], reset_row, zg[:, 0], 0.0, ALU.mult, ALU.add))
                steps.link(dve.tensor_tensor_scan(bcum[:, 1, ::-1], reset_row, zg[:, 1, ::-1], 0.0, ALU.mult, ALU.add))
                for d, last in ((0, CHUNK - 1), (1, 0)):
                    b4 = bcum[:, d].rearrange("p (n c) -> p n c", c=CHUNK)
                    ins = dve.tensor_tensor(zg[:, d].rearrange("p (n c) -> p n c", c=CHUNK),
                                            b4[:, :, last:last + 1].broadcast_to([P, NCH, CHUNK]), b4, ALU.subtract)
                    if d == 0:
                        steps.mark(ins)
                ins.then_inc(cum_ready, 1)
                dve.wait_ge(exps_ready, h + 1)
                q1 = plus(q0, 1)
                wait_done(dve, q1)
                for part, s, n in BOTH:
                    qp = tile_psum(q1, 0, part).unsqueeze(1).broadcast_to([P, 2, n])
                    steps.mark(dve.scalar_tensor_tensor(out=q_dec[:, :, s:s + n], in0=qp, scalar=DK_SCALE,
                                                        in1=q_dec[:, :, s:s + n], op0=ALU.mult, op1=ALU.mult))
                for n_, buf in enumerate((k_inv, k_end)):
                    for part, s, n in BOTH:
                        kp = tile_psum(q1, 1, part).unsqueeze(1).broadcast_to([P, 2, n])
                        ins = dve.tensor_tensor(buf[:, :, s:s + n], kp, buf[:, :, s:s + n], ALU.mult)
                        if n_ == 1 and part == 1:
                            moved(ins, q1)
                        else:
                            steps.mark(ins)
                section((SEC_HEAD, 1, h), (2, 1, h))
                qa = plus(q0, 4)
                wait_done(dve, qa)
                steps.link(dve.memset(att[:], 0.0))
                steps.mark(dve.memset(zero[:], 0.0))
                for d in range(2):
                    flat = duo(par(qa))[:].rearrange("p b n -> p (b n)")[:, d * TOK:(d + 1) * TOK]
                    ins = dve.copy_predicated(att[:, 6 * d:6 * d + 6], mask[:, d].bitcast(I32).unsqueeze(1).broadcast_to([P, 6, P]),
                                              flat.rearrange("p (t n) -> p t n", n=P))
                    if d == 0:
                        steps.mark(ins)
                moved(ins, qa)
                for g, (d, chunks) in enumerate(STATE_GROUPS):
                    qu = plus(q0, 5 + g)
                    wait_done(dve, qu)
                    for s, n in enumerate(chunks):
                        u = state_psum(qu, s)
                        new = STATE_AFTER[d][n]
                        if STATE_BEFORE[d][n] is None:
                            ins = dve.tensor_copy(states[:, new], u)
                        else:
                            ins = dve.scalar_tensor_tensor(out=states[:, new], in0=states[:, STATE_BEFORE[d][n]],
                                                           scalar=decay[:, d, n:n + 1], in1=u, op0=ALU.mult,
                                                           op1=ALU.add)
                        if s == len(chunks) - 1:
                            moved(ins, qu)
                            wait_moved(dve, qu)
                        else:
                            steps.link(ins)
            for h in range(HEADS):
                dve.wait_ge(o_squared, h + 1)
                dve.tensor_tensor(o_sum[h % 2][:], o_sq[h % 2][:, 0], o_sq[h % 2][:, 1], ALU.add).then_inc(o_summed, 1)
                if h >= 1:
                    wait_moved(dve, Q_NORM + h - 1)
                    dve.reciprocal(o_rinv[:, h - 1], o_rinv[:, h - 1]).then_inc(rinv_ready, 1)
            wait_moved(dve, Q_NORM + HEADS - 1)
            dve.reciprocal(o_rinv[:, HEADS - 1], o_rinv[:, HEADS - 1]).then_inc(rinv_ready, 1)
            dve.wait_ge(rinv_ready, HEADS)
            for h in range(HEADS):
                for t in range(2):
                    o = o_all[:, 2 * h + t]
                    steps.mark(dve.scalar_tensor_tensor(out=o, in0=o, scalar=vec[:, 1, V_HN + t:V_HN + t + 1],
                                                        in1=o_rinv[:, h], op0=ALU.mult, op1=ALU.mult))
                steps.wait()
                wait_moved(dve, Q_G + h)
                o = o_all[:, 2 * h:2 * h + 2]
                dve.tensor_tensor(o, o, silu_g[h % 2][:], ALU.mult).then_inc(gated, 1)

            def project_out(layer, parts):
                src = o_all if layer == 0 else lru_o
                width = parts[-1][1] + parts[-1][2]
                n = 8 if layer == 0 else 32
                for m in range(KT):
                    dve.wait_ge(hi_split, n + m + 1)
                    dve.tensor_tensor(a_lo[:, m, 0:width], src[:, m, 0:width], a_hi[:, m, 0:width].bitcast(F32),
                                      ALU.subtract).then_inc(a_ready, 1)
                q0 = Q_OUT0 if layer == 0 else Q_OUT1
                residual_loop(q0, layer, 2, parts, permuted=layer == 1)

            def residual_loop(q0, layer, place_, parts, permuted=False):
                with steps.loop(2, 2 * (2 * len(parts) - 1)) as i:
                    for b in range(2):
                        q, tile = (q0 + b, 2, i), 4 * i + 2 * b
                        wait_done(dve, q)
                        for t in range(2):
                            for part, s, w in parts:
                                xt = xres[:, bass.ds(tile + t, 1), s:s + w].rearrange("p o n -> p (o n)")
                                src = tile_psum(q, t, part)
                                if permuted:
                                    xt = xt.rearrange("p (r c) -> p r c", r=ROWS)
                                    src = src.rearrange("p (c r) -> p r c", r=ROWS)
                                g = mod[:, 6 * layer + place_, bass.ds(tile + t, 1), part:part + 1]
                                ins = dve.scalar_tensor_tensor(out=xt, in0=src, scalar=g.rearrange("p o n -> p (o n)"),
                                                               in1=xt, op0=ALU.mult, op1=ALU.add)
                                if t == 1 and part == parts[-1][0]:
                                    moved(ins, q)
                                else:
                                    steps.mark(ins)
                        wait_moved(dve, q)

            def ffn(layer, parts):
                q = Q_FFN0 if layer == 0 else Q_FFN1
                width = parts[-1][1] + parts[-1][2]
                for part, (first, n) in enumerate(FFN_PARTS):
                    with steps.loop(n // 2, 2 if len(parts) == 2 else 1) as i:
                        wait_moved(dve, (q, 2, i))
                        wait_done(dve, (q + 1, 2, i))
                        for k, s, w in parts:
                            ins = dve.tensor_tensor(hid[:, :, s:s + w], part_psum(q + 1, k), gate[:, :, s:s + w], ALU.mult)
                            if k == parts[-1][0]:
                                moved(ins, q + 1)
                            else:
                                steps.mark(ins)
                        wait_moved(dve, (q + 1, 2, i))
                        hh = h_hi[:, bass.ds(2 * i, 2), 0:width]
                        steps.link(dve.tensor_copy(hh, hid[:, :, 0:width]))
                        dve.tensor_tensor(h_lo[:, bass.ds(2 * i, 2), 0:width], hid[:, :, 0:width], hh.bitcast(F32),
                                          ALU.subtract).then_inc(hid_ready, 1)
                        dve.wait_ge(hid_ready, HID[layer][part] + i + 1)
                        if layer == 0 and part == 0:
                            section((SEC_HEAD + HEADS, 1, i), (6, 1, i))
                    q += n
                    residual_loop(q, layer, 5, parts)
                    q += 4

            project_out(0, BOTH)
            prep(0, 1, BOTH)
            ffn(0, BOTH)
            prep(1, 0, BOTH)
            dve.wait_ge(a_ready, 8 * (A_ORDER[("prep", 1, 0)] + 1))
            for lo_, hi_ in ((0, 2), (2 + LAT, 2 + LAT + GAP), (2 + UW, UW + 4)):
                ins = dve.memset(u_pad[:, :, lo_:hi_], 0.0)
            ins.then_inc(scanned, 1)
            dve.wait_ge(scanned, 1)
            with steps.loop(2, 44) as i:
                for b in range(2):
                    q0, n = (Q_LRU + 6 * b, 12, i), 2 * i + b
                    wait_moved(dve, q0)
                    for j in range(CONV_W):
                        for t in range(2):
                            col = vec[:, 1, bass.ds(V_CW + 8 * j + 2 * n + t, 1)]
                            if j == 0:
                                ins = dve.tensor_scalar(u_conv[:, t], u_pad[:, t, 0:UW], col,
                                                        vec[:, 1, bass.ds(V_CB + 2 * n + t, 1)], ALU.mult, ALU.add)
                            else:
                                ins = dve.scalar_tensor_tensor(out=u_conv[:, t], in0=u_pad[:, t, j:j + UW], scalar=col,
                                                               in1=u_conv[:, t], op0=ALU.mult, op1=ALU.add)
                            if j == CONV_W - 1 and t == 1:
                                ins.then_inc(conv_done, 1)
                            else:
                                steps.mark(ins)
                        if j < CONV_W - 1:
                            steps.wait()
                    dve.wait_ge(u_rounded, n + 1)
                    steps.mark(dve.tensor_tensor(u_lo[:, :, 0:LAT], u_conv[:, :, 0:LAT], u_hi[:, :, 0:LAT].bitcast(F32),
                                                 ALU.subtract))
                    dve.tensor_tensor(u_lo[:, :, LAT:TOK], u_conv[:, :, LAT + GAP:UW], u_hi[:, :, LAT:TOK].bitcast(F32),
                                      ALU.subtract).then_inc(u_ready, 1)
                    for d in range(2):
                        wait_moved(dve, plus(q0, 4 + d))
                        g = gates_r[:, 2 + d]
                        steps.mark(dve.tensor_tensor(g[:, :, 0:LAT], g[:, :, 0:LAT], u_conv[:, :, 0:LAT], ALU.mult))
                        ins = dve.tensor_tensor(g[:, :, LAT:TOK], g[:, :, LAT:TOK], u_conv[:, :, LAT + GAP:UW], ALU.mult)
                        if d == 0:
                            steps.mark(ins)
                    ins.then_inc(factor, 1)
                    for d in range(2):
                        dve.wait_ge(a_sq, 2 * n + d + 1)
                        dve.scalar_tensor_tensor(out=scan_h[d][:], in0=u_conv[:, :, 0:TOK], scalar=1.0, in1=scan_h[d][:],
                                                 op0=ALU.add, op1=ALU.mult).then_inc(factor, 1)
                    dve.wait_ge(factor, 3 * n + 3)
                    for d in range(2):
                        dve.wait_ge(root, 2 * n + d + 1)
                        g = gates_r[:, 2 + d]
                        steps.link(dve.tensor_tensor(g, g, scan_h[d][:], ALU.mult))
                        order_ = slice(None, None, -1) if d else slice(None)
                        for t in range(2):
                            a_, b_, o_ = gates_r[:, d, t], gates_r[:, 2 + d, t], scan_h[d][:, t]
                            cx = [v[:, LAT:TOK][:, order_] for v in (o_, a_, b_)]
                            steps.mark(dve.tensor_tensor_scan(*cx, 0.0, ALU.mult, ALU.add))
                        steps.wait()
                        for t in range(2):
                            a_, b_, o_ = gates_r[:, d, t], gates_r[:, 2 + d, t], scan_h[d][:, t]
                            lt = [v[:, 0:LAT][:, order_] for v in (o_, a_, b_)]
                            last = o_[:, LAT:LAT + 1] if d else o_[:, TOK - 1:TOK]
                            steps.mark(dve.tensor_tensor_scan(*lt, last, ALU.mult, ALU.add))
                        steps.wait()
                    steps.link(dve.tensor_tensor(scan_h[0][:, :, 0:LAT], scan_h[0][:, :, 0:LAT], scan_h[1][:, :, 0:LAT],
                                                 ALU.add))
                    wait_moved(dve, plus(q0, 1))
                    dve.tensor_tensor(lru_o[:, bass.ds(2 * n, 2)], scan_h[0][:, :, 0:LAT], lru_y[:], ALU.mult
                                      ).then_inc(scanned, 1)
                    if b == 0:
                        section((SEC_HEAD + HEADS + 4, 1, i), (10, 1, i))
            project_out(1, ONLY_LAT)
            prep(1, 1, ONLY_LAT)
            ffn(1, ONLY_LAT)
            dve.wait_ge(final_g_loaded, 16)
            for t in range(4):
                q = Q_FINAL + t
                dve.wait_ge(y_rooted, t + 1)
                steps.link(dve.reciprocal(ysum[:, 2, t:t + 1], ysum[:, 1, t:t + 1]))
                moved(dve.scalar_tensor_tensor(out=y_rows[t][:], in0=duo(q)[:, 0:2, :].rearrange("p b n -> p (b n)"),
                                               scalar=ysum[:, 2, t:t + 1], in1=final_g[:], op0=ALU.mult,
                                               op1=ALU.mult), q)


SCAN = [[8, 9, 10, 11, 0, 1, 2, 3, 4, 5, 6, 7], [11, 10, 9, 8, 7, 6, 5, 4, 3, 2, 1, 0]]
STATE_BASE = [11, 0]
STATE_AFTER = [{n: STATE_BASE[d] + s for s, n in enumerate(SCAN[d][:11])} for d in range(2)]
STATE_BEFORE = [{n: (STATE_BASE[d] + s - 1 if s else None) for s, n in enumerate(SCAN[d])} for d in range(2)]
STATE_GROUPS = [(1, SCAN[1][0:6]), (1, SCAN[1][6:11]), (0, SCAN[0][0:6]), (0, SCAN[0][6:11])]
HID = [[0, 4, 8], [11, 15, 19]]
HI_SPLIT = [0, 16, 24, 40]
A_ORDER = {("prep", 0, 0): 0, ("out", 0): 1, ("prep", 0, 1): 2, ("prep", 1, 0): 3, ("out", 1): 4, ("prep", 1, 1): 5}


_INS = ["x", "c", "ctx", "c_ctx", "norm_mix_g", "norm_ffn_g", "w_mod", "b_mod", "gla_w_in", "gla_gate_w1",
        "gla_gate_w2", "gla_gate_b", "gla_head_norm_g", "gla_w_out", "lru_w_in", "lru_conv_w", "lru_conv_b",
        "lru_gate_a_w", "lru_gate_a_b", "lru_gate_x_w", "lru_gate_x_b", "lru_lambda", "lru_w_out", "ffn_w1",
        "ffn_w3", "ffn_w2", "final_norm_g"]


def kernel(**inputs):
    import numpy as _np
    import concourse.bacc as _bacc
    from concourse import mybir as _mybir
    from concourse.bass_utils import run_bass_kernel_spmd as _run

    nc = _bacc.Bacc("TRN2", target_bir_lowering=False, num_devices=1)
    arrays, args = {}, []
    for name in _INS:
        a = _np.ascontiguousarray(inputs[name])
        arrays[f"in_{name}_dram"] = a
        args.append(nc.dram_tensor(f"in_{name}_dram", a.shape, _mybir.dt.from_np(a.dtype), kind="ExternalInput").ap())
    args.append(nc.dram_tensor("out_dram", (1, LAT, D), _mybir.dt.float32, kind="ExternalOutput").ap())
    build(nc, *args)
    r = _run(nc, [arrays], core_ids=[0])
    return r.results[0]["out_dram"]
```

```python
from contextlib import ExitStack, contextmanager

import concourse.bass as bass
from concourse import mybir

P = 128
F32 = mybir.dt.float32
F32R = mybir.dt.float32r
BF16 = mybir.dt.bfloat16
I32 = mybir.dt.int32
ALU = mybir.AluOpType
ACT = mybir.ActivationFunctionType

LAT, CTX = 512, 256
TOK = LAT + CTX
D = 1024
KT = D // P
HEADS = 4
CHUNK = 64
NCH = TOK // CHUNK
TT = TOK // P
TAU = 16.0
RANK = 16
EPS = 1e-6
GRID_W = 64
ROWS = LAT // GRID_W
FFN = 2816
FT = FFN // P
FFN_PARTS = [(0, 8), (8, 8), (16, 6)]
CONV_W = 4
LRU_C = 8.0
DK_SCALE = float(P) ** -0.5
BOTH = [(0, 0, LAT), (1, LAT, CTX)]
ONLY_LAT = [(0, 0, LAT)]

Q_TURN = 0
Q_STAT = [[4, 58], [0, 0]]
Q_T = 5
Q_HEAD = 6
PER_HEAD = 10
Q_NORM = Q_HEAD + HEADS * PER_HEAD
Q_G = Q_NORM + HEADS
Q_OUT0 = Q_G + 4
Q_STAT[0][1] = Q_OUT0 + 4
Q_FFN0 = Q_STAT[0][1] + 1
FFN_DUOS = sum(n + 4 for _, n in FFN_PARTS)
Q_STAT[1][0] = Q_FFN0 + FFN_DUOS
Q_LRU = Q_STAT[1][0] + 1
PER_BLOCK = 6
Q_OUT1 = Q_LRU + 4 * PER_BLOCK
Q_STAT[1][1] = Q_OUT1 + 4
Q_FFN1 = Q_STAT[1][1] + 1
Q_FINAL = Q_FFN1 + FFN_DUOS

C_GATE1 = 0
C_HEAD = 1
C_G = C_HEAD + 2 * HEADS
C_OUT0 = C_G + 4
C_FFN0 = C_OUT0 + 4
C_LRU = C_FFN0 + FFN_DUOS
C_OUT1 = C_LRU + 12
C_FFN1 = C_OUT1 + 4
CHUNKS = C_FFN1 + FFN_DUOS
assert (CHUNKS - 1) % 2 == 0

SEC_FIRST = [1, 0]
SEC_HEAD = 2
V_BMOD, V_NMIX, V_NFFN = 0, 96, 112
V_C, V_GB, V_HN, V_CW, V_CB, V_BA, V_BX, V_LAM, V_END = 0, 16, 24, 26, 58, 66, 82, 98, 114


class Steps:

    def __init__(self, eng, sem):
        self.eng, self.sem, self.base, self.k, self.i, self.per = eng, sem, 0, 0, 0, 0

    def mark(self, ins):
        ins.then_inc(self.sem, 1)
        self.k += 1

    def wait(self):
        self.eng.wait_ge(self.sem, self.base + self.i * self.per + self.k)

    def link(self, ins):
        self.mark(ins)
        self.wait()

    @contextmanager
    def loop(self, n, per):
        self.base, self.k, self.per = self.base + self.k, 0, per
        with self.eng.Fori(0, n) as i:
            self.i = i
            yield i
        assert self.k == per, (self.k, per)
        self.base, self.k, self.i, self.per = self.base + n * per, 0, 0, 0


def build(nc, x, c, ctx_in, c_ctx, norm_mix_g, norm_ffn_g, w_mod, b_mod, gla_w_in, gla_gate_w1, gla_gate_w2,
          gla_gate_b, gla_head_norm_g, gla_w_out, lru_w_in, lru_conv_w, lru_conv_b, lru_gate_a_w, lru_gate_a_b,
          lru_gate_x_w, lru_gate_x_b, lru_lambda, lru_w_out, ffn_w1, ffn_w3, ffn_w2, final_norm_g, out):
    es = ExitStack()
    with es:
        at = [-(-nc.sbuf_base // 64) * 64]

        def region(nbytes):
            start = at[0]
            at[0] += -(-nbytes // 32) * 32
            assert at[0] <= nc.sbuf_usable_end, at[0]
            return start

        def place(name, shape, dt, offset):
            return nc.alloc_sbuf_tensor_at(name, shape, dt, offset=offset)

        KB = 1024
        X_AT, A_AT, H_AT = region(24 * KB), region(48 * KB), region(48 * KB)
        W_AT, M_AT, T_AT = region(48 * KB), region(8 * KB), region(24 * KB)

        def small(name, shape, dt=F32):
            n = 2 if dt == BF16 else 4
            for s in shape[1:]:
                n *= s
            return place(name, shape, dt, region(n))

        xres = place("xres", [P, KT, TOK], F32, X_AT)
        a_hi = place("a_hi", [P, KT, TOK], F32R, A_AT)
        a_lo = place("a_lo", [P, KT, TOK], F32R, A_AT + 24 * KB)
        h_hi = place("h_hi", [P, 8, TOK], F32R, H_AT)
        h_lo = place("h_lo", [P, 8, TOK], F32R, H_AT + 24 * KB)
        raw = [place(f"raw{b}", [P, 8, 256], F32, W_AT + 8 * KB * b) for b in range(2)]
        w_hi = [place(f"w_hi{b}", [P, 8, 256], F32R, W_AT + 8 * KB * (2 + b)) for b in range(2)]
        w_lo = [place(f"w_lo{b}", [P, 8, 256], F32R, W_AT + 8 * KB * (4 + b)) for b in range(2)]
        mod_ring = [place(f"mod_ring{b}", [P, 8, P], F32, M_AT + 4 * KB * b) for b in range(2)]
        sec_rows = place("sec_rows", [2, 512], F32, H_AT + 46 * KB)
        first_rows = place("first_rows", [2, D], F32, T_AT + 18 * KB)
        mod_first = [place("mod_first0", [P, 8, D], F32, H_AT), place("mod_first1", [P, 8, D], F32, A_AT)]
        vec_rows = place("vec_rows", [P, 2, P], F32, A_AT + 32 * KB)
        x_rows = place("x_rows", [P, TT, D], F32, T_AT)
        sq = [place(f"sq{b}", [P, 2, TOK], F32, T_AT + 6 * KB * b) for b in range(2)]
        sqsum = place("sqsum", [P, TOK], F32, T_AT + 12 * KB)
        rinv = place("rinv", [P, TOK], F32, T_AT + 15 * KB)
        normed = [place(f"normed{b}", [P, TOK], F32, T_AT + 18 * KB + 3 * KB * b) for b in range(2)]
        o_all = place("o_all", [P, 8, TOK], F32, H_AT)
        t_low = place("t_low", [64, TOK], F32, H_AT + 18 * KB)
        gate2 = place("gate2", [64, 2, P], F32, H_AT + 22 * KB)
        states = place("states", [P, 22, 256], F32, H_AT + 24 * KB)
        k_end = place("k_end", [P, 2, TOK], F32, H_AT + (24 + 16) * KB)
        q_dec = place("q_dec", [P, 2, TOK], F32, T_AT)
        k_inv = place("k_inv", [P, 2, TOK], F32, T_AT + 6 * KB)
        att = place("att", [P, 12, P], F32, T_AT + 6 * KB)
        zg = place("zg", [P, 2, TOK], F32, T_AT + 12 * KB)
        k_tok = place("k_tok", [P, 12, P], F32, T_AT + 12 * KB)
        bcum = place("bcum", [P, 2, TOK], F32, T_AT + 18 * KB)
        v_tok = place("v_tok", [P, TT, 256], F32, T_AT + 18 * KB)
        o_sq = [place(f"o_sq{b}", [P, 2, TOK], F32, T_AT + 6 * KB * b) for b in range(2)]
        o_sum = [place(f"o_sum{b}", [P, TOK], F32, T_AT + 12 * KB + 3 * KB * b) for b in range(2)]
        silu_g = [place(f"silu_g{b}", [P, 2, TOK], F32, T_AT + 18 * KB - 6 * KB * b) for b in range(2)]
        o_rinv = place("o_rinv", [P, HEADS, TOK], F32, H_AT + 24 * KB)
        gate = place("gate", [P, 2, TOK], F32, T_AT)
        hid = place("hid", [P, 2, TOK], F32, T_AT + 6 * KB)
        GAP = 2
        UW = LAT + GAP + CTX
        lru_o = place("lru_o", [P, 8, LAT], F32, H_AT)
        lru_y = place("lru_y", [P, 2, LAT], F32, H_AT + 16 * KB)
        gates_r = place("gates_r", [P, 4, 2, TOK], F32, H_AT + 20 * KB)
        U_AT = H_AT + 44 * KB
        u_hi = place("u_hi", [P, 2, TOK], F32R, T_AT)
        u_lo = place("u_lo", [P, 2, TOK], F32R, T_AT + 6 * KB)
        scan_h = [place(f"scan_h{b}", [P, 2, TOK], F32, T_AT + 6 * KB * b) for b in range(2)]
        u_pad = place("u_pad", [P, 2, UW + 4], F32, T_AT + 12 * KB)
        UP_END = T_AT + 12 * KB + 2 * 4 * (UW + 4)
        u_conv = place("u_conv", [P, 2, UW], F32, -(-UP_END // 32) * 32)
        assert UP_END + 32 + 8 * UW <= T_AT + 24 * KB + 1024
        final_g = place("final_g", [P, D], F32, M_AT)
        y_rows = [place(f"y_rows{b}", [P, D], F32, T_AT + 4 * KB * b) for b in range(4)]
        y_junk = place("y_junk", [P, D], F32, T_AT + 16 * KB)
        region(512)

        ident = small("ident", [P, P])
        ones = small("ones", [P, P])
        mask = small("mask", [P, 2, P])
        resets = small("resets", [P, NCH, CHUNK], BF16)
        vec = small("vec", [P, 2, P])
        cs = small("cs", [P, KT, 2])
        mod = small("mod", [P, 2 * 6, KT, 2])
        gain = small("gain", [P, 4, KT, 2])
        decay = small("decay", [P, 2, NCH])
        lru_c = small("lru_c", [P, 2, 16])
        lw = small("lw", [P, 4, 16])
        eps = small("eps", [P, 1])
        zero = small("zero", [P, 1])
        ysum = small("ysum", [P, 3, 4])

        duo_psum = [es.enter_context(nc.psum_tensor(f"duo{b}", [P, 3, 512], F32)) for b in range(2)]
        vec_psum = es.enter_context(nc.psum_tensor("vec_psum", [P, 512], F32))
        mod_psum = es.enter_context(nc.psum_tensor("mod_psum", [P, 512], F32))

        def sem(name):
            return es.enter_context(nc.semaphore(name))

        consts_made, pads_made = sem("consts_made"), sem("pads_made")
        vec_loaded, x_loaded = sem("vec_loaded"), sem("x_loaded")
        first_loaded = [[sem(f"first_loaded{b}_{k}") for k in range(4)] for b in range(2)]
        vec_turned, vec_ready, cs_ready = sem("vec_turned"), sem("vec_ready"), sem("cs_ready")
        raw_loaded = [sem(f"raw_loaded{b}") for b in range(2)]
        hi_ready, lo_ready = sem("hi_ready"), sem("lo_ready")
        mod_loaded = [sem(f"mod_loaded{b}") for b in range(2)]
        mod_used, mod_rowed, mod_turned, mod_ready = (sem("mod_used"), sem("mod_rowed"), sem("mod_turned"),
                                                      sem("mod_ready"))
        gate2_zeroed, gate2_loaded, gates_loaded = sem("gate2_zeroed"), sem("gate2_loaded"), sem("gates_loaded")
        duo_done = sem("duo_done")
        duo_moved = [sem(f"duo_moved{b}") for b in range(2)]
        act_step, dve_step = sem("act_step"), sem("dve_step")
        squared, summed, scaled, hi_split, a_ready = (sem("squared"), sem("summed"), sem("scaled"),
                                                      sem("hi_split"), sem("a_ready"))
        z_logged, cum_ready, exps_ready = sem("z_logged"), sem("cum_ready"), sem("exps_ready")
        o_squared, o_summed, rinv_ready, gated = (sem("o_squared"), sem("o_summed"), sem("rinv_ready"),
                                                  sem("gated"))
        hid_ready = sem("hid_ready")
        conv_done, u_ready, sig_done, tanh_done, a_sq, factor, root, scanned, lruc_ready = (
            sem("conv_done"), sem("u_ready"), sem("sig_done"), sem("tanh_done"), sem("a_sq"), sem("factor"),
            sem("root"), sem("scanned"), sem("lruc_ready"))
        u_rounded = sem("u_rounded")
        y_rooted, final_g_loaded, stored = sem("y_rooted"), sem("final_g_loaded"), sem("stored")
        l_exp, l_w = sem("l_exp"), sem("l_w")

        def duo(q):
            return duo_psum[q % 2]

        def state_psum(q, s):
            if s < 4:
                return duo(par(q))[:, s % 2, (s // 2) * 256:(s // 2) * 256 + 256]
            return duo(par(q))[:, 2, 0:256] if s == 4 else vec_psum[:, 0:256]

        def half(i):
            if isinstance(i, tuple):
                base, per, reg = i
                assert per % 2 == 0
                return base // 2 + (per // 2) * reg
            return i // 2

        def whole(i):
            return i[0] + i[1] * i[2] if isinstance(i, tuple) else i

        def plus(i, k):
            return (i[0] + k, i[1], i[2]) if isinstance(i, tuple) else i + k

        def par(i):
            return (i[0] if isinstance(i, tuple) else i) % 2

        def wait_done(eng, q):
            eng.wait_ge(duo_done, whole(q) + 1)

        def wait_moved(eng, q):
            eng.wait_ge(duo_moved[par(q)], half(q) + 1)

        def moved(ins, q):
            ins.then_inc(duo_moved[par(q)], 1)

        def turn_column(s):
            return 256 + 16 * (not isinstance(s, tuple) and s == 10)

        A_READY = {key: KT * n for key, n in A_ORDER.items()}
        block = es.enter_context(nc.Block())

        @block.sync
        def _(sp):
            def raw_free(ch):
                if isinstance(ch, tuple) or ch >= 2:
                    sp.wait_ge(lo_ready, whole(ch) - 1)

            def load(ch, first, second):
                raw_free(ch)
                for dst, src in (first, second):
                    sp.dma_start(dst, src).then_inc(raw_loaded[par(ch)], 16)

            def columns(ch, w, col, rows=8):
                r = raw[par(ch)]
                v = w.rearrange("(k p) n -> p k n", p=P)
                m = rows // 2
                load(ch, (r[:, 0:m], v[:, 0:m, bass.ds(col, 256)]), (r[:, m:rows], v[:, m:rows, bass.ds(col, 256)]))

            def mod_pieces(u, layer, col, pieces=range(8)):
                v = w_mod[layer].rearrange("(k p) n -> p k n", p=P)
                for p in pieces:
                    sp.wait_ge(mod_used, whole(u) + p + 1)
                    sp.dma_start(mod_ring[p % 2][:], v[:, :, bass.ds(col + p * P, P)]).then_inc(mod_loaded[p % 2], 16)

            def mod_section(s, pieces=range(8)):
                mod_pieces(8 * (s - SEC_HEAD), s // 6, (s % 6) * D, pieces)

            def rows(dst, src):
                sp.dma_start(dst, src).then_inc(vec_loaded, 16)

            r0, r1 = vec_rows[:, 0], vec_rows[:, 1]
            rows(r0[V_BMOD:V_BMOD + 96], b_mod.rearrange("l (m p) -> (l m) p", p=P))
            rows(r0[V_NMIX:V_NMIX + 16], norm_mix_g.rearrange("l (m p) -> (l m) p", p=P))
            rows(r0[V_NFFN:V_NFFN + 16], norm_ffn_g.rearrange("l (m p) -> (l m) p", p=P))
            rows(r1[V_C:V_C + 8], c.rearrange("b (m p) -> (b m) p", p=P))
            rows(r1[V_C + 8:V_C + 16], c_ctx.rearrange("(m p) -> m p", p=P))
            rows(r1[V_GB:V_GB + 8], gla_gate_b.rearrange("j d (m p) -> (j d m) p", p=P))
            rows(r1[V_HN:V_HN + 2], gla_head_norm_g.rearrange("j (m p) -> (j m) p", p=P))
            rows(r1[V_CW:V_CW + 32], lru_conv_w.rearrange("j w (m p) -> (j w m) p", p=P))
            rows(r1[V_CB:V_CB + 8], lru_conv_b.rearrange("j (m p) -> (j m) p", p=P))
            rows(r1[V_BA:V_BA + 16], lru_gate_a_b.rearrange("j d (m p) -> (j d m) p", p=P))
            rows(r1[V_BX:V_BX + 16], lru_gate_x_b.rearrange("j d (m p) -> (j d m) p", p=P))
            rows(r1[V_LAM:V_LAM + 16], lru_lambda.rearrange("j d (m p) -> (j d m) p", p=P))
            sp.dma_start(x_rows[:, 0:4], x[0].rearrange("(t p) n -> p t n", p=P)).then_inc(x_loaded, 16)
            sp.dma_start(x_rows[:, 4:6], ctx_in[0].rearrange("(t p) n -> p t n", p=P)).then_inc(x_loaded, 16)
            sp.wait_ge(pads_made, 1)
            g1 = gla_gate_w1[0].rearrange("d (k p) r -> d p k r", p=P)
            load(C_GATE1, (raw[0][:, :, 0:RANK], g1[0]), (raw[0][:, :, 32:32 + RANK], g1[1]))
            for b, sec in enumerate(SEC_FIRST):
                for k in range(0, KT, 2):
                    sp.dma_start(mod_first[b][:, k:k + 2], w_mod[0].rearrange("(k p) n -> p k n", p=P)[
                        :, k:k + 2, sec * D:(sec + 1) * D]).then_inc(first_loaded[b][k // 2], 16)
            qk = gla_w_in[0, :, 0:2 * LAT].rearrange("(k p) (s n) -> p k s n", p=P, s=2)

            def head_loads(ch, h):
                r = raw[par(ch)]
                load(ch, (r[:, :, 0:P], qk[:, :, 0, bass.ds(h * P, P)]), (r[:, :, P:2 * P], qk[:, :, 1, bass.ds(h * P, P)]))
                columns(plus(ch, 1), gla_w_in[0], 2 * LAT + 256 * h)

            def gate2_load(h):
                for d in range(2):
                    sp.dma_start(gate2[32 * d:32 * d + RANK, d], gla_gate_w2[0, d, :, bass.ds(h * P, P)]
                                 ).then_inc(gate2_loaded, 16)

            head_loads(C_HEAD, 0)
            sp.wait_ge(gate2_zeroed, 1)
            gate2_load(0)
            with sp.Fori(0, HEADS - 1) as h:
                head_loads((C_HEAD + 2, 2, h), h + 1)
                sp.wait_ge(duo_done, Q_HEAD + 1 + PER_HEAD * h)
                gate2_load(h + 1)
                mod_pieces((0, 8, h), 0, 2 * D + D * h)

            def gate_columns(n):
                columns(C_G + n, gla_w_in[0], 2 * LAT + D + 256 * n)

            gate_columns(0)
            gate_columns(1)
            mod_section(5)
            mod_section(6, (0, 1))
            gate_columns(2)
            mod_section(6, (2, 3))
            gate_columns(3)
            mod_section(6, (4, 5))
            columns(C_OUT0, gla_w_out[0], 0)
            mod_section(6, (6, 7))
            for n in range(1, 4):
                columns(C_OUT0 + n, gla_w_out[0], 256 * n)

            def ffn_loads(layer, section):
                ch = C_FFN0 if layer == 0 else C_FFN1
                for part, (first, n) in enumerate(FFN_PARTS):
                    begin = 0
                    if part == 0:
                        columns(ch, ffn_w1[layer], first * P)
                        columns(ch + 1, ffn_w3[layer], first * P)
                        mod_section(section)
                        begin = 1
                    with sp.Fori(begin, n // 2) as i:
                        columns((ch, 2, i), ffn_w1[layer], first * P + 256 * i)
                        columns((ch + 1, 2, i), ffn_w3[layer], first * P + 256 * i)
                    ch += n
                    w2 = ffn_w2[layer, first * P:(first + n) * P]
                    with sp.Fori(0, 2) as i:
                        for b in range(2):
                            columns((ch + b, 2, i), w2, 512 * i + 256 * b, rows=n)
                    ch += 4

            ffn_loads(0, 7)
            ga = lru_gate_a_w[0].rearrange("d g (k p) j -> d g p k j", p=P)
            gx = lru_gate_x_w[0].rearrange("d g (k p) j -> d g p k j", p=P)
            for n in range(4):
                ch = C_LRU + 3 * n
                columns(ch, lru_w_in[0], D + 256 * n)
                columns(ch + 1, lru_w_in[0], 256 * n)
                if n == 0:
                    mod_section(8)
                mod_section(9, (2 * n, 2 * n + 1))
                raw_free(ch + 2)
                r = raw[par(ch + 2)]
                for d in range(2):
                    for m, w in enumerate((ga, gx)):
                        sp.dma_start(r[:, 4 * d + 2 * m:4 * d + 2 * m + 2], w[d, n]
                                     ).then_inc((raw_loaded[par(ch + 2)], gates_loaded)[m], 16)
            columns(C_OUT1, lru_w_out[0], 0)
            columns(C_OUT1 + 1, lru_w_out[0], 256)
            mod_section(10)
            for n in range(2, 4):
                columns(C_OUT1 + n, lru_w_out[0], 256 * n)
            ffn_loads(1, 11)
            sp.wait_ge(mod_used, 2 + 8 * 10)
            sp.dma_start(final_g[:], final_norm_g.partition_broadcast(P)).then_inc(final_g_loaded, 16)
            y_dram = out[0].rearrange("(t p) n -> t p n", p=P)
            for t in range(4):
                wait_moved(sp, Q_FINAL + t)
                sp.dma_start(y_dram[t], y_rows[t][:]).then_inc(stored, 16)
            sp.wait_ge(stored, 64)

        @block.gpsimd
        def _(pool):
            pool.memset(raw[0][:, :, 0:P], 0.0).then_inc(pads_made, 1)
            pool.memset(ident[:], 0.0)
            pool.memset(ones[:], 1.0)
            pool.memset(mask[:], 1.0)
            pool.memset(resets[:], 1.0)
            pool.memset(zero[:], 0.0)
            pool.memset(eps[:], EPS).then_inc(pads_made, 1)
            pool.wait_ge(pads_made, 2)
            pool.memset(resets[:, :, 0:1], 0.0)
            pool.affine_select(out=ident[:], in_=ident[:], compare_op=ALU.not_equal, fill=1.0, base=0,
                               pattern=[[-1, P]], channel_multiplier=1)
            pool.affine_select(out=mask[:, 0], in_=mask[:, 0], compare_op=ALU.is_ge, fill=0.0, base=0,
                               pattern=[[1, P]], channel_multiplier=-1)
            pool.affine_select(out=mask[:, 1], in_=mask[:, 1], compare_op=ALU.is_ge, fill=0.0, base=0,
                               pattern=[[-1, P]], channel_multiplier=1).then_inc(pads_made, 1)
            pool.wait_ge(pads_made, 3)
            pool.memset(mask[0:CHUNK, 0, CHUNK:P], 0.0)
            pool.memset(mask[CHUNK:P, 1, 0:CHUNK], 0.0).then_inc(consts_made, 1)

            def low(ch, cols=256):
                b = par(ch)
                pool.wait_ge(hi_ready, whole(ch) + 1)
                pool.tensor_tensor(w_lo[b][:, :, 0:cols], raw[b][:, :, 0:cols],
                                   w_hi[b][:, :, 0:cols].bitcast(F32), ALU.subtract).then_inc(lo_ready, 1)

            low(C_GATE1, P)
            with pool.Fori(0, (CHUNKS - 1) // 2) as i:
                for b in range(2):
                    low((1 + b, 2, i))

        @block.tensor
        def _(pe):
            def duo_wait(q):
                if isinstance(q, tuple) or q >= 2:
                    pe.wait_ge(duo_moved[par(q)], half(q))

            def chunk_wait(ch):
                pe.wait_ge(hi_ready, whole(ch) + 1)
                pe.wait_ge(lo_ready, whole(ch) + 1)

            def tile_out(ps, t, part, n):
                return ps[:, t, 0:n] if part == 0 else ps[:, 2, t * CTX:t * CTX + n]

            def tile_pair(ch, q, parts, act_hi, act_lo, rows=8, ready=None, pieces=None, cols=(0, 1), k0=0,
                          by_row=True):
                chunk_wait(ch)
                duo_wait(q)
                ps, hi, lo = duo(par(q)), w_hi[par(ch)], w_lo[par(ch)]
                by_row = by_row and ready is not None
                order = [(t, k) for k in range(rows) for t in cols] if by_row else [(t, k) for t in cols for k in range(rows)]
                for n_, (t, k) in enumerate(order):
                    if ready is not None and t == cols[0]:
                        ready(k)
                    if pieces is not None and n_ % rows == rows // 2:
                        pieces(n_ // rows)
                    first, last = k == 0, k == rows - 1
                    wh, wl = hi[:, k0 + k, t * P:(t + 1) * P], lo[:, k0 + k, t * P:(t + 1) * P]
                    for part, s, n in parts:
                        begin = first and not (by_row and part == 1 and t != cols[0])
                        pe.matmul(tile_out(ps, t, part, n), wh, act_hi[:, k, s:s + n], start=begin, stop=False,
                                  skip_group_check=True)
                    for part, s, n in parts:
                        pe.matmul(tile_out(ps, t, part, n), wh, act_lo[:, k, s:s + n], start=False, stop=False,
                                  skip_group_check=True)
                    for part, s, n in parts:
                        mm = pe.matmul(tile_out(ps, t, part, n), wl, act_hi[:, k, s:s + n], start=False, stop=last,
                                       skip_group_check=True)
                return mm

            def a_wait(key):
                return lambda k: pe.wait_ge(a_ready, A_READY[key] + k + 1)

            def mod_piece(s, p):
                u = plus(p, 8 * (s - SEC_HEAD)) if not isinstance(s, tuple) else (8 * (s[0] - SEC_HEAD) + p, 8, s[2])
                if p in (0, 4) or isinstance(p, tuple) and p[0] in (0, 4):
                    pe.wait_ge(mod_rowed, 2 * whole(s) + (p // 4 if not isinstance(p, tuple) else p[2]))
                    if p == 0 and isinstance(s, tuple):
                        pe.wait_ge(mod_ready, 2)
                pe.wait_ge(mod_loaded[par(p)], 16 * (half(u) + 1))
                at_ = P * (p % 4 if not isinstance(p, tuple) else p[0])
                for k in range(KT):
                    mm = pe.matmul(mod_psum[0:2, at_:at_ + P], cs[:, k], mod_ring[par(p)][:, k], start=k == 0,
                                   stop=k == KT - 1, skip_group_check=True)
                mm.then_inc(mod_used, 1)

            def turn(s, h):
                reg = isinstance(h, tuple)
                pe.wait_ge(mod_rowed, 2 * whole(s) + (h[2] if reg else h) + 1)
                c0 = turn_column(s) + 8 * (h[2] if reg else h)
                for p in range(4):
                    out_ = vec_psum[:, bass.ds(c0 + 2 * p, 2)]
                    mm = pe.matmul(out_, sec_rows[:, p * P:(p + 1) * P], ident[0:2, 0:2], start=True, stop=True,
                                   skip_group_check=True)
                mm.then_inc(mod_turned, 1)

            def rms_sum(q, parts, src, ready, n):
                pe.wait_ge(ready, n)
                duo_wait(q)
                for part, s, w in parts:
                    mm = pe.matmul(tile_out(duo(q), 0, part, w), ones[:], src[:, s:s + w], start=True, stop=True)
                mm.then_inc(duo_done, 1)

            pe.wait_ge(consts_made, 1)
            pe.wait_ge(vec_loaded, 16 * 12)
            pe.transpose(vec_psum[:, 0:P], vec_rows[:, 0], ident[:])
            pe.transpose(vec_psum[:, P:P + V_END], vec_rows[0:V_END, 1], ident[0:V_END, 0:V_END]).then_inc(vec_turned, 1)
            pe.wait_ge(x_loaded, 32)
            for i in range(4):
                q = Q_TURN + i
                duo_wait(q)
                for t in range(2):
                    f = 2 * i + t
                    for tau in range(TT):
                        dst = (duo(q)[:, t, tau * P:(tau + 1) * P] if tau < 4
                               else duo(q)[:, 2, t * CTX + (tau - 4) * P:t * CTX + (tau - 3) * P])
                        mm = pe.transpose(dst, x_rows[:, tau, f * P:(f + 1) * P], ident[:])
                mm.then_inc(duo_done, 1)
            pe.wait_ge(cs_ready, 1)
            for b in range(2):
                if b:
                    pe.wait_ge(mod_ready, b)
                for k in range(KT):
                    pe.wait_ge(first_loaded[b][k // 2], 16)
                    for n, ps in enumerate((mod_psum, vec_psum)):
                        mm = pe.matmul(ps[0:2, :], cs[:, k], mod_first[b][:, k, n * 512:(n + 1) * 512], start=k == 0,
                                       stop=k == KT - 1, skip_group_check=True)
                mm.then_inc(mod_used, 1)
                if b == 0:
                    rms_sum(Q_STAT[0][0], BOTH, sqsum, summed, SUMMED[0])
                pe.wait_ge(mod_rowed, 2 * b + 2)
                for p in range(8):
                    mm = pe.matmul(mod_psum[:, 2 * p:2 * p + 2], first_rows[:, p * P:(p + 1) * P], ident[0:2, 0:2],
                                   start=True, stop=True, skip_group_check=True)
                    if p % 4 == 3:
                        mm.then_inc(mod_turned, 1)

            tile_pair(C_GATE1, Q_T, BOTH, a_hi, a_lo, ready=a_wait(("prep", 0, 0)), cols=(0,)).then_inc(duo_done, 1)
            wait_moved(pe, Q_T)
            with pe.Fori(0, HEADS) as h:
                q0 = (Q_HEAD, PER_HEAD, h)
                pe.wait_ge(gate2_loaded, 32 * h + 32)
                duo_wait(q0)
                for d in range(2):
                    for part, s, n in BOTH:
                        mm = pe.matmul(tile_out(duo(par(q0)), d, part, n), gate2[:, d], t_low[:, s:s + n], start=True, stop=True,
                                       skip_group_check=True)
                mm.then_inc(duo_done, 1)
                ch = (C_HEAD, 2, h)
                tile_pair(ch, plus(q0, 1), BOTH, a_hi, a_lo).then_inc(duo_done, 1)
                chv, qv = plus(ch, 1), plus(q0, 2)
                chunk_wait(chv)
                duo_wait(qv)
                hi, lo = w_hi[par(chv)], w_lo[par(chv)]
                for tau in range(TT):
                    dst = duo(par(qv))[:, tau // 2, (tau % 2) * 256:(tau % 2) * 256 + 256]
                    for k in range(KT):
                        ah, al = a_hi[:, k, tau * P:(tau + 1) * P], a_lo[:, k, tau * P:(tau + 1) * P]
                        pe.matmul(dst, ah, hi[:, k], start=k == 0, stop=False, skip_group_check=True)
                        pe.matmul(dst, ah, lo[:, k], start=False, stop=False, skip_group_check=True)
                        mm = pe.matmul(dst, al, hi[:, k], start=False, stop=k == KT - 1, skip_group_check=True)
                mm.then_inc(duo_done, 1)
                sec = (SEC_HEAD, 1, h)
                mod_piece(sec, 0)
                wait_moved(pe, plus(q0, 1))
                qt = plus(q0, 3)
                duo_wait(qt)
                for j in range(12):
                    d, tau = j // 6, j % 6
                    mm = pe.transpose(duo(par(qt))[:, j // 4, (j % 4) * P:(j % 4 + 1) * P],
                                      k_end[:, d, tau * P:(tau + 1) * P], ident[:])
                mm.then_inc(duo_done, 1)
                mod_piece(sec, 1)
                qa = plus(q0, 4)
                duo_wait(qa)
                for j in range(12):
                    d, tau = j // 6, j % 6
                    mm = pe.matmul(duo(par(qa))[:, j // 4, (j % 4) * P:(j % 4 + 1) * P],
                                   k_inv[:, d, tau * P:(tau + 1) * P], q_dec[:, d, tau * P:(tau + 1) * P],
                                   start=True, stop=True, skip_group_check=True)
                mm.then_inc(duo_done, 1)
                mod_piece(sec, 2)
                mod_piece(sec, 3)
                pe.wait_ge(mod_ready, whole(sec))
                wait_moved(pe, qt)
                wait_moved(pe, qv)
                for g, (d, chunks) in enumerate(STATE_GROUPS):
                    qu = plus(q0, 5 + g)
                    duo_wait(qu)
                    for s, n in enumerate(chunks):
                        r = CHUNK * (n % 2)
                        mm = pe.matmul(state_psum(qu, s),
                                       k_tok[r:r + CHUNK, d * 6 + n // 2], v_tok[r:r + CHUNK, n // 2],
                                       start=True, stop=True, skip_group_check=True)
                    mm.then_inc(duo_done, 1)
                    if g == 1:
                        wait_moved(pe, plus(q0, 5))
                        turn(sec, 0)
                    if g >= 1:
                        mod_piece(sec, 3 + g)
                mod_piece(sec, 7)
                for g in range(4):
                    wait_moved(pe, plus(q0, 5 + g)) if g >= 2 else None
                wait_moved(pe, qa)
                qo = plus(q0, 9)
                duo_wait(qo)
                for tau in range(TT):
                    for v in range(2):
                        c0 = (tau % 2) * 256 + v * P
                        dst = duo(par(qo))[:, tau // 2, c0:c0 + P]
                        pe.matmul(dst, v_tok[:, tau, v * P:(v + 1) * P], att[:, tau], start=True, stop=False,
                                  skip_group_check=True)
                        mm = pe.matmul(dst, v_tok[:, tau, v * P:(v + 1) * P], att[:, 6 + tau], start=False,
                                       stop=False, skip_group_check=True)
                        for n in (2 * tau, 2 * tau + 1):
                            for d in range(2):
                                s = STATE_BEFORE[d][n]
                                if s is not None:
                                    mm = pe.matmul(duo(par(qo))[:, tau // 2, c0 + CHUNK * (n % 2):c0 + CHUNK * (n % 2) + CHUNK],
                                                   states[:, s, v * P:(v + 1) * P],
                                                   q_dec[:, d, n * CHUNK:(n + 1) * CHUNK], start=False,
                                                   stop=n % 2 == 1 and d == 1, skip_group_check=True)
                mm.then_inc(duo_done, 1)
                turn(sec, 1)

            for h in range(HEADS):
                rms_sum(Q_NORM + h, BOTH, o_sum[h % 2], o_summed, h + 1)
            with pe.Fori(0, 2) as i:
                for b in range(2):
                    tile_pair((C_G + b, 2, i), (Q_G + b, 2, i), BOTH, a_hi, a_lo,
                              pieces=lambda p: mod_piece(6, (2 * b + p, 4, i))).then_inc(duo_done, 1)
                turn(6, (0, 1, i))

            def project_out(layer, parts):
                c0, q0 = (C_OUT0, Q_OUT0) if layer == 0 else (C_OUT1, Q_OUT1)
                if layer == 1:
                    for h in range(2):
                        mod_pair(10, h)
                        turn(10, h)
                with pe.Fori(0, 2) as i:
                    for b in range(2):
                        tile_pair((c0 + b, 2, i), (q0 + b, 2, i), parts, a_hi, a_lo,
                                  ready=a_wait(("out", layer)) if b == 0 else None).then_inc(duo_done, 1)

            def ffn(layer, parts):
                ch, q = (C_FFN0, Q_FFN0) if layer == 0 else (C_FFN1, Q_FFN1)
                mod_pair(7 if layer == 0 else 11, 0)
                rms_sum(Q_STAT[layer][1], parts, sqsum, summed, SUMMED[2 * layer + 1])
                turn(7 if layer == 0 else 11, 0)
                mod_pair(7 if layer == 0 else 11, 1)
                turn(7 if layer == 0 else 11, 1)
                hb = 0 if layer == 0 else FT // 2
                for part, (first, n) in enumerate(FFN_PARTS):
                    with pe.Fori(0, n // 2) as i:
                        tile_pair((ch, 2, i), (q, 2, i), parts, a_hi, a_lo,
                                  ready=a_wait(("prep", layer, 1)) if part == 0 else None).then_inc(duo_done, 1)
                        tile_pair((ch + 1, 2, i), (q + 1, 2, i), parts, a_hi, a_lo).then_inc(duo_done, 1)
                    ch, q, hb = ch + n, q + n, hb + n // 2
                    with pe.Fori(0, 2) as i:
                        for b in range(2):
                            rd = (lambda k: pe.wait_ge(hid_ready, hb - n // 2 + k // 2 + 1) if k % 2 == 0 else None)
                            tile_pair((ch + b, 2, i), (q + b, 2, i), parts, h_hi, h_lo, rows=n,
                                      ready=rd if b == 0 else None, by_row=False).then_inc(duo_done, 1)
                    ch, q = ch + 4, q + 4

            def mod_pair(s, half_):
                for p in range(4 * half_, 4 * half_ + 4):
                    mod_piece(s, p)

            project_out(0, BOTH)
            ffn(0, BOTH)
            mod_pair(8, 0)
            rms_sum(Q_STAT[1][0], BOTH, sqsum, summed, SUMMED[2])
            turn(8, 0)
            mod_pair(8, 1)
            turn(8, 1)
            with pe.Fori(0, 2) as i:
                for b in range(2):
                    q0, ch = (Q_LRU + 6 * b, 12, i), (C_LRU + 3 * b, 6, i)
                    tile_pair(ch, q0, BOTH, a_hi, a_lo, ready=a_wait(("prep", 1, 0)) if b == 0 else None
                              ).then_inc(duo_done, 1)
                    tile_pair(plus(ch, 1), plus(q0, 1), ONLY_LAT, a_hi, a_lo,
                              pieces=lambda p: mod_piece(9, (2 * b + p, 4, i))).then_inc(duo_done, 1)
                    pe.wait_ge(u_ready, 2 * i + b + 1)
                    for gi in range(4):
                        tile_pair(plus(ch, 2), plus(q0, 2 + gi), BOTH, u_hi, u_lo, rows=2, k0=2 * gi
                                  ).then_inc(duo_done, 1)
                turn(9, (0, 1, i))
            project_out(1, ONLY_LAT)
            ffn(1, ONLY_LAT)
            wait_moved(pe, Q_FINAL - 2)
            wait_moved(pe, Q_FINAL - 1)
            for t in range(4):
                q = Q_FINAL + t
                duo_wait(q)
                for f in range(KT):
                    mm = pe.transpose(duo(q)[:, f // 4, (f % 4) * P:(f % 4 + 1) * P], xres[:, f, t * P:(t + 1) * P],
                                      ident[:])
                mm.then_inc(duo_done, 1)

        @block.scalar
        def _(act):
            steps = Steps(act, act_step)

            def high(ch, q_before, cols=256):
                if not isinstance(ch, tuple) and ch >= CHUNKS:
                    return
                b = par(ch)
                act.wait_ge(raw_loaded[b], 32 * (half(ch) + 1))
                if q_before is not None:
                    wait_done(act, q_before)
                act.activation(w_hi[b][:, :, 0:cols], raw[b][:, :, 0:cols], ACT.Copy).then_inc(hi_ready, 1)

            def part_psum(q, part):
                ps = duo(par(q))
                return ps[:, 0:2, :] if part == 0 else ps[:, 2, :].rearrange("p (t n) -> p t n", t=2)

            def tile_psum(q, t, part):
                ps = duo(par(q))
                return ps[:, t, :] if part == 0 else ps[:, 2, t * CTX:(t + 1) * CTX]

            def square(pair, n, width):
                if not isinstance(pair, tuple) and pair >= 2 or isinstance(pair, tuple) and pair[0] >= 2:
                    act.wait_ge(summed, whole(pair) - 1)
                act.activation(sq[par(pair)][:, :, 0:width], xres[:, bass.ds(2 * whole(n), 2), 0:width], ACT.Square
                               ).then_inc(squared, 1)

            def prep(layer, which, parts):
                n = 2 * layer + which
                q = Q_STAT[layer][which]
                wait_done(act, q)
                for part, s, w in parts:
                    ins = act.activation(rinv[:, s:s + w], tile_psum(q, 0, part), ACT.Sqrt, bias=eps[:, 0:1],
                                         scale=1.0 / D)
                    if part == parts[-1][0]:
                        moved(ins, q)
                sec = 6 * layer + 3 * which
                if n == 0:
                    act.wait_ge(mod_ready, 2)
                for m in range(KT):
                    act.wait_ge(scaled, 8 * n + m + 1)
                    for part, s, w in parts:
                        dst, src = a_hi[:, m, s:s + w], normed[m % 2][:, s:s + w]
                        if part == 0 and (layer, which) == (1, 0):
                            dst = dst.rearrange("p (c r) -> p r c", r=ROWS)
                            src = src.rearrange("p (r c) -> p r c", r=ROWS)
                        ins = act.activation(dst, src, ACT.Identity, bias=mod[:, sec, m, part:part + 1])
                    ins.then_inc(hi_split, 1)
                    if n > 0 and m == 0:
                        row_copy([0, 7, 8, 11][n], 1)

            def row_copy(s, h):
                h = h[2] if isinstance(h, tuple) else h
                act.wait_ge(mod_used, 8 * whole(s) + 4 * h - 10)
                act.wait_ge(mod_turned, 2 * whole(s) + h)
                act.activation(sec_rows[:], mod_psum[0:2, :], ACT.Copy).then_inc(mod_rowed, 1)

            act.wait_ge(vec_ready, 1)
            act.activation(cs[:].rearrange("p k v -> p v k"), vec[:, 1, V_C:V_C + 16].rearrange("p (v k) -> p v k", v=2),
                           ACT.Silu).then_inc(cs_ready, 1)
            for i in (1, 3):
                q = Q_TURN + i
                wait_done(act, q)
                steps.mark(act.activation(xres[:, 2 * i:2 * i + 2, 0:LAT], part_psum(q, 0), ACT.Copy))
                moved(act.activation(xres[:, 2 * i:2 * i + 2, LAT:TOK], part_psum(q, 1), ACT.Copy), q)
            for i in range(4):
                wait_moved(act, Q_TURN + i)
            for n in range(4):
                square(n, n, TOK)
            high(0, None, P)
            for b in range(2):
                act.wait_ge(mod_used, b + 1)
                if b:
                    act.wait_ge(mod_turned, 2 * b)
                for n, ps in enumerate((mod_psum, vec_psum)):
                    act.activation(first_rows[:, n * 512:(n + 1) * 512], ps[0:2, :], ACT.Copy).then_inc(mod_rowed, 1)
            prep(0, 0, BOTH)
            high(1, None)

            act.preload_act_table_set("natural_log_exp_and_others")
            act.wait_ge(l_w, 1)
            act.activation(lw[:, 0], lw[:, 3], ACT.Exp, scale=-1.0).then_inc(l_exp, 1)
            wait_done(act, Q_T)
            steps.mark(act.activation(t_low[:, 0:LAT], duo(Q_T)[0:64, 0, :], ACT.Copy))
            moved(act.activation(t_low[:, LAT:TOK], duo(Q_T)[0:64, 2, 0:CTX], ACT.Copy), Q_T)
            high(2, Q_T)
            with steps.loop(HEADS, 10) as h:
                q0 = (Q_HEAD, PER_HEAD, h)
                wait_done(act, q0)
                for d in range(2):
                    for part, s, n in BOTH:
                        ins = act.activation(zg[:, d, s:s + n], tile_psum(q0, d, part), ACT.Identity,
                                             bias=vec[:, 1, bass.ds(V_GB + 4 * d + h, 1)])
                        if d == 1 and part == 1:
                            moved(ins, q0)
                        else:
                            steps.mark(ins)
                wait_moved(act, q0)
                steps.link(act.activation(bcum[:], zg[:], ACT.Abs))
                steps.link(act.activation(bcum[:], bcum[:], ACT.Exp, scale=-1.0))
                act.activation(bcum[:], bcum[:], ACT.Ln, bias=1.0).then_inc(z_logged, 1)
                act.wait_ge(cum_ready, h + 1)
                steps.mark(act.activation(q_dec[:], bcum[:], ACT.Exp, scale=1.0 / TAU))
                steps.mark(act.activation(k_inv[:], bcum[:], ACT.Exp, scale=-1.0 / TAU))
                steps.mark(act.activation(k_end[:], zg[:], ACT.Exp, scale=1.0 / TAU))
                steps.mark(act.activation(decay[:, 0], bcum[:, 0, CHUNK - 1::CHUNK], ACT.Exp, scale=1.0 / TAU))
                act.activation(decay[:, 1], bcum[:, 1, 0::CHUNK], ACT.Exp, scale=1.0 / TAU).then_inc(exps_ready, 1)
                ch = (C_HEAD, 2, h)
                act.wait_ge(exps_ready, h + 1)
                wait_done(act, plus(q0, 2))
                moved(act.activation(v_tok[:].rearrange("p t n -> p (t n)"),
                                     duo(par(q0))[:].rearrange("p b n -> p (b n)"), ACT.Copy), plus(q0, 2))
                wait_done(act, plus(q0, 3))
                moved(act.activation(k_tok[:].rearrange("p t n -> p (t n)"),
                                     duo(par(plus(q0, 3)))[:].rearrange("p b n -> p (b n)"), ACT.Copy), plus(q0, 3))
                high(plus(ch, 2), plus(q0, 1))
                high(plus(ch, 3), plus(q0, 2))
                row_copy((SEC_HEAD, 1, h), 0)
                row_copy((SEC_HEAD, 1, h), 1)
                qo = plus(q0, 9)
                wait_done(act, qo)
                src = duo(par(qo))[:].rearrange("p b (t v n) -> p v (b t) n", t=2, v=2)
                steps.mark(act.activation(o_all[:, bass.ds(2 * h, 1)].rearrange("p o (t n) -> p (o t) n", n=P), src[:, 0],
                                          ACT.Copy))
                moved(act.activation(o_all[:, bass.ds(2 * h + 1, 1)].rearrange("p o (t n) -> p (o t) n", n=P), src[:, 1],
                                     ACT.Copy), qo)
            wait_moved(act, Q_HEAD + HEADS * PER_HEAD - 1)
            for h in range(HEADS):
                if h >= 2:
                    act.wait_ge(o_summed, h - 1)
                act.activation(o_sq[h % 2][:], o_all[:, 2 * h:2 * h + 2], ACT.Square).then_inc(o_squared, 1)
            for h in range(HEADS):
                wait_done(act, Q_NORM + h)
                for part, s, n in BOTH:
                    ins = act.activation(o_rinv[:, h, s:s + n], tile_psum(Q_NORM + h, 0, part), ACT.Sqrt,
                                         bias=eps[:, 0:1], scale=1.0 / 256)
                    if part:
                        moved(ins, Q_NORM + h)
            for h in range(HEADS):
                q = Q_G + h
                if h % 2:
                    row_copy(6, h // 2)
                wait_done(act, q)
                if h >= 2:
                    act.wait_ge(gated, h - 1)
                act.activation(silu_g[h % 2][:, :, 0:LAT], part_psum(q, 0), ACT.Silu)
                moved(act.activation(silu_g[h % 2][:, :, LAT:TOK], part_psum(q, 1), ACT.Silu), q)
                high(C_G + h + 2, q)

            def split_out(layer, parts):
                src = o_all if layer == 0 else lru_o
                width = parts[-1][1] + parts[-1][2]
                last = Q_OUT0 - 1 if layer == 0 else Q_OUT1 - 1
                wait_done(act, last)
                for m in range(KT):
                    if m % 2 == 0:
                        act.wait_ge(gated if layer == 0 else scanned, m // 2 + 1 + layer)
                    act.activation(a_hi[:, m, 0:width], src[:, m, 0:width], ACT.Copy).then_inc(hi_split, 1)
                c0, q0 = (C_OUT0, Q_OUT0) if layer == 0 else (C_OUT1, Q_OUT1)
                residual_loop(c0, q0, PAIRS[2 * layer + 1], width)

            def residual_loop(c0, q0, pair, width, last=False):
                with act.Fori(0, 2) as i:
                    for b in range(2):
                        if not last:
                            high((c0 + 2 + b, 2, i), (q0 + b, 2, i))
                        wait_moved(act, (q0 + b, 2, i))
                        if pair is not None:
                            square((pair + b, 2, i), (b, 2, i), width)

            def ffn(layer, parts):
                ch, q = (C_FFN0, Q_FFN0) if layer == 0 else (C_FFN1, Q_FFN1)
                for part, (first, n) in enumerate(FFN_PARTS):
                    with act.Fori(0, n // 2) as i:
                        wait_done(act, (q, 2, i))
                        act.wait_ge(duo_moved[(q + 1) % 2], half((q + 1, 2, i)))
                        for k, s, w in parts:
                            ins = act.activation(gate[:, :, s:s + w], part_psum(q, k), ACT.Silu)
                            if k == parts[-1][0]:
                                moved(ins, q)
                        high((ch + 2, 2, i), (q, 2, i))
                        high((ch + 3, 2, i), (q + 1, 2, i))
                    ch, q = ch + n, q + n
                    last = layer == 1 and part == len(FFN_PARTS) - 1
                    if last:
                        for b in range(2):
                            high(ch + 2 + b, q + b)
                    elif part == len(FFN_PARTS) - 1:
                        residual_loop(ch, q, PAIRS[2], TOK)
                    else:
                        with act.Fori(0, 2) as i:
                            for b in range(2):
                                high((ch + 2 + b, 2, i), (q + b, 2, i))
                    ch, q = ch + 4, q + 4

            split_out(0, BOTH)
            row_copy(7, 0)
            prep(0, 1, BOTH)
            ffn(0, BOTH)
            row_copy(8, 0)
            prep(1, 0, BOTH)
            with steps.loop(2, 44) as i:
                for b in range(2):
                    q0, ch, n = (Q_LRU + 6 * b, 12, i), (C_LRU + 3 * b, 6, i), 2 * i + b
                    wait_done(act, q0)
                    steps.mark(act.activation(u_pad[:, :, 2:2 + LAT], part_psum(q0, 0), ACT.Copy))
                    moved(act.activation(u_pad[:, :, 2 + LAT + GAP:2 + UW], part_psum(q0, 1), ACT.Copy), q0)
                    act.wait_ge(gates_loaded, 32 * n + 32)
                    high(plus(ch, 2), q0)
                    act.wait_ge(conv_done, n + 1)
                    act.wait_ge(scanned, n + 1)
                    steps.mark(act.activation(u_hi[:, :, 0:LAT], u_conv[:, :, 0:LAT], ACT.Copy))
                    act.activation(u_hi[:, :, LAT:TOK], u_conv[:, :, LAT + GAP:UW], ACT.Copy).then_inc(u_rounded, 1)
                    wait_done(act, plus(q0, 1))
                    moved(act.activation(lru_y[:], part_psum(plus(q0, 1), 0), ACT.Gelu_apprx_tanh), plus(q0, 1))
                    high(plus(ch, 3), plus(q0, 1))
                    if b:
                        row_copy(9, (0, 1, i))
                    act.wait_ge(lruc_ready, 1)
                    for d in range(2):
                        for g in range(2):
                            q = plus(q0, 2 + 2 * d + g)
                            col = (V_BX if g else V_BA) + 8 * d
                            wait_done(act, q)
                            for t in range(2):
                                for part, s, w in BOTH:
                                    ins = act.activation(gates_r[:, 2 * d + g, t, s:s + w], tile_psum(q, t, part),
                                                         ACT.Sigmoid, bias=vec[:, 1, bass.ds(col + 2 * n + t, 1)])
                                    if t == 1 and part == 1:
                                        moved(ins, q)
                                    else:
                                        steps.mark(ins)
                            if g == 1:
                                wait_moved(act, plus(q0, 2 + 2 * d))
                                if d == 0:
                                    wait_done(act, plus(q0, 5))
                                for t in range(2):
                                    steps.mark(act.activation(scan_h[d][:, t], gates_r[:, 2 * d, t], ACT.Tanh,
                                                              scale=lru_c[:, 0, bass.ds(8 * d + 2 * n + t, 1)]))
                    steps.wait()
                    for d in range(2):
                        for t in range(2):
                            steps.mark(act.activation(gates_r[:, 2 * d, t], gates_r[:, 2 * d, t], ACT.Exp,
                                                      scale=lru_c[:, 1, bass.ds(8 * d + 2 * n + t, 1)]))
                    steps.wait()
                    for d in range(2):
                        act.wait_ge(factor, 3 * n + 1 + d)
                        act.activation(u_conv[:, :, 0:TOK], gates_r[:, 2 * d], ACT.Square).then_inc(a_sq, 1)
                    for d in range(2):
                        act.wait_ge(factor, 3 * n + 2 + d)
                        act.activation(scan_h[d][:], scan_h[d][:], ACT.Sqrt).then_inc(root, 1)
                    high(plus(ch, 4), plus(q0, 5))
            for half_ in range(2):
                row_copy(10, half_)
            split_out(1, ONLY_LAT)
            row_copy(11, 0)
            prep(1, 1, ONLY_LAT)
            ffn(1, ONLY_LAT)
            for t in range(4):
                q = Q_FINAL + t
                wait_done(act, q)
                steps.link(act.activation(y_junk[:], duo(q)[:, 0:2, :].rearrange("p b n -> p (b n)"), ACT.Square,
                                          accum_out=ysum[:, 0, t:t + 1]))
                act.activation(ysum[:, 1, t:t + 1], ysum[:, 0, t:t + 1], ACT.Sqrt, bias=eps[:, 0:1], scale=1.0 / D
                               ).then_inc(y_rooted, 1)

        @block.vector
        def _(dve):
            steps = Steps(dve, dve_step)

            def part_psum(q, part):
                ps = duo(par(q))
                return ps[:, 0:2, :] if part == 0 else ps[:, 2, :].rearrange("p (t n) -> p t n", t=2)

            def tile_psum(q, t, part):
                ps = duo(par(q))
                return ps[:, t, :] if part == 0 else ps[:, 2, t * CTX:(t + 1) * CTX]

            def section(s, row):
                dve.wait_ge(mod_turned, 2 * whole(s) + 2 if s != 9 else 22)
                r = whole(row)
                ps, c0 = (mod_psum, 0) if s in (0, 1) else (vec_psum, turn_column(s))
                dve.tensor_tensor(mod[:, bass.ds(r, 1)].rearrange("p o m v -> p (o m) v"),
                                  ps[:, c0:c0 + 16].rearrange("p (m v) -> p m v", v=2),
                                  vec[:, 0, bass.ds(V_BMOD + 8 * r, 8)].unsqueeze(2).broadcast_to([P, 8, 2]),
                                  ALU.add).then_inc(mod_ready, 1)

            def add_squares(pair, n, width):
                dve.wait_ge(squared, whole(pair) + 1)
                for t in range(2):
                    ins = dve.tensor_tensor(sqsum[:, 0:width], sqsum[:, 0:width], sq[par(pair)][:, t, 0:width], ALU.add)
                    if t == 0:
                        steps.link(ins)
                ins.then_inc(summed, 1)
                dve.wait_ge(summed, whole(pair) + 1)

            def clear_sum():
                steps.link(dve.memset(sqsum[:], 0.0))

            def prep(layer, which, parts):
                n = 2 * layer + which
                width = parts[-1][1] + parts[-1][2]
                g = vec[:, 0, (V_NMIX if which == 0 else V_NFFN) + 8 * layer:][:, 0:8]
                sec = 6 * layer + 3 * which
                dve.wait_ge(mod_ready, [1, 6, 8, 11][n])
                steps.link(dve.scalar_tensor_tensor(out=gain[:, n], in0=mod[:, sec + 1], scalar=1.0,
                                                    in1=g.unsqueeze(2).broadcast_to([P, 8, 2]), op0=ALU.add,
                                                    op1=ALU.mult))
                if n == 0:
                    section(1, SEC_FIRST[1])
                wait_moved(dve, Q_STAT[layer][which])
                steps.link(dve.reciprocal(rinv[:, 0:width], rinv[:, 0:width]))
                if n == 0:
                    dve.wait_ge(mod_ready, 2)

                def scale(m):
                    if m >= 2:
                        dve.wait_ge(hi_split, HI_SPLIT[n] + m - 1)
                    for part, s, w in parts:
                        ins = dve.scalar_tensor_tensor(out=normed[m % 2][:, s:s + w], in0=xres[:, m, s:s + w],
                                                       scalar=gain[:, n, m, part:part + 1], in1=rinv[:, s:s + w],
                                                       op0=ALU.mult, op1=ALU.mult)
                    ins.then_inc(scaled, 1)

                scale(0)
                for m in range(KT):
                    if m + 1 < KT:
                        if m >= 1:
                            dve.wait_ge(a_ready, 8 * A_ORDER[("prep", layer, which)] + m)
                        scale(m + 1)
                    dve.wait_ge(hi_split, HI_SPLIT[n] + m + 1)
                    for part, s, w in parts:
                        dst, hi, src = a_lo[:, m, s:s + w], a_hi[:, m, s:s + w], normed[m % 2][:, s:s + w]
                        if part == 0 and (layer, which) == (1, 0):
                            dst = dst.rearrange("p (c r) -> p r c", r=ROWS)
                            hi = hi.rearrange("p (c r) -> p r c", r=ROWS)
                            src = src.rearrange("p (r c) -> p r c", r=ROWS)
                        ins = dve.scalar_tensor_tensor(out=dst, in0=src, scalar=mod[:, sec, m, part:part + 1],
                                                       in1=hi.bitcast(F32), op0=ALU.add, op1=ALU.subtract)
                    ins.then_inc(a_ready, 1)

            dve.wait_ge(vec_turned, 1)
            steps.mark(dve.tensor_copy(vec[:, 0], vec_psum[:, 0:P]))
            dve.tensor_copy(vec[:, 1, 0:V_END], vec_psum[:, P:P + V_END]).then_inc(vec_ready, 1)
            dve.wait_ge(vec_ready, 1)
            steps.wait()
            lam = vec[:, 1, V_LAM:V_LAM + 16]
            steps.link(dve.tensor_scalar(lw[:, 1], lam, -1.0, 0.0, ALU.mult, ALU.max))
            steps.link(dve.tensor_scalar(lw[:, 2], lam, 0.0, None, ALU.max))
            dve.tensor_tensor(lw[:, 3], lw[:, 1], lw[:, 2], ALU.add).then_inc(l_w, 1)
            for i in (0, 2):
                q = Q_TURN + i
                wait_done(dve, q)
                steps.mark(dve.tensor_copy(xres[:, 2 * i:2 * i + 2, 0:LAT], part_psum(q, 0)))
                moved(dve.tensor_copy(xres[:, 2 * i:2 * i + 2, LAT:TOK], part_psum(q, 1)), q)
            clear_sum()
            for n in range(4):
                add_squares(n, n, TOK)
            section(0, SEC_FIRST[0])
            dve.memset(gate2[:], 0.0).then_inc(gate2_zeroed, 1)
            dve.wait_ge(mod_ready, 1)
            prep(0, 0, BOTH)

            dve.wait_ge(l_exp, 1)
            steps.link(dve.tensor_scalar(lw[:, 2], lw[:, 0], 2.0, None, ALU.add))
            steps.link(dve.reciprocal(lw[:, 2], lw[:, 2]))
            steps.link(dve.tensor_tensor(lw[:, 0], lw[:, 0], lw[:, 2], ALU.mult))
            steps.link(dve.tensor_tensor(lw[:, 2], lw[:, 0], lw[:, 0], ALU.mult))
            steps.link(dve.tensor_scalar(lw[:, 3], lw[:, 2], 1.0 / 15, 1.0 / 13, ALU.mult, ALU.add))
            for odd in (11, 9, 7, 5, 3, 1):
                steps.link(dve.tensor_tensor(lw[:, 3], lw[:, 3], lw[:, 2], ALU.mult))
                steps.link(dve.tensor_scalar(lw[:, 3], lw[:, 3], 1.0 / odd, None, ALU.add))
            steps.link(dve.tensor_tensor(lw[:, 3], lw[:, 3], lw[:, 0], ALU.mult))
            steps.link(dve.scalar_tensor_tensor(out=lw[:, 0], in0=lw[:, 3], scalar=2.0, in1=lw[:, 1], op0=ALU.mult,
                                                op1=ALU.add))
            steps.mark(dve.tensor_scalar(lru_c[:, 0], lw[:, 0], LRU_C, None, ALU.mult))
            dve.tensor_scalar(lru_c[:, 1], lw[:, 0], -LRU_C, None, ALU.mult).then_inc(lruc_ready, 1)
            dve.wait_ge(consts_made, 1)
            reset_row = resets[:].rearrange("p n c -> p (n c)")
            with steps.loop(HEADS, 30) as h:
                q0 = (Q_HEAD, PER_HEAD, h)
                dve.wait_ge(z_logged, h + 1)
                steps.link(dve.scalar_tensor_tensor(out=zg[:], in0=zg[:], scalar=0.0, in1=bcum[:], op0=ALU.min,
                                                    op1=ALU.subtract))
                steps.mark(dve.tensor_tensor_scan(bcum[:, 0], reset_row, zg[:, 0], 0.0, ALU.mult, ALU.add))
                steps.link(dve.tensor_tensor_scan(bcum[:, 1, ::-1], reset_row, zg[:, 1, ::-1], 0.0, ALU.mult, ALU.add))
                for d, last in ((0, CHUNK - 1), (1, 0)):
                    b4 = bcum[:, d].rearrange("p (n c) -> p n c", c=CHUNK)
                    ins = dve.tensor_tensor(zg[:, d].rearrange("p (n c) -> p n c", c=CHUNK),
                                            b4[:, :, last:last + 1].broadcast_to([P, NCH, CHUNK]), b4, ALU.subtract)
                    if d == 0:
                        steps.mark(ins)
                ins.then_inc(cum_ready, 1)
                dve.wait_ge(exps_ready, h + 1)
                q1 = plus(q0, 1)
                wait_done(dve, q1)
                for part, s, n in BOTH:
                    qp = tile_psum(q1, 0, part).unsqueeze(1).broadcast_to([P, 2, n])
                    steps.mark(dve.scalar_tensor_tensor(out=q_dec[:, :, s:s + n], in0=qp, scalar=DK_SCALE,
                                                        in1=q_dec[:, :, s:s + n], op0=ALU.mult, op1=ALU.mult))
                for n_, buf in enumerate((k_inv, k_end)):
                    for part, s, n in BOTH:
                        kp = tile_psum(q1, 1, part).unsqueeze(1).broadcast_to([P, 2, n])
                        ins = dve.tensor_tensor(buf[:, :, s:s + n], kp, buf[:, :, s:s + n], ALU.mult)
                        if n_ == 1 and part == 1:
                            moved(ins, q1)
                        else:
                            steps.mark(ins)
                qa = plus(q0, 4)
                wait_done(dve, qa)
                steps.link(dve.memset(att[:], 0.0))
                steps.mark(dve.memset(zero[:], 0.0))
                for d in range(2):
                    flat = duo(par(qa))[:].rearrange("p b n -> p (b n)")[:, d * TOK:(d + 1) * TOK]
                    ins = dve.copy_predicated(att[:, 6 * d:6 * d + 6], mask[:, d].bitcast(I32).unsqueeze(1).broadcast_to([P, 6, P]),
                                              flat.rearrange("p (t n) -> p t n", n=P))
                    if d == 0:
                        steps.mark(ins)
                moved(ins, qa)
                for g, (d, chunks) in enumerate(STATE_GROUPS):
                    qu = plus(q0, 5 + g)
                    wait_done(dve, qu)
                    for s, n in enumerate(chunks):
                        u = state_psum(qu, s)
                        new = STATE_AFTER[d][n]
                        if STATE_BEFORE[d][n] is None:
                            ins = dve.tensor_copy(states[:, new], u)
                        else:
                            ins = dve.scalar_tensor_tensor(out=states[:, new], in0=states[:, STATE_BEFORE[d][n]],
                                                           scalar=decay[:, d, n:n + 1], in1=u, op0=ALU.mult,
                                                           op1=ALU.add)
                        if s == len(chunks) - 1:
                            moved(ins, qu)
                            wait_moved(dve, qu)
                        else:
                            steps.link(ins)
                section((SEC_HEAD, 1, h), (2, 1, h))
            for h in range(HEADS):
                dve.wait_ge(o_squared, h + 1)
                dve.tensor_tensor(o_sum[h % 2][:], o_sq[h % 2][:, 0], o_sq[h % 2][:, 1], ALU.add).then_inc(o_summed, 1)
                if h >= 1:
                    wait_moved(dve, Q_NORM + h - 1)
                    dve.reciprocal(o_rinv[:, h - 1], o_rinv[:, h - 1]).then_inc(rinv_ready, 1)
            wait_moved(dve, Q_NORM + HEADS - 1)
            dve.reciprocal(o_rinv[:, HEADS - 1], o_rinv[:, HEADS - 1]).then_inc(rinv_ready, 1)
            dve.wait_ge(rinv_ready, HEADS)
            def split_low(layer, m, width):
                src = o_all if layer == 0 else lru_o
                dve.wait_ge(hi_split, (8 if layer == 0 else 32) + m + 1)
                dve.tensor_tensor(a_lo[:, m, 0:width], src[:, m, 0:width], a_hi[:, m, 0:width].bitcast(F32),
                                  ALU.subtract).then_inc(a_ready, 1)

            for h in range(HEADS):
                for t in range(2):
                    o = o_all[:, 2 * h + t]
                    steps.mark(dve.scalar_tensor_tensor(out=o, in0=o, scalar=vec[:, 1, V_HN + t:V_HN + t + 1],
                                                        in1=o_rinv[:, h], op0=ALU.mult, op1=ALU.mult))
                steps.wait()
                wait_moved(dve, Q_G + h)
                o = o_all[:, 2 * h:2 * h + 2]
                dve.tensor_tensor(o, o, silu_g[h % 2][:], ALU.mult).then_inc(gated, 1)

            def project_out(layer, parts):
                for m in range(KT):
                    split_low(layer, m, parts[-1][1] + parts[-1][2])
                q0 = Q_OUT0 if layer == 0 else Q_OUT1
                if layer == 0:
                    section(6, 6)
                else:
                    section(9, 9)
                    section(10, 10)
                residual_loop(q0, layer, 2, parts, PAIRS[2 * layer + 1], permuted=layer == 1)

            def residual_loop(q0, layer, place_, parts, pair=None, permuted=False):
                if pair is not None:
                    clear_sum()
                with steps.loop(2, 2 * (2 * len(parts) - 1 + (pair is not None))) as i:
                    for b in range(2):
                        q, tile = (q0 + b, 2, i), 4 * i + 2 * b
                        wait_done(dve, q)
                        for t in range(2):
                            for part, s, w in parts:
                                xt = xres[:, bass.ds(tile + t, 1), s:s + w].rearrange("p o n -> p (o n)")
                                src = tile_psum(q, t, part)
                                if permuted:
                                    xt = xt.rearrange("p (r c) -> p r c", r=ROWS)
                                    src = src.rearrange("p (c r) -> p r c", r=ROWS)
                                g = mod[:, 6 * layer + place_, bass.ds(tile + t, 1), part:part + 1]
                                ins = dve.scalar_tensor_tensor(out=xt, in0=src, scalar=g.rearrange("p o n -> p (o n)"),
                                                               in1=xt, op0=ALU.mult, op1=ALU.add)
                                if t == 1 and part == parts[-1][0]:
                                    moved(ins, q)
                                else:
                                    steps.mark(ins)
                        wait_moved(dve, q)
                        if pair is not None:
                            add_squares((pair + b, 2, i), (b, 2, i), parts[-1][1] + parts[-1][2])

            def ffn(layer, parts):
                q = Q_FFN0 if layer == 0 else Q_FFN1
                width = parts[-1][1] + parts[-1][2]
                for part, (first, n) in enumerate(FFN_PARTS):
                    with steps.loop(n // 2, 2 if len(parts) == 2 else 1) as i:
                        wait_moved(dve, (q, 2, i))
                        wait_done(dve, (q + 1, 2, i))
                        for k, s, w in parts:
                            ins = dve.tensor_tensor(hid[:, :, s:s + w], part_psum(q + 1, k), gate[:, :, s:s + w], ALU.mult)
                            if k == parts[-1][0]:
                                moved(ins, q + 1)
                            else:
                                steps.mark(ins)
                        wait_moved(dve, (q + 1, 2, i))
                        hh = h_hi[:, bass.ds(2 * i, 2), 0:width]
                        steps.link(dve.tensor_copy(hh, hid[:, :, 0:width]))
                        dve.tensor_tensor(h_lo[:, bass.ds(2 * i, 2), 0:width], hid[:, :, 0:width], hh.bitcast(F32),
                                          ALU.subtract).then_inc(hid_ready, 1)
                        dve.wait_ge(hid_ready, HID[layer][part] + i + 1)
                    q += n
                    residual_loop(q, layer, 5, parts, PAIRS[2] if layer == 0 and part == len(FFN_PARTS) - 1 else None)
                    q += 4

            project_out(0, BOTH)
            prep(0, 1, BOTH)
            section(7, 7)
            ffn(0, BOTH)
            prep(1, 0, BOTH)
            section(8, 8)
            dve.wait_ge(a_ready, 8 * (A_ORDER[("prep", 1, 0)] + 1))
            for lo_, hi_ in ((0, 2), (2 + LAT, 2 + LAT + GAP), (2 + UW, UW + 4)):
                ins = dve.memset(u_pad[:, :, lo_:hi_], 0.0)
            ins.then_inc(scanned, 1)
            dve.wait_ge(scanned, 1)
            with steps.loop(2, 44) as i:
                for b in range(2):
                    q0, n = (Q_LRU + 6 * b, 12, i), 2 * i + b
                    wait_moved(dve, q0)
                    for j in range(CONV_W):
                        for t in range(2):
                            col = vec[:, 1, bass.ds(V_CW + 8 * j + 2 * n + t, 1)]
                            if j == 0:
                                ins = dve.tensor_scalar(u_conv[:, t], u_pad[:, t, 0:UW], col,
                                                        vec[:, 1, bass.ds(V_CB + 2 * n + t, 1)], ALU.mult, ALU.add)
                            else:
                                ins = dve.scalar_tensor_tensor(out=u_conv[:, t], in0=u_pad[:, t, j:j + UW], scalar=col,
                                                               in1=u_conv[:, t], op0=ALU.mult, op1=ALU.add)
                            if j == CONV_W - 1 and t == 1:
                                ins.then_inc(conv_done, 1)
                            else:
                                steps.mark(ins)
                        if j < CONV_W - 1:
                            steps.wait()
                    dve.wait_ge(u_rounded, n + 1)
                    steps.mark(dve.tensor_tensor(u_lo[:, :, 0:LAT], u_conv[:, :, 0:LAT], u_hi[:, :, 0:LAT].bitcast(F32),
                                                 ALU.subtract))
                    dve.tensor_tensor(u_lo[:, :, LAT:TOK], u_conv[:, :, LAT + GAP:UW], u_hi[:, :, LAT:TOK].bitcast(F32),
                                      ALU.subtract).then_inc(u_ready, 1)
                    for d in range(2):
                        wait_moved(dve, plus(q0, 3 + 2 * d))
                        g = gates_r[:, 2 * d + 1]
                        steps.mark(dve.tensor_tensor(g[:, :, 0:LAT], g[:, :, 0:LAT], u_conv[:, :, 0:LAT], ALU.mult))
                        ins = dve.tensor_tensor(g[:, :, LAT:TOK], g[:, :, LAT:TOK], u_conv[:, :, LAT + GAP:UW], ALU.mult)
                        if d == 0:
                            steps.mark(ins)
                    ins.then_inc(factor, 1)
                    for d in range(2):
                        dve.wait_ge(a_sq, 2 * n + d + 1)
                        dve.scalar_tensor_tensor(out=scan_h[d][:], in0=u_conv[:, :, 0:TOK], scalar=1.0, in1=scan_h[d][:],
                                                 op0=ALU.add, op1=ALU.mult).then_inc(factor, 1)
                    dve.wait_ge(factor, 3 * n + 3)
                    for d in range(2):
                        dve.wait_ge(root, 2 * n + d + 1)
                        g = gates_r[:, 2 * d + 1]
                        steps.link(dve.tensor_tensor(g, g, scan_h[d][:], ALU.mult))
                        order_ = slice(None, None, -1) if d else slice(None)
                        for t in range(2):
                            a_, b_, o_ = gates_r[:, 2 * d, t], gates_r[:, 2 * d + 1, t], scan_h[d][:, t]
                            cx = [v[:, LAT:TOK][:, order_] for v in (o_, a_, b_)]
                            steps.mark(dve.tensor_tensor_scan(*cx, 0.0, ALU.mult, ALU.add))
                        steps.wait()
                        for t in range(2):
                            a_, b_, o_ = gates_r[:, 2 * d, t], gates_r[:, 2 * d + 1, t], scan_h[d][:, t]
                            lt = [v[:, 0:LAT][:, order_] for v in (o_, a_, b_)]
                            last = o_[:, LAT:LAT + 1] if d else o_[:, TOK - 1:TOK]
                            steps.mark(dve.tensor_tensor_scan(*lt, last, ALU.mult, ALU.add))
                        steps.wait()
                    steps.link(dve.tensor_tensor(scan_h[0][:, :, 0:LAT], scan_h[0][:, :, 0:LAT], scan_h[1][:, :, 0:LAT],
                                                 ALU.add))
                    wait_moved(dve, plus(q0, 1))
                    dve.tensor_tensor(lru_o[:, bass.ds(2 * n, 2)], scan_h[0][:, :, 0:LAT], lru_y[:], ALU.mult
                                      ).then_inc(scanned, 1)
            project_out(1, ONLY_LAT)
            prep(1, 1, ONLY_LAT)
            section(11, 11)
            ffn(1, ONLY_LAT)
            dve.wait_ge(final_g_loaded, 16)
            for t in range(4):
                q = Q_FINAL + t
                dve.wait_ge(y_rooted, t + 1)
                steps.link(dve.reciprocal(ysum[:, 2, t:t + 1], ysum[:, 1, t:t + 1]))
                moved(dve.scalar_tensor_tensor(out=y_rows[t][:], in0=duo(q)[:, 0:2, :].rearrange("p b n -> p (b n)"),
                                               scalar=ysum[:, 2, t:t + 1], in1=final_g[:], op0=ALU.mult,
                                               op1=ALU.mult), q)


SCAN = [[8, 9, 10, 11, 0, 1, 2, 3, 4, 5, 6, 7], [11, 10, 9, 8, 7, 6, 5, 4, 3, 2, 1, 0]]
STATE_BASE = [11, 0]
STATE_AFTER = [{n: STATE_BASE[d] + s for s, n in enumerate(SCAN[d][:11])} for d in range(2)]
STATE_BEFORE = [{n: (STATE_BASE[d] + s - 1 if s else None) for s, n in enumerate(SCAN[d])} for d in range(2)]
STATE_GROUPS = [(1, SCAN[1][0:6]), (1, SCAN[1][6:11]), (0, SCAN[0][0:6]), (0, SCAN[0][6:11])]
HID = [[0, 4, 8], [11, 15, 19]]
HI_SPLIT = [0, 16, 24, 40]
PAIRS = [0, 4, 8, 12]
SUMMED = [4, 8, 12, 16]
A_ORDER = {("prep", 0, 0): 0, ("out", 0): 1, ("prep", 0, 1): 2, ("prep", 1, 0): 3, ("out", 1): 4, ("prep", 1, 1): 5}


_INS = ["x", "c", "ctx", "c_ctx", "norm_mix_g", "norm_ffn_g", "w_mod", "b_mod", "gla_w_in", "gla_gate_w1",
        "gla_gate_w2", "gla_gate_b", "gla_head_norm_g", "gla_w_out", "lru_w_in", "lru_conv_w", "lru_conv_b",
        "lru_gate_a_w", "lru_gate_a_b", "lru_gate_x_w", "lru_gate_x_b", "lru_lambda", "lru_w_out", "ffn_w1",
        "ffn_w3", "ffn_w2", "final_norm_g"]


def kernel(**inputs):
    import numpy as _np
    import concourse.bacc as _bacc
    from concourse import mybir as _mybir
    from concourse.bass_utils import run_bass_kernel_spmd as _run

    nc = _bacc.Bacc("TRN2", target_bir_lowering=False, num_devices=1)
    arrays, args = {}, []
    for name in _INS:
        a = _np.ascontiguousarray(inputs[name])
        arrays[f"in_{name}_dram"] = a
        args.append(nc.dram_tensor(f"in_{name}_dram", a.shape, _mybir.dt.from_np(a.dtype), kind="ExternalInput").ap())
    args.append(nc.dram_tensor("out_dram", (1, LAT, D), _mybir.dt.float32, kind="ExternalOutput").ap())
    build(nc, *args)
    r = _run(nc, [arrays], core_ids=[0])
    return r.results[0]["out_dram"]
```

```python
from contextlib import ExitStack, contextmanager

import concourse.bass as bass
from concourse import mybir

P = 128
F32 = mybir.dt.float32
F32R = mybir.dt.float32r
BF16 = mybir.dt.bfloat16
I32 = mybir.dt.int32
ALU = mybir.AluOpType
ACT = mybir.ActivationFunctionType

LAT, CTX = 512, 256
TOK = LAT + CTX
D = 1024
KT = D // P
HEADS = 4
CHUNK = 64
NCH = TOK // CHUNK
TT = TOK // P
TAU = 16.0
RANK = 16
EPS = 1e-6
GRID_W = 64
ROWS = LAT // GRID_W
FFN = 2816
FT = FFN // P
FFN_PARTS = [(0, 8), (8, 8), (16, 6)]
CONV_W = 4
LRU_C = 8.0
DK_SCALE = float(P) ** -0.5
BOTH = [(0, 0, LAT), (1, LAT, CTX)]
ONLY_LAT = [(0, 0, LAT)]

Q_TURN = 0
Q_STAT = [[4, 58], [0, 0]]
Q_T = 5
Q_HEAD = 6
PER_HEAD = 10
Q_NG = Q_HEAD + HEADS * PER_HEAD
Q_OUT0 = Q_NG + 2 * HEADS
Q_STAT[0][1] = Q_OUT0 + 4
Q_FFN0 = Q_STAT[0][1] + 1
FFN_DUOS = sum(n + 4 for _, n in FFN_PARTS)
Q_STAT[1][0] = Q_FFN0 + FFN_DUOS
Q_LRU = Q_STAT[1][0] + 1
BLOCKS = 4
PER_BLOCK = 6
Q_OUT1 = Q_LRU + BLOCKS * PER_BLOCK
Q_STAT[1][1] = Q_OUT1 + 4
Q_FFN1 = Q_STAT[1][1] + 1
Q_FINAL = Q_FFN1 + FFN_DUOS

C_GATE1 = 0
C_HEAD = 1
C_G = C_HEAD + 2 * HEADS
C_OUT0 = C_G + 4
C_FFN0 = C_OUT0 + 4
C_LRU = C_FFN0 + FFN_DUOS
C_OUT1 = C_LRU + 4 * BLOCKS
C_FFN1 = C_OUT1 + 4
CHUNKS = C_FFN1 + FFN_DUOS
assert (CHUNKS - 1) % 2 == 0 and (C_OUT1 + 1) % 2 == 0

SEC_FIRST = [1, 0]
SEC_HEAD = 2
V_BMOD, V_NMIX, V_NFFN = 0, 96, 112
V_C, V_GB, V_HN, V_CW, V_CB, V_BA, V_BX, V_LAM, V_END = 0, 16, 24, 26, 58, 66, 82, 98, 114


class Steps:

    def __init__(self, eng, sem):
        self.eng, self.sem, self.base, self.k, self.i, self.per = eng, sem, 0, 0, 0, 0

    def mark(self, ins):
        ins.then_inc(self.sem, 1)
        self.k += 1

    def wait(self):
        self.eng.wait_ge(self.sem, self.base + self.i * self.per + self.k)

    def link(self, ins):
        self.mark(ins)
        self.wait()

    @contextmanager
    def loop(self, n, per):
        self.base, self.k, self.per = self.base + self.k, 0, per
        with self.eng.Fori(0, n) as i:
            self.i = i
            yield i
        assert self.k == per, (self.k, per)
        self.base, self.k, self.i, self.per = self.base + n * per, 0, 0, 0


def build(nc, x, c, ctx_in, c_ctx, norm_mix_g, norm_ffn_g, w_mod, b_mod, gla_w_in, gla_gate_w1, gla_gate_w2,
          gla_gate_b, gla_head_norm_g, gla_w_out, lru_w_in, lru_conv_w, lru_conv_b, lru_gate_a_w, lru_gate_a_b,
          lru_gate_x_w, lru_gate_x_b, lru_lambda, lru_w_out, ffn_w1, ffn_w3, ffn_w2, final_norm_g, out):
    es = ExitStack()
    with es:
        at = [-(-nc.sbuf_base // 64) * 64]

        def region(nbytes):
            start = at[0]
            at[0] += -(-nbytes // 32) * 32
            assert at[0] <= nc.sbuf_usable_end, at[0]
            return start

        def place(name, shape, dt, offset):
            return nc.alloc_sbuf_tensor_at(name, shape, dt, offset=offset)

        KB = 1024
        X_AT, A_AT, H_AT = region(24 * KB), region(48 * KB), region(48 * KB)
        W_AT, M_AT, T_AT = region(48 * KB), region(8 * KB), region(24 * KB)

        def small(name, shape, dt=F32):
            n = 2 if dt == BF16 else 4
            for s in shape[1:]:
                n *= s
            return place(name, shape, dt, region(n))

        xres = place("xres", [P, KT, TOK], F32, X_AT)
        a_hi = place("a_hi", [P, KT, TOK], F32R, A_AT)
        a_lo = place("a_lo", [P, KT, TOK], F32R, A_AT + 24 * KB)
        h_hi = place("h_hi", [P, 8, TOK], F32R, H_AT)
        h_lo = place("h_lo", [P, 8, TOK], F32R, H_AT + 24 * KB)
        raw = [place(f"raw{b}", [P, 8, 256], F32, W_AT + 8 * KB * b) for b in range(2)]
        w_hi = [place(f"w_hi{b}", [P, 8, 256], F32R, W_AT + 8 * KB * (2 + b)) for b in range(2)]
        w_lo = [place(f"w_lo{b}", [P, 8, 256], F32R, W_AT + 8 * KB * (4 + b)) for b in range(2)]
        mod_ring = [place(f"mod_ring{b}", [P, 8, P], F32, M_AT + 4 * KB * b) for b in range(2)]
        sec_rows = place("sec_rows", [2, 512], F32, H_AT + 46 * KB)
        first_rows = place("first_rows", [2, D], F32, W_AT + 40 * KB)
        mod_first = [place("mod_first0", [P, 8, D], F32, H_AT), place("mod_first1", [P, 8, D], F32, A_AT)]
        vec_rows = place("vec_rows", [P, 2, P], F32, A_AT + 32 * KB)
        x_rows = place("x_rows", [P, TT, D], F32, T_AT)
        sq = [place(f"sq{b}", [P, 2, TOK], F32, T_AT + 6 * KB * b) for b in range(2)]
        sqsum = place("sqsum", [P, TOK], F32, T_AT + 12 * KB)
        rdiag = place("rdiag", [P, TT, P], F32, T_AT + 15 * KB)
        normed = [place(f"normed{b}", [P, TOK], F32, T_AT + 18 * KB + 3 * KB * b) for b in range(2)]
        o_all = place("o_all", [P, 8, TOK], F32, H_AT)
        t_low = place("t_low", [64, TOK], F32, H_AT + 18 * KB)
        gate2 = place("gate2", [64, 2, P], F32, H_AT + 22 * KB)
        states = place("states", [P, 22, 256], F32, H_AT + 24 * KB)
        k_end = place("k_end", [P, 2, TOK], F32, H_AT + (24 + 16) * KB)
        q_dec = place("q_dec", [P, 2, TOK], F32, T_AT)
        k_inv = place("k_inv", [P, 2, TOK], F32, T_AT + 6 * KB)
        att = place("att", [P, 12, P], F32, T_AT + 6 * KB)
        zg = place("zg", [P, 2, TOK], F32, T_AT + 12 * KB)
        k_tok = place("k_tok", [P, 12, P], F32, T_AT + 12 * KB)
        bcum = place("bcum", [P, 2, TOK], F32, T_AT + 18 * KB)
        v_tok = place("v_tok", [P, TT, 256], F32, T_AT + 18 * KB)
        o_sq = place("o_sq", [P, 2, TOK], F32, T_AT)
        o_sum = [place(f"o_sum{b}", [P, TOK], F32, T_AT + 6 * KB + 3 * KB * b) for b in range(2)]
        silu_g = [place(f"silu_g{b}", [P, 2, TOK], F32, T_AT + 12 * KB + 6 * KB * b) for b in range(2)]
        o_rinv = place("o_rinv", [P, HEADS, TOK], F32, H_AT + 24 * KB)
        gate = place("gate", [P, 2, TOK], F32, T_AT)
        hid = place("hid", [P, 2, TOK], F32, T_AT + 6 * KB)
        GAP = 2
        UW = LAT + GAP + CTX
        lru_o = place("lru_o", [P, 8, LAT], F32, H_AT)
        lru_y = place("lru_y", [P, 2, LAT], F32, H_AT + 16 * KB)
        gates_r = place("gates_r", [P, 4, 2, TOK], F32, H_AT + 20 * KB)
        u_hi = place("u_hi", [P, 2, TOK], F32R, T_AT)
        u_lo = place("u_lo", [P, 2, TOK], F32R, T_AT + 6 * KB)
        scan_h = [place(f"scan_h{b}", [P, 2, TOK], F32, T_AT + 6 * KB * b) for b in range(2)]
        u_pad = place("u_pad", [P, 2, UW + 4], F32, T_AT + 12 * KB)
        UP_END = T_AT + 12 * KB + 2 * 4 * (UW + 4)
        u_conv = place("u_conv", [P, 2, UW], F32, -(-UP_END // 32) * 32)
        assert UP_END + 32 + 8 * UW <= T_AT + 24 * KB + 1024
        a_squares = [xres[:, 3 * t:3 * t + 3, LAT:TOK] for t in range(2)]
        final_g = place("final_g", [P, D], F32, M_AT)
        y_rows = [place(f"y_rows{b}", [P, D], F32, T_AT + 4 * KB * b) for b in range(4)]
        y_junk = place("y_junk", [P, D], F32, T_AT + 16 * KB)
        region(512)

        ident = small("ident", [P, P])
        ones = small("ones", [P, P])
        mask = small("mask", [P, 2, P])
        resets = small("resets", [P, NCH, CHUNK], BF16)
        vec = small("vec", [P, 2, P])
        cs = small("cs", [P, KT, 2])
        mod = small("mod", [P, 2 * 6, KT, 2])
        gain = small("gain", [P, 4, KT, 2])
        decay = small("decay", [P, 2, NCH])
        lru_c = small("lru_c", [P, 2, 16])
        lw = small("lw", [P, 4, 16])
        eps = small("eps", [P, 1])
        zero = small("zero", [P, 1])
        rms = small("rms", [P, 2, 8])
        ysum = small("ysum", [P, 3, 4])

        duo_psum = [es.enter_context(nc.psum_tensor(f"duo{b}", [P, 3, 512], F32)) for b in range(2)]
        vec_psum = es.enter_context(nc.psum_tensor("vec_psum", [P, 512], F32))
        mod_psum = es.enter_context(nc.psum_tensor("mod_psum", [P, 512], F32))

        def sem(name):
            return es.enter_context(nc.semaphore(name))

        consts_made, pads_made = sem("consts_made"), sem("pads_made")
        vec_loaded, x_loaded = sem("vec_loaded"), sem("x_loaded")
        first_loaded = [[sem(f"first_loaded{b}_{k}") for k in range(4)] for b in range(2)]
        vec_turned, vec_ready, cs_ready = sem("vec_turned"), sem("vec_ready"), sem("cs_ready")
        raw_loaded = [sem(f"raw_loaded{b}") for b in range(2)]
        hi_ready, lo_ready = sem("hi_ready"), sem("lo_ready")
        mod_loaded = [sem(f"mod_loaded{b}") for b in range(2)]
        mod_used, mod_rowed, mod_turned, mod_ready = (sem("mod_used"), sem("mod_rowed"), sem("mod_turned"),
                                                      sem("mod_ready"))
        gate2_zeroed, gate2_loaded = sem("gate2_zeroed"), sem("gate2_loaded")
        duo_done = sem("duo_done")
        duo_moved = [sem(f"duo_moved{b}") for b in range(2)]
        act_step, dve_step = sem("act_step"), sem("dve_step")
        token_summed, rooted, diag_ready = sem("token_summed"), sem("rooted"), sem("diag_ready")
        squared, summed, scaled, hi_split, a_ready = (sem("squared"), sem("summed"), sem("scaled"),
                                                      sem("hi_split"), sem("a_ready"))
        z_logged, cum_ready, exps_ready = sem("z_logged"), sem("cum_ready"), sem("exps_ready")
        o_squared, o_summed, rinv_ready, gated = (sem("o_squared"), sem("o_summed"), sem("rinv_ready"),
                                                  sem("gated"))
        hid_ready, att_ready = sem("hid_ready"), sem("att_ready")
        scans_added = sem("scans_added")
        early_hi, early_split = sem("early_hi"), sem("early_split")
        conv_done, u_ready, a_sq, factor, root, scanned, lruc_ready = (
            sem("conv_done"), sem("u_ready"), sem("a_sq"), sem("factor"), sem("root"), sem("scanned"),
            sem("lruc_ready"))
        u_rounded = sem("u_rounded")
        y_rooted, final_g_loaded, stored = sem("y_rooted"), sem("final_g_loaded"), sem("stored")
        l_exp, l_w = sem("l_exp"), sem("l_w")

        def duo(q):
            return duo_psum[q % 2]

        def state_psum(q, s):
            if s < 4:
                return duo(par(q))[:, s % 2, (s // 2) * 256:(s // 2) * 256 + 256]
            return duo(par(q))[:, 2, 0:256] if s == 4 else vec_psum[:, 0:256]

        def half(i):
            if isinstance(i, tuple):
                base, per, reg = i
                assert per % 2 == 0
                return base // 2 + (per // 2) * reg
            return i // 2

        def whole(i):
            return i[0] + i[1] * i[2] if isinstance(i, tuple) else i

        def plus(i, k):
            return (i[0] + k, i[1], i[2]) if isinstance(i, tuple) else i + k

        def par(i):
            return (i[0] if isinstance(i, tuple) else i) % 2

        def wait_done(eng, q):
            eng.wait_ge(duo_done, whole(q) + 1)

        def wait_moved(eng, q):
            eng.wait_ge(duo_moved[par(q)], half(q) + 1)

        def moved(ins, q):
            ins.then_inc(duo_moved[par(q)], 1)

        def turn_column(s):
            return 256 + 16 * (not isinstance(s, tuple) and s == 10)

        A_READY = {key: KT * n - (6 if n > 4 else 0) for key, n in A_ORDER.items()}
        block = es.enter_context(nc.Block())

        @block.sync
        def _(sp):
            def raw_free(ch):
                if isinstance(ch, tuple) or ch >= 2:
                    sp.wait_ge(lo_ready, whole(ch) - 1)

            def load(ch, first, second):
                raw_free(ch)
                for dst, src in (first, second):
                    sp.dma_start(dst, src).then_inc(raw_loaded[par(ch)], 16)

            def columns(ch, w, col, rows=8):
                r = raw[par(ch)]
                v = w.rearrange("(k p) n -> p k n", p=P)
                m = rows // 2
                load(ch, (r[:, 0:m], v[:, 0:m, bass.ds(col, 256)]), (r[:, m:rows], v[:, m:rows, bass.ds(col, 256)]))

            def mod_pieces(u, layer, col, pieces=range(8)):
                v = w_mod[layer].rearrange("(k p) n -> p k n", p=P)
                for p in pieces:
                    sp.wait_ge(mod_used, whole(u) + p + 1)
                    sp.dma_start(mod_ring[p % 2][:], v[:, :, bass.ds(col + p * P, P)]).then_inc(mod_loaded[p % 2], 16)

            def mod_section(s, pieces=range(8)):
                mod_pieces(8 * (s - SEC_HEAD), s // 6, (s % 6) * D, pieces)

            def rows(dst, src):
                sp.dma_start(dst, src).then_inc(vec_loaded, 16)

            r0, r1 = vec_rows[:, 0], vec_rows[:, 1]
            rows(r0[V_BMOD:V_BMOD + 96], b_mod.rearrange("l (m p) -> (l m) p", p=P))
            rows(r0[V_NMIX:V_NMIX + 16], norm_mix_g.rearrange("l (m p) -> (l m) p", p=P))
            rows(r0[V_NFFN:V_NFFN + 16], norm_ffn_g.rearrange("l (m p) -> (l m) p", p=P))
            rows(r1[V_C:V_C + 8], c.rearrange("b (m p) -> (b m) p", p=P))
            rows(r1[V_C + 8:V_C + 16], c_ctx.rearrange("(m p) -> m p", p=P))
            rows(r1[V_GB:V_GB + 8], gla_gate_b.rearrange("j d (m p) -> (j d m) p", p=P))
            rows(r1[V_HN:V_HN + 2], gla_head_norm_g.rearrange("j (m p) -> (j m) p", p=P))
            rows(r1[V_CW:V_CW + 32], lru_conv_w.rearrange("j w (m p) -> (j w m) p", p=P))
            rows(r1[V_CB:V_CB + 8], lru_conv_b.rearrange("j (m p) -> (j m) p", p=P))
            rows(r1[V_BA:V_BA + 16], lru_gate_a_b.rearrange("j d (m p) -> (j d m) p", p=P))
            rows(r1[V_BX:V_BX + 16], lru_gate_x_b.rearrange("j d (m p) -> (j d m) p", p=P))
            rows(r1[V_LAM:V_LAM + 16], lru_lambda.rearrange("j d (m p) -> (j d m) p", p=P))
            def first_section(b):
                sec = SEC_FIRST[b]
                for k in range(0, KT, 2):
                    sp.dma_start(mod_first[b][:, k:k + 2], w_mod[0].rearrange("(k p) n -> p k n", p=P)[
                        :, k:k + 2, sec * D:(sec + 1) * D]).then_inc(first_loaded[b][k // 2], 16)

            first_section(0)
            sp.dma_start(x_rows[:, 0:4], x[0].rearrange("(t p) n -> p t n", p=P)).then_inc(x_loaded, 16)
            sp.dma_start(x_rows[:, 4:6], ctx_in[0].rearrange("(t p) n -> p t n", p=P)).then_inc(x_loaded, 16)
            first_section(1)
            sp.wait_ge(pads_made, 1)
            g1 = gla_gate_w1[0].rearrange("d (k p) r -> d p k r", p=P)
            load(C_GATE1, (raw[0][:, :, 0:RANK], g1[0]), (raw[0][:, :, 32:32 + RANK], g1[1]))
            qk = gla_w_in[0, :, 0:2 * LAT].rearrange("(k p) (s n) -> p k s n", p=P, s=2)

            def head_loads(ch, h):
                r = raw[par(ch)]
                load(ch, (r[:, :, 0:P], qk[:, :, 0, bass.ds(h * P, P)]), (r[:, :, P:2 * P], qk[:, :, 1, bass.ds(h * P, P)]))
                columns(plus(ch, 1), gla_w_in[0], 2 * LAT + 256 * h)

            def gate2_load(h):
                for d in range(2):
                    sp.dma_start(gate2[32 * d:32 * d + RANK, d], gla_gate_w2[0, d, :, bass.ds(h * P, P)]
                                 ).then_inc(gate2_loaded, 16)

            head_loads(C_HEAD, 0)
            sp.wait_ge(gate2_zeroed, 1)
            gate2_load(0)
            with sp.Fori(0, HEADS - 1) as h:
                head_loads((C_HEAD + 2, 2, h), h + 1)
                sp.wait_ge(duo_done, Q_HEAD + 1 + PER_HEAD * h)
                gate2_load(h + 1)
                mod_pieces((0, 8, h), 0, 2 * D + D * h)

            def gate_columns(n):
                columns(C_G + n, gla_w_in[0], 2 * LAT + D + 256 * n)

            gate_columns(0)
            gate_columns(1)
            mod_section(5)
            mod_section(6, (0, 1))
            gate_columns(2)
            mod_section(6, (2, 3))
            gate_columns(3)
            mod_section(6, (4, 5))
            columns(C_OUT0, gla_w_out[0], 0)
            mod_section(6, (6, 7))
            for n in range(1, 4):
                columns(C_OUT0 + n, gla_w_out[0], 256 * n)

            def ffn_loads(layer, section):
                ch = C_FFN0 if layer == 0 else C_FFN1
                for part, (first, n) in enumerate(FFN_PARTS):
                    begin = 0
                    if part == 0:
                        columns(ch, ffn_w1[layer], first * P)
                        columns(ch + 1, ffn_w3[layer], first * P)
                        mod_section(section)
                        begin = 1
                    with sp.Fori(begin, n // 2) as i:
                        columns((ch, 2, i), ffn_w1[layer], first * P + 256 * i)
                        columns((ch + 1, 2, i), ffn_w3[layer], first * P + 256 * i)
                    ch += n
                    w2 = ffn_w2[layer, first * P:(first + n) * P]
                    with sp.Fori(0, 2) as i:
                        for b in range(2):
                            columns((ch + b, 2, i), w2, 512 * i + 256 * b, rows=n)
                    ch += 4

            ffn_loads(0, 7)
            ga = lru_gate_a_w[0].rearrange("d g (k p) j -> d g p k j", p=P)
            gx = lru_gate_x_w[0].rearrange("d g (k p) j -> d g p k j", p=P)
            columns(C_LRU, lru_w_in[0], D)
            for n in range(BLOCKS):
                ch = C_LRU + 1 + 4 * n
                columns(ch, lru_w_in[0], 256 * n)
                if n == 0:
                    mod_section(8)
                if n < BLOCKS - 1:
                    ch += 1
                    columns(ch, lru_w_in[0], D + 256 * (n + 1))
                for d in range(2):
                    r = raw[par(ch + 1 + d)]
                    load(ch + 1 + d, (r[:, 0:2], ga[d, n]), (r[:, 2:4], gx[d, n]))
            mod_section(9)
            columns(C_OUT1, lru_w_out[0], 0)
            columns(C_OUT1 + 1, lru_w_out[0], 256)
            mod_section(10)
            for n in range(2, 4):
                columns(C_OUT1 + n, lru_w_out[0], 256 * n)
            ffn_loads(1, 11)
            sp.wait_ge(mod_used, 2 + 8 * 10)
            sp.dma_start(final_g[:], final_norm_g.partition_broadcast(P)).then_inc(final_g_loaded, 16)
            y_dram = out[0].rearrange("(t p) n -> t p n", p=P)
            for t in range(4):
                wait_moved(sp, Q_FINAL + t)
                sp.dma_start(y_dram[t], y_rows[t][:]).then_inc(stored, 16)
            sp.wait_ge(stored, 64)

        @block.gpsimd
        def _(pool):
            pool.memset(raw[0][:, :, 0:P], 0.0).then_inc(pads_made, 1)
            pool.memset(ident[:], 0.0)
            pool.memset(ones[:], 1.0)
            pool.memset(mask[:], 1.0)
            pool.memset(resets[:], 1.0)
            pool.memset(zero[:], 0.0)
            pool.memset(eps[:], EPS).then_inc(pads_made, 1)
            pool.wait_ge(pads_made, 2)
            pool.memset(resets[:, :, 0:1], 0.0)
            pool.affine_select(out=ident[:], in_=ident[:], compare_op=ALU.not_equal, fill=1.0, base=0,
                               pattern=[[-1, P]], channel_multiplier=1)
            pool.affine_select(out=mask[:, 0], in_=mask[:, 0], compare_op=ALU.is_ge, fill=0.0, base=0,
                               pattern=[[1, P]], channel_multiplier=-1)
            pool.affine_select(out=mask[:, 1], in_=mask[:, 1], compare_op=ALU.is_ge, fill=0.0, base=0,
                               pattern=[[-1, P]], channel_multiplier=1).then_inc(pads_made, 1)
            pool.wait_ge(pads_made, 3)
            pool.memset(mask[0:CHUNK, 0, CHUNK:P], 0.0)
            pool.memset(mask[CHUNK:P, 1, 0:CHUNK], 0.0).then_inc(consts_made, 1)

            def low(ch, cols=256):
                b = par(ch)
                pool.wait_ge(hi_ready, whole(ch) + 1)
                pool.tensor_tensor(w_lo[b][:, :, 0:cols], raw[b][:, :, 0:cols],
                                   w_hi[b][:, :, 0:cols].bitcast(F32), ALU.subtract).then_inc(lo_ready, 1)

            low(C_GATE1, P)
            with pool.Fori(0, (C_OUT1 + 1) // 2) as i:
                for b in range(2):
                    low((1 + b, 2, i))
            pool.wait_ge(duo_done, Q_OUT1 - 4)
            for m in range(6):
                if m % 2 == 0:
                    pool.wait_ge(scanned, m // 2 + 2)
                pool.tensor_copy(a_hi[:, m, 0:LAT], lru_o[:, m]).then_inc(early_hi, 1)
                pool.wait_ge(early_hi, m + 1)
                pool.tensor_tensor(a_lo[:, m, 0:LAT], lru_o[:, m], a_hi[:, m, 0:LAT].bitcast(F32),
                                   ALU.subtract).then_inc(early_split, 1)
            with pool.Fori(0, (CHUNKS - C_OUT1 - 2) // 2) as i:
                for b in range(2):
                    low((C_OUT1 + 2 + b, 2, i))

        @block.tensor
        def _(pe):
            def duo_wait(q):
                if isinstance(q, tuple) or q >= 2:
                    pe.wait_ge(duo_moved[par(q)], half(q))

            def chunk_wait(ch):
                pe.wait_ge(hi_ready, whole(ch) + 1)
                pe.wait_ge(lo_ready, whole(ch) + 1)

            def tile_out(ps, t, part, n):
                return ps[:, t, 0:n] if part == 0 else ps[:, 2, t * CTX:t * CTX + n]

            def tile_pair(ch, q, parts, act_hi, act_lo, rows=8, ready=None, pieces=None, cols=(0, 1), k0=0,
                          by_row=True):
                chunk_wait(ch)
                duo_wait(q)
                ps, hi, lo = duo(par(q)), w_hi[par(ch)], w_lo[par(ch)]
                by_row = by_row and ready is not None
                order = [(t, k) for k in range(rows) for t in cols] if by_row else [(t, k) for t in cols for k in range(rows)]
                for n_, (t, k) in enumerate(order):
                    if ready is not None and t == cols[0]:
                        ready(k)
                    if pieces is not None and n_ % rows == rows // 2:
                        pieces(n_ // rows)
                    first, last = k == 0, k == rows - 1
                    wh, wl = hi[:, k0 + k, t * P:(t + 1) * P], lo[:, k0 + k, t * P:(t + 1) * P]
                    for part, s, n in parts:
                        begin = first and not (by_row and part == 1 and t != cols[0])
                        pe.matmul(tile_out(ps, t, part, n), wh, act_hi[:, k, s:s + n], start=begin, stop=False,
                                  skip_group_check=True)
                    for part, s, n in parts:
                        pe.matmul(tile_out(ps, t, part, n), wh, act_lo[:, k, s:s + n], start=False, stop=False,
                                  skip_group_check=True)
                    for part, s, n in parts:
                        mm = pe.matmul(tile_out(ps, t, part, n), wl, act_hi[:, k, s:s + n], start=False, stop=last,
                                       skip_group_check=True)
                return mm

            def a_wait(key):
                return lambda k: pe.wait_ge(a_ready, A_READY[key] + k + 1)

            def split_wait(layer):
                def wait(k):
                    if layer == 0:
                        pe.wait_ge(a_ready, A_READY[("out", 0)] + k + 1)
                    elif k < 6:
                        pe.wait_ge(early_split, k + 1)
                    else:
                        pe.wait_ge(a_ready, A_READY[("out", 1)] + k - 5)
                return wait

            def mod_piece(s, p):
                u = plus(p, 8 * (s - SEC_HEAD)) if not isinstance(s, tuple) else (8 * (s[0] - SEC_HEAD) + p, 8, s[2])
                if p in (0, 4) or isinstance(p, tuple) and p[0] in (0, 4):
                    pe.wait_ge(mod_rowed, 2 * whole(s) + (p // 4 if not isinstance(p, tuple) else p[2]))
                    if p == 0 and isinstance(s, tuple):
                        pe.wait_ge(mod_ready, 2)
                pe.wait_ge(mod_loaded[par(p)], 16 * (half(u) + 1))
                at_ = P * (p % 4 if not isinstance(p, tuple) else p[0])
                for k in range(KT):
                    mm = pe.matmul(mod_psum[0:2, at_:at_ + P], cs[:, k], mod_ring[par(p)][:, k], start=k == 0,
                                   stop=k == KT - 1, skip_group_check=True)
                mm.then_inc(mod_used, 1)

            def turn(s, h):
                reg = isinstance(h, tuple)
                pe.wait_ge(mod_rowed, 2 * whole(s) + (h[2] if reg else h) + 1)
                c0 = turn_column(s) + 8 * (h[2] if reg else h)
                for p in range(4):
                    out_ = vec_psum[:, bass.ds(c0 + 2 * p, 2)]
                    mm = pe.matmul(out_, sec_rows[:, p * P:(p + 1) * P], ident[0:2, 0:2], start=True, stop=True,
                                   skip_group_check=True)
                mm.then_inc(mod_turned, 1)

            def rms_sum(q, parts, src, ready, n):
                pe.wait_ge(ready, n)
                duo_wait(q)
                for part, s, w in parts:
                    mm = pe.matmul(tile_out(duo(par(q)), 0, part, w), ones[:], src[:, s:s + w], start=True, stop=True)
                mm.then_inc(duo_done, 1)

            def token_sums(n, parts):
                q = Q_STAT[n // 2][n % 2]
                pe.wait_ge(summed, SUMMED[n])
                duo_wait(q)
                for t in range((parts[-1][1] + parts[-1][2]) // P):
                    mm = pe.matmul(duo(q)[:, 1, 2 * t:2 * t + 2], sqsum[:, t * P:(t + 1) * P], ones[:, 0:2], start=True,
                                   stop=True, skip_group_check=True)
                mm.then_inc(token_summed, 1)

            def spread(n, parts):
                q = Q_STAT[n // 2][n % 2]
                pe.wait_ge(diag_ready, n + 1)
                for part, s, w in parts:
                    mm = pe.matmul(tile_out(duo(q), 0, part, w), ones[:],
                                   rdiag[:, s // P:(s + w) // P].rearrange("p t n -> p (t n)"), start=True, stop=True)
                mm.then_inc(duo_done, 1)

            pe.wait_ge(consts_made, 1)
            pe.wait_ge(vec_loaded, 16 * 12)
            pe.transpose(vec_psum[:, 0:P], vec_rows[:, 0], ident[:])
            pe.transpose(vec_psum[:, P:P + V_END], vec_rows[0:V_END, 1], ident[0:V_END, 0:V_END]).then_inc(vec_turned, 1)
            def first_section(b, between=None):
                if b:
                    pe.wait_ge(mod_ready, b)
                for k in range(KT):
                    if between is not None and k == KT - 2:
                        between()
                    pe.wait_ge(first_loaded[b][k // 2], 16)
                    for n, ps in enumerate((mod_psum, vec_psum)):
                        mm = pe.matmul(ps[0:2, :], cs[:, k], mod_first[b][:, k, n * 512:(n + 1) * 512], start=k == 0,
                                       stop=k == KT - 1, skip_group_check=True)
                mm.then_inc(mod_used, 1)
                if b:
                    spread(0, BOTH)
                pe.wait_ge(mod_rowed, 2 * b + 2)
                for p in range(8):
                    mm = pe.matmul(mod_psum[:, 2 * p:2 * p + 2], first_rows[:, p * P:(p + 1) * P], ident[0:2, 0:2],
                                   start=True, stop=True, skip_group_check=True)
                    if p % 4 == 3:
                        mm.then_inc(mod_turned, 1)

            pe.wait_ge(cs_ready, 1)
            first_section(0)
            pe.wait_ge(x_loaded, 32)
            for i in range(4):
                q = Q_TURN + i
                duo_wait(q)
                for t in range(2):
                    f = 2 * i + t
                    for tau in range(TT):
                        dst = (duo(q)[:, t, tau * P:(tau + 1) * P] if tau < 4
                               else duo(q)[:, 2, t * CTX + (tau - 4) * P:t * CTX + (tau - 3) * P])
                        mm = pe.transpose(dst, x_rows[:, tau, f * P:(f + 1) * P], ident[:])
                mm.then_inc(duo_done, 1)
            first_section(1, lambda: token_sums(0, BOTH))

            tile_pair(C_GATE1, Q_T, BOTH, a_hi, a_lo, ready=a_wait(("prep", 0, 0)), cols=(0,)).then_inc(duo_done, 1)
            wait_moved(pe, Q_T)
            with pe.Fori(0, HEADS) as h:
                q0 = (Q_HEAD, PER_HEAD, h)
                pe.wait_ge(gate2_loaded, 32 * h + 32)
                duo_wait(q0)
                for d in range(2):
                    for part, s, n in BOTH:
                        mm = pe.matmul(tile_out(duo(par(q0)), d, part, n), gate2[:, d], t_low[:, s:s + n], start=True, stop=True,
                                       skip_group_check=True)
                mm.then_inc(duo_done, 1)
                ch = (C_HEAD, 2, h)
                tile_pair(ch, plus(q0, 1), BOTH, a_hi, a_lo).then_inc(duo_done, 1)
                chv, qv = plus(ch, 1), plus(q0, 2)
                chunk_wait(chv)
                duo_wait(qv)
                hi, lo = w_hi[par(chv)], w_lo[par(chv)]
                for tau in range(TT):
                    dst = duo(par(qv))[:, tau // 2, (tau % 2) * 256:(tau % 2) * 256 + 256]
                    for k in range(KT):
                        ah, al = a_hi[:, k, tau * P:(tau + 1) * P], a_lo[:, k, tau * P:(tau + 1) * P]
                        pe.matmul(dst, ah, hi[:, k], start=k == 0, stop=False, skip_group_check=True)
                        pe.matmul(dst, ah, lo[:, k], start=False, stop=False, skip_group_check=True)
                        mm = pe.matmul(dst, al, hi[:, k], start=False, stop=k == KT - 1, skip_group_check=True)
                mm.then_inc(duo_done, 1)
                sec = (SEC_HEAD, 1, h)
                mod_piece(sec, 0)
                wait_moved(pe, plus(q0, 1))
                qt = plus(q0, 3)
                duo_wait(qt)
                for j in range(12):
                    d, tau = j // 6, j % 6
                    mm = pe.transpose(duo(par(qt))[:, j // 4, (j % 4) * P:(j % 4 + 1) * P],
                                      k_end[:, d, tau * P:(tau + 1) * P], ident[:])
                mm.then_inc(duo_done, 1)
                mod_piece(sec, 1)
                qa = plus(q0, 4)
                duo_wait(qa)
                for j in range(12):
                    d, tau = j // 6, j % 6
                    mm = pe.matmul(duo(par(qa))[:, j // 4, (j % 4) * P:(j % 4 + 1) * P],
                                   k_inv[:, d, tau * P:(tau + 1) * P], q_dec[:, d, tau * P:(tau + 1) * P],
                                   start=True, stop=True, skip_group_check=True)
                mm.then_inc(duo_done, 1)
                mod_piece(sec, 2)
                mod_piece(sec, 3)
                pe.wait_ge(mod_ready, whole(sec))
                wait_moved(pe, qt)
                wait_moved(pe, qv)
                for g, (d, chunks) in enumerate(STATE_GROUPS):
                    qu = plus(q0, 5 + g)
                    duo_wait(qu)
                    for s, n in enumerate(chunks):
                        r = CHUNK * (n % 2)
                        mm = pe.matmul(state_psum(qu, s),
                                       k_tok[r:r + CHUNK, d * 6 + n // 2], v_tok[r:r + CHUNK, n // 2],
                                       start=True, stop=True, skip_group_check=True)
                    mm.then_inc(duo_done, 1)
                    if g == 1:
                        wait_moved(pe, plus(q0, 5))
                        turn(sec, 0)
                    if g >= 1:
                        mod_piece(sec, 3 + g)
                mod_piece(sec, 7)
                for g in range(4):
                    wait_moved(pe, plus(q0, 5 + g)) if g >= 2 else None
                pe.wait_ge(att_ready, h + 1)
                qo = plus(q0, 9)
                duo_wait(qo)
                for tau in range(TT):
                    for v in range(2):
                        c0 = (tau % 2) * 256 + v * P
                        dst = duo(par(qo))[:, tau // 2, c0:c0 + P]
                        pe.matmul(dst, v_tok[:, tau, v * P:(v + 1) * P], att[:, tau], start=True, stop=False,
                                  skip_group_check=True)
                        for n in (2 * tau, 2 * tau + 1):
                            for d in range(2):
                                s = STATE_BEFORE[d][n]
                                if s is not None:
                                    mm = pe.matmul(duo(par(qo))[:, tau // 2, c0 + CHUNK * (n % 2):c0 + CHUNK * (n % 2) + CHUNK],
                                                   states[:, s, v * P:(v + 1) * P],
                                                   q_dec[:, d, n * CHUNK:(n + 1) * CHUNK], start=False,
                                                   stop=n % 2 == 1 and d == 1, skip_group_check=True)
                mm.then_inc(duo_done, 1)
                turn(sec, 1)

            with pe.Fori(0, 2) as i:
                for b in range(2):
                    rms_sum((Q_NG + 2 * b, 4, i), BOTH, o_sum[b], o_summed, 2 * i + b + 1)
                    tile_pair((C_G + b, 2, i), (Q_NG + 2 * b + 1, 4, i), BOTH, a_hi, a_lo,
                              pieces=lambda p: mod_piece(6, (2 * b + p, 4, i))).then_inc(duo_done, 1)
                turn(6, (0, 1, i))

            def project_out(layer, parts):
                c0, q0 = (C_OUT0, Q_OUT0) if layer == 0 else (C_OUT1, Q_OUT1)
                if layer == 1:
                    for h in range(2):
                        mod_pair(10, h)
                        turn(10, h)
                with pe.Fori(0, 2) as i:
                    for b in range(2):
                        tile_pair((c0 + b, 2, i), (q0 + b, 2, i), parts, a_hi, a_lo,
                                  ready=split_wait(layer) if b == 0 else None).then_inc(duo_done, 1)

            def ffn(layer, parts):
                ch, q = (C_FFN0, Q_FFN0) if layer == 0 else (C_FFN1, Q_FFN1)
                norm_sums(7 if layer == 0 else 11, 2 * layer + 1, parts)
                hb = 0 if layer == 0 else FT // 2
                for part, (first, n) in enumerate(FFN_PARTS):
                    with pe.Fori(0, n // 2) as i:
                        tile_pair((ch, 2, i), (q, 2, i), parts, a_hi, a_lo,
                                  ready=a_wait(("prep", layer, 1)) if part == 0 else None).then_inc(duo_done, 1)
                        tile_pair((ch + 1, 2, i), (q + 1, 2, i), parts, a_hi, a_lo).then_inc(duo_done, 1)
                    ch, q, hb = ch + n, q + n, hb + n // 2
                    with pe.Fori(0, 2) as i:
                        for b in range(2):
                            rd = (lambda k: pe.wait_ge(hid_ready, hb - n // 2 + k // 2 + 1) if k % 2 == 0 else None)
                            tile_pair((ch + b, 2, i), (q + b, 2, i), parts, h_hi, h_lo, rows=n,
                                      ready=rd if b == 0 else None, by_row=False).then_inc(duo_done, 1)
                    ch, q = ch + 4, q + 4

            def mod_pair(s, half_):
                for p in range(4 * half_, 4 * half_ + 4):
                    mod_piece(s, p)

            def norm_sums(s, n, parts):
                mod_pair(s, 0)
                token_sums(n, parts)
                turn(s, 0)
                mod_piece(s, 4)
                spread(n, parts)
                for p in range(5, 8):
                    mod_piece(s, p)
                turn(s, 1)

            project_out(0, BOTH)
            ffn(0, BOTH)
            norm_sums(8, 2, BOTH)
            tile_pair(C_LRU, Q_LRU, BOTH, a_hi, a_lo, ready=a_wait(("prep", 1, 0))).then_inc(duo_done, 1)

            def lru_block(n, ch, q, last):
                tile_pair(ch, q, ONLY_LAT, a_hi, a_lo).then_inc(duo_done, 1)
                if not last:
                    ch, q = plus(ch, 1), plus(q, 1)
                    tile_pair(ch, q, BOTH, a_hi, a_lo).then_inc(duo_done, 1)
                else:
                    for h in range(2):
                        mod_pair(9, h)
                        turn(9, h)
                pe.wait_ge(u_ready, n + 1)
                for gi in range(4):
                    tile_pair(plus(ch, 1 + gi // 2), plus(q, 1 + gi), BOTH, u_hi, u_lo, rows=2, k0=2 * (gi % 2)
                              ).then_inc(duo_done, 1)

            with pe.Fori(0, BLOCKS - 1) as n:
                lru_block(n, (C_LRU + 1, 4, n), (Q_LRU + 1, PER_BLOCK, n), False)
            lru_block(BLOCKS - 1, C_OUT1 - 3, Q_OUT1 - 5, True)
            project_out(1, ONLY_LAT)
            ffn(1, ONLY_LAT)
            wait_moved(pe, Q_FINAL - 2)
            wait_moved(pe, Q_FINAL - 1)
            for t in range(4):
                q = Q_FINAL + t
                duo_wait(q)
                for f in range(KT):
                    mm = pe.transpose(duo(q)[:, f // 4, (f % 4) * P:(f % 4 + 1) * P], xres[:, f, t * P:(t + 1) * P],
                                      ident[:])
                mm.then_inc(duo_done, 1)

        @block.scalar
        def _(act):
            steps = Steps(act, act_step)

            def high(ch, q_before, cols=256, rows=8):
                if not isinstance(ch, tuple) and ch >= CHUNKS:
                    return
                b = par(ch)
                act.wait_ge(raw_loaded[b], 32 * (half(ch) + 1))
                if q_before is not None:
                    wait_done(act, q_before)
                act.activation(w_hi[b][:, 0:rows, 0:cols], raw[b][:, 0:rows, 0:cols], ACT.Copy).then_inc(hi_ready, 1)

            def part_psum(q, part):
                ps = duo(par(q))
                return ps[:, 0:2, :] if part == 0 else ps[:, 2, :].rearrange("p (t n) -> p t n", t=2)

            def tile_psum(q, t, part):
                ps = duo(par(q))
                return ps[:, t, :] if part == 0 else ps[:, 2, t * CTX:(t + 1) * CTX]

            def square(pair, n, width):
                if not isinstance(pair, tuple) and pair >= 2 or isinstance(pair, tuple) and pair[0] >= 2:
                    act.wait_ge(summed, whole(pair) - 1)
                act.activation(sq[par(pair)][:, :, 0:width], xres[:, bass.ds(2 * whole(n), 2), 0:width], ACT.Square
                               ).then_inc(squared, 1)

            def prep(layer, which, parts):
                n = 2 * layer + which
                q = Q_STAT[layer][which]
                act.wait_ge(token_summed, n + 1)
                tiles = (parts[-1][1] + parts[-1][2]) // P
                act.activation(rms[:, 0, 0:tiles], duo(q)[:, 1, 0:2 * tiles:2],
                               ACT.Sqrt, bias=eps[:, 0:1], scale=1.0 / D).then_inc(rooted, 1)
                sec = 6 * layer + 3 * which
                if n == 0:
                    first_copy(1)
                    act.wait_ge(mod_ready, 2)
                for m in range(KT):
                    act.wait_ge(scaled, 8 * n + m + 1)
                    for part, s, w in parts:
                        dst, src = a_hi[:, m, s:s + w], normed[m % 2][:, s:s + w]
                        if part == 0 and (layer, which) == (1, 0):
                            dst = dst.rearrange("p (c r) -> p r c", r=ROWS)
                            src = src.rearrange("p (r c) -> p r c", r=ROWS)
                        ins = act.activation(dst, src, ACT.Identity, bias=mod[:, sec, m, part:part + 1])
                    ins.then_inc(hi_split, 1)
                    if n > 0 and m == 0:
                        row_copy([0, 7, 8, 11][n], 1)

            def row_copy(s, h):
                h = h[2] if isinstance(h, tuple) else h
                act.wait_ge(mod_used, 8 * whole(s) + 4 * h - 10)
                act.wait_ge(mod_turned, 2 * whole(s) + h)
                act.activation(sec_rows[:], mod_psum[0:2, :], ACT.Copy).then_inc(mod_rowed, 1)

            act.wait_ge(vec_ready, 1)
            act.activation(cs[:].rearrange("p k v -> p v k"), vec[:, 1, V_C:V_C + 16].rearrange("p (v k) -> p v k", v=2),
                           ACT.Silu).then_inc(cs_ready, 1)

            def first_copy(b):
                act.wait_ge(mod_used, b + 1)
                if b:
                    act.wait_ge(mod_turned, 2 * b)
                for n, ps in enumerate((mod_psum, vec_psum)):
                    act.activation(first_rows[:, n * 512:(n + 1) * 512], ps[0:2, :], ACT.Copy).then_inc(mod_rowed, 1)

            first_copy(0)
            for i in (1, 3):
                q = Q_TURN + i
                wait_done(act, q)
                steps.mark(act.activation(xres[:, 2 * i:2 * i + 2, 0:LAT], part_psum(q, 0), ACT.Copy))
                moved(act.activation(xres[:, 2 * i:2 * i + 2, LAT:TOK], part_psum(q, 1), ACT.Copy), q)
            for i in range(4):
                wait_moved(act, Q_TURN + i)
            for n in range(4):
                square(n, n, TOK)
            high(0, None, P)
            prep(0, 0, BOTH)
            high(1, None)

            act.preload_act_table_set("natural_log_exp_and_others")
            act.wait_ge(l_w, 1)
            act.activation(lw[:, 0], lw[:, 3], ACT.Exp, scale=-1.0).then_inc(l_exp, 1)
            wait_done(act, Q_T)
            steps.mark(act.activation(t_low[:, 0:LAT], duo(Q_T)[0:64, 0, :], ACT.Copy))
            moved(act.activation(t_low[:, LAT:TOK], duo(Q_T)[0:64, 2, 0:CTX], ACT.Copy), Q_T)
            high(2, Q_T)
            with steps.loop(HEADS, 10) as h:
                q0 = (Q_HEAD, PER_HEAD, h)
                wait_done(act, q0)
                for d in range(2):
                    for part, s, n in BOTH:
                        ins = act.activation(zg[:, d, s:s + n], tile_psum(q0, d, part), ACT.Identity,
                                             bias=vec[:, 1, bass.ds(V_GB + 4 * d + h, 1)])
                        if d == 1 and part == 1:
                            moved(ins, q0)
                        else:
                            steps.mark(ins)
                wait_moved(act, q0)
                steps.link(act.activation(bcum[:], zg[:], ACT.Abs))
                steps.link(act.activation(bcum[:], bcum[:], ACT.Exp, scale=-1.0))
                act.activation(bcum[:], bcum[:], ACT.Ln, bias=1.0).then_inc(z_logged, 1)
                act.wait_ge(cum_ready, h + 1)
                steps.mark(act.activation(q_dec[:], bcum[:], ACT.Exp, scale=1.0 / TAU))
                steps.mark(act.activation(k_inv[:], bcum[:], ACT.Exp, scale=-1.0 / TAU))
                steps.mark(act.activation(k_end[:], zg[:], ACT.Exp, scale=1.0 / TAU))
                steps.mark(act.activation(decay[:, 0], bcum[:, 0, CHUNK - 1::CHUNK], ACT.Exp, scale=1.0 / TAU))
                act.activation(decay[:, 1], bcum[:, 1, 0::CHUNK], ACT.Exp, scale=1.0 / TAU).then_inc(exps_ready, 1)
                ch = (C_HEAD, 2, h)
                act.wait_ge(exps_ready, h + 1)
                wait_done(act, plus(q0, 2))
                moved(act.activation(v_tok[:].rearrange("p t n -> p (t n)"),
                                     duo(par(q0))[:].rearrange("p b n -> p (b n)"), ACT.Copy), plus(q0, 2))
                wait_done(act, plus(q0, 3))
                moved(act.activation(k_tok[:].rearrange("p t n -> p (t n)"),
                                     duo(par(plus(q0, 3)))[:].rearrange("p b n -> p (b n)"), ACT.Copy), plus(q0, 3))
                high(plus(ch, 2), plus(q0, 1))
                high(plus(ch, 3), plus(q0, 2))
                row_copy((SEC_HEAD, 1, h), 0)
                row_copy((SEC_HEAD, 1, h), 1)
                qo = plus(q0, 9)
                wait_done(act, qo)
                src = duo(par(qo))[:].rearrange("p b (t v n) -> p v (b t) n", t=2, v=2)
                steps.mark(act.activation(o_all[:, bass.ds(2 * h, 1)].rearrange("p o (t n) -> p (o t) n", n=P), src[:, 0],
                                          ACT.Copy))
                moved(act.activation(o_all[:, bass.ds(2 * h + 1, 1)].rearrange("p o (t n) -> p (o t) n", n=P), src[:, 1],
                                     ACT.Copy), qo)
            wait_moved(act, Q_NG - 1)

            def head_square(h):
                if h:
                    act.wait_ge(o_summed, h)
                act.activation(o_sq[:], o_all[:, 2 * h:2 * h + 2], ACT.Square).then_inc(o_squared, 1)

            def output_gate(h):
                q = Q_NG + 2 * h + 1
                wait_done(act, q)
                if h >= 2:
                    act.wait_ge(gated, h - 1)
                act.activation(silu_g[h % 2][:, :, 0:LAT], part_psum(q, 0), ACT.Silu)
                moved(act.activation(silu_g[h % 2][:, :, LAT:TOK], part_psum(q, 1), ACT.Silu), q)

            head_square(0)
            head_square(1)
            for h in range(HEADS):
                q = Q_NG + 2 * h
                wait_done(act, q)
                for part, s, n in BOTH:
                    ins = act.activation(o_rinv[:, h, s:s + n], tile_psum(q, 0, part), ACT.Sqrt,
                                         bias=eps[:, 0:1], scale=1.0 / 256)
                    if part:
                        moved(ins, q)
                if h < 2:
                    head_square(h + 2)
                if h % 2:
                    row_copy(6, h // 2)
                if h < HEADS - 1:
                    output_gate(h)
                    high(C_G + h + 2, q + 1)

            def split_out(layer, parts):
                src = o_all if layer == 0 else lru_o
                width = parts[-1][1] + parts[-1][2]
                wait_done(act, Q_OUT0 - 1 if layer == 0 else Q_OUT1 - 1)
                for m in range(0 if layer == 0 else 6, KT):
                    if layer == 0 and m == 2:
                        output_gate(HEADS - 1)
                        high(C_OUT0 + 1, Q_OUT0 - 1)
                    if m % 2 == 0:
                        act.wait_ge(gated if layer == 0 else scanned, m // 2 + 1 + layer)
                    act.activation(a_hi[:, m, 0:width], src[:, m, 0:width], ACT.Copy).then_inc(hi_split, 1)
                c0, q0 = (C_OUT0, Q_OUT0) if layer == 0 else (C_OUT1, Q_OUT1)
                residual_loop(c0, q0, PAIRS[2 * layer + 1], width)

            def residual_loop(c0, q0, pair, width, last=False):
                with act.Fori(0, 2) as i:
                    for b in range(2):
                        if not last:
                            high((c0 + 2 + b, 2, i), (q0 + b, 2, i))
                        wait_moved(act, (q0 + b, 2, i))
                        if pair is not None:
                            square((pair + b, 2, i), (b, 2, i), width)

            def ffn(layer, parts):
                ch, q = (C_FFN0, Q_FFN0) if layer == 0 else (C_FFN1, Q_FFN1)
                for part, (first, n) in enumerate(FFN_PARTS):
                    with act.Fori(0, n // 2) as i:
                        wait_done(act, (q, 2, i))
                        act.wait_ge(duo_moved[(q + 1) % 2], half((q + 1, 2, i)))
                        for k, s, w in parts:
                            ins = act.activation(gate[:, :, s:s + w], part_psum(q, k), ACT.Silu)
                            if k == parts[-1][0]:
                                moved(ins, q)
                        high((ch + 2, 2, i), (q, 2, i))
                        high((ch + 3, 2, i), (q + 1, 2, i))
                    ch, q = ch + n, q + n
                    last = layer == 1 and part == len(FFN_PARTS) - 1
                    if last:
                        for b in range(2):
                            high(ch + 2 + b, q + b)
                    elif part == len(FFN_PARTS) - 1:
                        residual_loop(ch, q, PAIRS[2], TOK)
                    else:
                        with act.Fori(0, 2) as i:
                            for b in range(2):
                                high((ch + 2 + b, 2, i), (q + b, 2, i))
                    ch, q = ch + 4, q + 4

            split_out(0, BOTH)
            act.preload_act_table_set("sqrt_and_others")
            row_copy(7, 0)
            prep(0, 1, BOTH)
            ffn(0, BOTH)
            act.preload_act_table_set("sqrt_and_others")
            row_copy(8, 0)
            prep(1, 0, BOTH)
            def block_input(q):
                wait_done(act, q)
                steps.mark(act.activation(u_pad[:, :, 2:2 + LAT], part_psum(q, 0), ACT.Copy))
                moved(act.activation(u_pad[:, :, 2 + LAT + GAP:2 + UW], part_psum(q, 1), ACT.Copy), q)

            def lru_block(n, ch, q, last):
                cg = plus(ch, 1 if last else 2)
                qg = plus(q, 1 if last else 2)
                if not last:
                    high(cg, q, rows=4)
                else:
                    row_copy(9, 0)
                    row_copy(9, 1)
                act.wait_ge(conv_done, n + 1)
                act.wait_ge(scans_added, n + 1)
                steps.mark(act.activation(u_hi[:, :, 0:LAT], u_conv[:, :, 0:LAT], ACT.Copy))
                act.activation(u_hi[:, :, LAT:TOK], u_conv[:, :, LAT + GAP:UW], ACT.Copy).then_inc(u_rounded, 1)
                wait_done(act, q)
                act.wait_ge(scanned, n + 1)
                moved(act.activation(lru_y[:], part_psum(q, 0), ACT.Gelu_apprx_tanh), q)
                if last:
                    high(cg + 1, q, rows=4)
                else:
                    high(plus(cg, 1), plus(q, 1), rows=4)
                    block_input(plus(q, 1))
                act.preload_act_table_set("sigmoid_and_others")
                for d in range(2):
                    for g in range(2):
                        qd = plus(qg, 2 * d + g)
                        col = (V_BX if g else V_BA) + 8 * d
                        wait_done(act, qd)
                        for t in range(2):
                            for part, s, w in BOTH:
                                ins = act.activation(gates_r[:, 2 * d + g, t, s:s + w], tile_psum(qd, t, part),
                                                     ACT.Sigmoid, bias=vec[:, 1, bass.ds(col + 2 * n + t, 1)])
                                if t == 1 and part == 1:
                                    moved(ins, qd)
                                else:
                                    steps.mark(ins)
                    if d == 0:
                        high(plus(cg, 2), plus(qg, 1))
                steps.wait()
                wait_moved(act, plus(qg, 2))
                wait_moved(act, plus(qg, 3))
                for d in range(2):
                    for t in range(2):
                        steps.mark(act.activation(scan_h[d][:, t], gates_r[:, 2 * d, t], ACT.Tanh,
                                                  scale=lru_c[:, 0, bass.ds(8 * d + 2 * n + t, 1)]))
                high(plus(cg, 3), plus(qg, 3))
                steps.wait()
                for d in range(2):
                    for t in range(2):
                        steps.mark(act.activation(gates_r[:, 2 * d, t], gates_r[:, 2 * d, t], ACT.Exp,
                                                  scale=lru_c[:, 1, bass.ds(8 * d + 2 * n + t, 1)]))
                act.preload_act_table_set("sqrt_and_others")
                steps.wait()
                if last:
                    row_copy(10, 0)
                for k in range(4):
                    act.wait_ge(factor, 5 * n + (1 if k < 2 else k))
                    act.activation(a_squares[k % 2], gates_r[:, 2 * (k // 2), k % 2].rearrange("p (j n) -> p j n", n=CTX),
                                   ACT.Square).then_inc(a_sq, 1)
                for d in range(2):
                    act.wait_ge(factor, 5 * n + 3 + 2 * d)
                    act.activation(scan_h[d][:], scan_h[d][:], ACT.Sqrt).then_inc(root, 1)

            act.wait_ge(lruc_ready, 1)
            block_input(Q_LRU)
            high(C_LRU + 2, Q_LRU)
            with steps.loop(BLOCKS - 1, 22) as n:
                lru_block(n, (C_LRU + 1, 4, n), (Q_LRU + 1, PER_BLOCK, n), False)
            lru_block(BLOCKS - 1, C_OUT1 - 3, Q_OUT1 - 5, True)
            row_copy(10, 1)
            split_out(1, ONLY_LAT)
            act.preload_act_table_set("sqrt_and_others")
            row_copy(11, 0)
            prep(1, 1, ONLY_LAT)
            ffn(1, ONLY_LAT)
            for t in range(4):
                q = Q_FINAL + t
                wait_done(act, q)
                steps.link(act.activation(y_junk[:], duo(q)[:, 0:2, :].rearrange("p b n -> p (b n)"), ACT.Square,
                                          accum_out=ysum[:, 0, t:t + 1]))
                act.activation(ysum[:, 1, t:t + 1], ysum[:, 0, t:t + 1], ACT.Sqrt, bias=eps[:, 0:1], scale=1.0 / D
                               ).then_inc(y_rooted, 1)

        @block.vector
        def _(dve):
            steps = Steps(dve, dve_step)

            def part_psum(q, part):
                ps = duo(par(q))
                return ps[:, 0:2, :] if part == 0 else ps[:, 2, :].rearrange("p (t n) -> p t n", t=2)

            def tile_psum(q, t, part):
                ps = duo(par(q))
                return ps[:, t, :] if part == 0 else ps[:, 2, t * CTX:(t + 1) * CTX]

            def section(s, row):
                dve.wait_ge(mod_turned, 2 * whole(s) + 2 if s != 9 else 22)
                r = whole(row)
                ps, c0 = (mod_psum, 0) if s in (0, 1) else (vec_psum, turn_column(s))
                dve.tensor_tensor(mod[:, bass.ds(r, 1)].rearrange("p o m v -> p (o m) v"),
                                  ps[:, c0:c0 + 16].rearrange("p (m v) -> p m v", v=2),
                                  vec[:, 0, bass.ds(V_BMOD + 8 * r, 8)].unsqueeze(2).broadcast_to([P, 8, 2]),
                                  ALU.add).then_inc(mod_ready, 1)

            def add_squares(pair, n, width):
                dve.wait_ge(squared, whole(pair) + 1)
                for t in range(2):
                    ins = dve.tensor_tensor(sqsum[:, 0:width], sqsum[:, 0:width], sq[par(pair)][:, t, 0:width], ALU.add)
                    if t == 0:
                        steps.link(ins)
                ins.then_inc(summed, 1)
                dve.wait_ge(summed, whole(pair) + 1)

            def clear_sum():
                steps.link(dve.memset(sqsum[:], 0.0))

            def prep(layer, which, parts):
                n = 2 * layer + which
                width = parts[-1][1] + parts[-1][2]
                g = vec[:, 0, (V_NMIX if which == 0 else V_NFFN) + 8 * layer:][:, 0:8]
                sec = 6 * layer + 3 * which
                dve.wait_ge(mod_ready, [1, 6, 8, 11][n])
                steps.link(dve.scalar_tensor_tensor(out=gain[:, n], in0=mod[:, sec + 1], scalar=1.0,
                                                    in1=g.unsqueeze(2).broadcast_to([P, 8, 2]), op0=ALU.add,
                                                    op1=ALU.mult))
                tiles = width // P
                dve.wait_ge(rooted, n + 1)
                steps.link(dve.reciprocal(rms[:, 1, 0:tiles], rms[:, 0, 0:tiles]))
                if n == 0:
                    dve.wait_ge(consts_made, 1)
                dve.tensor_tensor(rdiag[:, 0:tiles], ident[:].unsqueeze(1).broadcast_to([P, tiles, P]),
                                  rms[:, 1, 0:tiles].unsqueeze(2).broadcast_to([P, tiles, P]), ALU.mult
                                  ).then_inc(diag_ready, 1)
                wait_done(dve, Q_STAT[layer][which])
                if n == 0:
                    section(1, SEC_FIRST[1])
                    dve.wait_ge(mod_ready, 2)

                def scale(m):
                    if m >= 2:
                        dve.wait_ge(hi_split, HI_SPLIT[n] + m - 1)
                    for part, s, w in parts:
                        ins = dve.scalar_tensor_tensor(out=normed[m % 2][:, s:s + w], in0=xres[:, m, s:s + w],
                                                       scalar=gain[:, n, m, part:part + 1],
                                                       in1=tile_psum(Q_STAT[layer][which], 0, part),
                                                       op0=ALU.mult, op1=ALU.mult)
                    ins.then_inc(scaled, 1)

                scale(0)
                for m in range(KT):
                    if m + 1 < KT:
                        if m >= 1:
                            dve.wait_ge(a_ready, A_READY[("prep", layer, which)] + m)
                        scale(m + 1)
                    else:
                        dve.wait_ge(scaled, 8 * n + 8)
                        moved(dve.memset(zero[:], 0.0), Q_STAT[layer][which])
                    dve.wait_ge(hi_split, HI_SPLIT[n] + m + 1)
                    for part, s, w in parts:
                        dst, hi, src = a_lo[:, m, s:s + w], a_hi[:, m, s:s + w], normed[m % 2][:, s:s + w]
                        if part == 0 and (layer, which) == (1, 0):
                            dst = dst.rearrange("p (c r) -> p r c", r=ROWS)
                            hi = hi.rearrange("p (c r) -> p r c", r=ROWS)
                            src = src.rearrange("p (r c) -> p r c", r=ROWS)
                        ins = dve.scalar_tensor_tensor(out=dst, in0=src, scalar=mod[:, sec, m, part:part + 1],
                                                       in1=hi.bitcast(F32), op0=ALU.add, op1=ALU.subtract)
                    ins.then_inc(a_ready, 1)

            dve.wait_ge(vec_turned, 1)
            steps.mark(dve.tensor_copy(vec[:, 0], vec_psum[:, 0:P]))
            dve.tensor_copy(vec[:, 1, 0:V_END], vec_psum[:, P:P + V_END]).then_inc(vec_ready, 1)
            dve.wait_ge(vec_ready, 1)
            steps.wait()
            lam = vec[:, 1, V_LAM:V_LAM + 16]
            steps.link(dve.tensor_scalar(lw[:, 1], lam, -1.0, 0.0, ALU.mult, ALU.max))
            steps.link(dve.tensor_scalar(lw[:, 2], lam, 0.0, None, ALU.max))
            dve.tensor_tensor(lw[:, 3], lw[:, 1], lw[:, 2], ALU.add).then_inc(l_w, 1)
            section(0, SEC_FIRST[0])
            dve.memset(gate2[:], 0.0).then_inc(gate2_zeroed, 1)
            for i in (0, 2):
                q = Q_TURN + i
                wait_done(dve, q)
                steps.mark(dve.tensor_copy(xres[:, 2 * i:2 * i + 2, 0:LAT], part_psum(q, 0)))
                moved(dve.tensor_copy(xres[:, 2 * i:2 * i + 2, LAT:TOK], part_psum(q, 1)), q)
            clear_sum()
            for n in range(4):
                add_squares(n, n, TOK)
            prep(0, 0, BOTH)

            dve.wait_ge(l_exp, 1)
            steps.link(dve.tensor_scalar(lw[:, 2], lw[:, 0], 2.0, None, ALU.add))
            steps.link(dve.reciprocal(lw[:, 2], lw[:, 2]))
            steps.link(dve.tensor_tensor(lw[:, 0], lw[:, 0], lw[:, 2], ALU.mult))
            steps.link(dve.tensor_tensor(lw[:, 2], lw[:, 0], lw[:, 0], ALU.mult))
            steps.link(dve.tensor_scalar(lw[:, 3], lw[:, 2], 1.0 / 15, 1.0 / 13, ALU.mult, ALU.add))
            for odd in (11, 9, 7, 5, 3, 1):
                steps.link(dve.tensor_tensor(lw[:, 3], lw[:, 3], lw[:, 2], ALU.mult))
                steps.link(dve.tensor_scalar(lw[:, 3], lw[:, 3], 1.0 / odd, None, ALU.add))
            steps.link(dve.tensor_tensor(lw[:, 3], lw[:, 3], lw[:, 0], ALU.mult))
            steps.link(dve.scalar_tensor_tensor(out=lw[:, 0], in0=lw[:, 3], scalar=2.0, in1=lw[:, 1], op0=ALU.mult,
                                                op1=ALU.add))
            steps.mark(dve.tensor_scalar(lru_c[:, 0], lw[:, 0], LRU_C, None, ALU.mult))
            dve.tensor_scalar(lru_c[:, 1], lw[:, 0], -LRU_C, None, ALU.mult).then_inc(lruc_ready, 1)
            dve.wait_ge(consts_made, 1)
            reset_row = resets[:].rearrange("p n c -> p (n c)")
            with steps.loop(HEADS, 30) as h:
                q0 = (Q_HEAD, PER_HEAD, h)
                dve.wait_ge(z_logged, h + 1)
                steps.link(dve.scalar_tensor_tensor(out=zg[:], in0=zg[:], scalar=0.0, in1=bcum[:], op0=ALU.min,
                                                    op1=ALU.subtract))
                steps.mark(dve.tensor_tensor_scan(bcum[:, 0], reset_row, zg[:, 0], 0.0, ALU.mult, ALU.add))
                steps.link(dve.tensor_tensor_scan(bcum[:, 1, ::-1], reset_row, zg[:, 1, ::-1], 0.0, ALU.mult, ALU.add))
                for d, last in ((0, CHUNK - 1), (1, 0)):
                    b4 = bcum[:, d].rearrange("p (n c) -> p n c", c=CHUNK)
                    ins = dve.tensor_tensor(zg[:, d].rearrange("p (n c) -> p n c", c=CHUNK),
                                            b4[:, :, last:last + 1].broadcast_to([P, NCH, CHUNK]), b4, ALU.subtract)
                    if d == 0:
                        steps.mark(ins)
                ins.then_inc(cum_ready, 1)
                dve.wait_ge(exps_ready, h + 1)
                q1 = plus(q0, 1)
                wait_done(dve, q1)
                for part, s, n in BOTH:
                    qp = tile_psum(q1, 0, part).unsqueeze(1).broadcast_to([P, 2, n])
                    steps.mark(dve.scalar_tensor_tensor(out=q_dec[:, :, s:s + n], in0=qp, scalar=DK_SCALE,
                                                        in1=q_dec[:, :, s:s + n], op0=ALU.mult, op1=ALU.mult))
                for n_, buf in enumerate((k_inv, k_end)):
                    for part, s, n in BOTH:
                        kp = tile_psum(q1, 1, part).unsqueeze(1).broadcast_to([P, 2, n])
                        ins = dve.tensor_tensor(buf[:, :, s:s + n], kp, buf[:, :, s:s + n], ALU.mult)
                        if n_ == 1 and part == 1:
                            moved(ins, q1)
                        else:
                            steps.mark(ins)
                qa = plus(q0, 4)
                wait_done(dve, qa)
                steps.link(dve.memset(att[:], 0.0))
                steps.mark(dve.memset(zero[:], 0.0))
                for d in range(2):
                    flat = duo(par(qa))[:].rearrange("p b n -> p (b n)")[:, d * TOK:(d + 1) * TOK]
                    ins = dve.copy_predicated(att[:, 6 * d:6 * d + 6], mask[:, d].bitcast(I32).unsqueeze(1).broadcast_to([P, 6, P]),
                                              flat.rearrange("p (t n) -> p t n", n=P))
                    if d == 0:
                        steps.mark(ins)
                moved(ins, qa)
                wait_moved(dve, qa)
                dve.tensor_tensor(att[:, 0:6], att[:, 0:6], att[:, 6:12], ALU.add).then_inc(att_ready, 1)
                for g, (d, chunks) in enumerate(STATE_GROUPS):
                    qu = plus(q0, 5 + g)
                    wait_done(dve, qu)
                    for s, n in enumerate(chunks):
                        u = state_psum(qu, s)
                        new = STATE_AFTER[d][n]
                        if STATE_BEFORE[d][n] is None:
                            ins = dve.tensor_copy(states[:, new], u)
                        else:
                            ins = dve.scalar_tensor_tensor(out=states[:, new], in0=states[:, STATE_BEFORE[d][n]],
                                                           scalar=decay[:, d, n:n + 1], in1=u, op0=ALU.mult,
                                                           op1=ALU.add)
                        if s == len(chunks) - 1:
                            moved(ins, qu)
                            wait_moved(dve, qu)
                        else:
                            steps.link(ins)
                section((SEC_HEAD, 1, h), (2, 1, h))
            def head_sum(h):
                dve.wait_ge(o_squared, h + 1)
                dve.tensor_tensor(o_sum[h % 2][:], o_sq[:, 0], o_sq[:, 1], ALU.add).then_inc(o_summed, 1)

            def split_low(layer, m, width):
                src = o_all if layer == 0 else lru_o
                dve.wait_ge(hi_split, m + 9 if layer == 0 else m + 27)
                dve.tensor_tensor(a_lo[:, m, 0:width], src[:, m, 0:width], a_hi[:, m, 0:width].bitcast(F32),
                                  ALU.subtract).then_inc(a_ready, 1)

            def apply_gate(h):
                wait_moved(dve, Q_NG + 2 * h + 1)
                o = o_all[:, 2 * h:2 * h + 2]
                dve.tensor_tensor(o, o, silu_g[h % 2][:], ALU.mult).then_inc(gated, 1)

            head_sum(0)
            head_sum(1)
            for h in range(HEADS):
                wait_moved(dve, Q_NG + 2 * h)
                dve.reciprocal(o_rinv[:, h], o_rinv[:, h]).then_inc(rinv_ready, 1)
                if h < 2:
                    head_sum(h + 2)
                dve.wait_ge(rinv_ready, h + 1)
                for t in range(2):
                    o = o_all[:, 2 * h + t]
                    steps.mark(dve.scalar_tensor_tensor(out=o, in0=o, scalar=vec[:, 1, V_HN + t:V_HN + t + 1],
                                                        in1=o_rinv[:, h], op0=ALU.mult, op1=ALU.mult))
                steps.wait()
                if h < HEADS - 1:
                    apply_gate(h)

            def project_out(layer, parts):
                for m in range(0 if layer == 0 else 6, KT):
                    if layer == 0 and m == 2:
                        apply_gate(HEADS - 1)
                    split_low(layer, m, parts[-1][1] + parts[-1][2])
                q0 = Q_OUT0 if layer == 0 else Q_OUT1
                if layer == 0:
                    section(6, 6)
                else:
                    section(9, 9)
                    section(10, 10)
                residual_loop(q0, layer, 2, parts, PAIRS[2 * layer + 1], permuted=layer == 1)

            def residual_loop(q0, layer, place_, parts, pair=None, permuted=False):
                if pair is not None:
                    clear_sum()
                with steps.loop(2, 2 * (2 * len(parts) - 1 + (pair is not None))) as i:
                    for b in range(2):
                        q, tile = (q0 + b, 2, i), 4 * i + 2 * b
                        wait_done(dve, q)
                        for t in range(2):
                            for part, s, w in parts:
                                xt = xres[:, bass.ds(tile + t, 1), s:s + w].rearrange("p o n -> p (o n)")
                                src = tile_psum(q, t, part)
                                if permuted:
                                    xt = xt.rearrange("p (r c) -> p r c", r=ROWS)
                                    src = src.rearrange("p (c r) -> p r c", r=ROWS)
                                g = mod[:, 6 * layer + place_, bass.ds(tile + t, 1), part:part + 1]
                                ins = dve.scalar_tensor_tensor(out=xt, in0=src, scalar=g.rearrange("p o n -> p (o n)"),
                                                               in1=xt, op0=ALU.mult, op1=ALU.add)
                                if t == 1 and part == parts[-1][0]:
                                    moved(ins, q)
                                else:
                                    steps.mark(ins)
                        wait_moved(dve, q)
                        if pair is not None:
                            add_squares((pair + b, 2, i), (b, 2, i), parts[-1][1] + parts[-1][2])

            def ffn(layer, parts):
                q = Q_FFN0 if layer == 0 else Q_FFN1
                width = parts[-1][1] + parts[-1][2]
                for part, (first, n) in enumerate(FFN_PARTS):
                    with steps.loop(n // 2, 2 if len(parts) == 2 else 1) as i:
                        wait_moved(dve, (q, 2, i))
                        wait_done(dve, (q + 1, 2, i))
                        for k, s, w in parts:
                            ins = dve.tensor_tensor(hid[:, :, s:s + w], part_psum(q + 1, k), gate[:, :, s:s + w], ALU.mult)
                            if k == parts[-1][0]:
                                moved(ins, q + 1)
                            else:
                                steps.mark(ins)
                        wait_moved(dve, (q + 1, 2, i))
                        hh = h_hi[:, bass.ds(2 * i, 2), 0:width]
                        steps.link(dve.tensor_copy(hh, hid[:, :, 0:width]))
                        dve.tensor_tensor(h_lo[:, bass.ds(2 * i, 2), 0:width], hid[:, :, 0:width], hh.bitcast(F32),
                                          ALU.subtract).then_inc(hid_ready, 1)
                        dve.wait_ge(hid_ready, HID[layer][part] + i + 1)
                    q += n
                    residual_loop(q, layer, 5, parts, PAIRS[2] if layer == 0 and part == len(FFN_PARTS) - 1 else None)
                    q += 4

            project_out(0, BOTH)
            prep(0, 1, BOTH)
            section(7, 7)
            ffn(0, BOTH)
            prep(1, 0, BOTH)
            section(8, 8)
            dve.wait_ge(a_ready, A_READY[("prep", 1, 0)] + KT)
            dve.memset(u_pad[:, :, 0:2], 0.0).then_inc(scans_added, 1)
            steps.mark(dve.memset(u_pad[:, :, 2 + LAT:2 + LAT + GAP], 0.0))
            dve.memset(u_pad[:, :, 2 + UW:UW + 4], 0.0).then_inc(scanned, 1)
            dve.wait_ge(scanned, 1)
            def conv(n, q):
                wait_moved(dve, q)
                for j in range(CONV_W):
                    for t in range(2):
                        col = vec[:, 1, bass.ds(V_CW + 8 * j + 2 * n + t, 1)]
                        if j == 0:
                            ins = dve.tensor_scalar(u_conv[:, t], u_pad[:, t, 0:UW], col,
                                                    vec[:, 1, bass.ds(V_CB + 2 * n + t, 1)], ALU.mult, ALU.add)
                        else:
                            ins = dve.scalar_tensor_tensor(out=u_conv[:, t], in0=u_pad[:, t, j:j + UW], scalar=col,
                                                           in1=u_conv[:, t], op0=ALU.mult, op1=ALU.add)
                        if j == CONV_W - 1 and t == 1:
                            ins.then_inc(conv_done, 1)
                        else:
                            steps.mark(ins)
                    if j < CONV_W - 1:
                        steps.wait()

            def lru_block(n, q, last):
                qg = plus(q, 1 if last else 2)
                dve.wait_ge(scanned, n + 1)
                dve.wait_ge(u_rounded, n + 1)
                steps.mark(dve.tensor_tensor(u_lo[:, :, 0:LAT], u_conv[:, :, 0:LAT], u_hi[:, :, 0:LAT].bitcast(F32),
                                             ALU.subtract))
                dve.tensor_tensor(u_lo[:, :, LAT:TOK], u_conv[:, :, LAT + GAP:UW], u_hi[:, :, LAT:TOK].bitcast(F32),
                                  ALU.subtract).then_inc(u_ready, 1)
                for d in range(2):
                    wait_moved(dve, plus(qg, 1 + 2 * d))
                    g = gates_r[:, 2 * d + 1]
                    steps.mark(dve.tensor_tensor(g[:, :, 0:LAT], g[:, :, 0:LAT], u_conv[:, :, 0:LAT], ALU.mult))
                    ins = dve.tensor_tensor(g[:, :, LAT:TOK], g[:, :, LAT:TOK], u_conv[:, :, LAT + GAP:UW], ALU.mult)
                    if d == 0:
                        steps.mark(ins)
                ins.then_inc(factor, 1)
                if not last:
                    dve.wait_ge(factor, 5 * n + 1)
                    conv(n + 1, plus(q, 1))
                for k in range(4):
                    dve.wait_ge(a_sq, 4 * n + k + 1)
                    h = scan_h[k // 2][:, k % 2].rearrange("p (j n) -> p j n", n=CTX)
                    dve.scalar_tensor_tensor(out=h, in0=a_squares[k % 2], scalar=1.0, in1=h, op0=ALU.add,
                                             op1=ALU.mult).then_inc(factor, 1)
                dve.wait_ge(factor, 5 * n + 5)
                for d in range(2):
                    dve.wait_ge(root, 2 * n + d + 1)
                    g = gates_r[:, 2 * d + 1]
                    steps.link(dve.tensor_tensor(g, g, scan_h[d][:], ALU.mult))
                    order_ = slice(None, None, -1) if d else slice(None)
                    for t in range(2):
                        a_, b_, o_ = gates_r[:, 2 * d, t], gates_r[:, 2 * d + 1, t], scan_h[d][:, t]
                        cx = [v[:, LAT:TOK][:, order_] for v in (o_, a_, b_)]
                        steps.mark(dve.tensor_tensor_scan(*cx, 0.0, ALU.mult, ALU.add))
                    steps.wait()
                    for t in range(2):
                        a_, b_, o_ = gates_r[:, 2 * d, t], gates_r[:, 2 * d + 1, t], scan_h[d][:, t]
                        lt = [v[:, 0:LAT][:, order_] for v in (o_, a_, b_)]
                        last_ = o_[:, LAT:LAT + 1] if d else o_[:, TOK - 1:TOK]
                        steps.mark(dve.tensor_tensor_scan(*lt, last_, ALU.mult, ALU.add))
                    steps.wait()
                dve.tensor_tensor(scan_h[1][:, :, 0:LAT], scan_h[0][:, :, 0:LAT], scan_h[1][:, :, 0:LAT],
                                  ALU.add).then_inc(scans_added, 1)
                dve.wait_ge(scans_added, n + 2)
                wait_moved(dve, q)
                dve.tensor_tensor(lru_o[:, bass.ds(2 * n, 2)], scan_h[1][:, :, 0:LAT], lru_y[:], ALU.mult
                                  ).then_inc(scanned, 1)

            conv(0, Q_LRU)
            with steps.loop(BLOCKS - 1, 21) as n:
                lru_block(n, (Q_LRU + 1, PER_BLOCK, n), False)
            lru_block(BLOCKS - 1, Q_OUT1 - 5, True)
            project_out(1, ONLY_LAT)
            prep(1, 1, ONLY_LAT)
            section(11, 11)
            ffn(1, ONLY_LAT)
            dve.wait_ge(final_g_loaded, 16)
            for t in range(4):
                q = Q_FINAL + t
                dve.wait_ge(y_rooted, t + 1)
                steps.link(dve.reciprocal(ysum[:, 2, t:t + 1], ysum[:, 1, t:t + 1]))
                moved(dve.scalar_tensor_tensor(out=y_rows[t][:], in0=duo(q)[:, 0:2, :].rearrange("p b n -> p (b n)"),
                                               scalar=ysum[:, 2, t:t + 1], in1=final_g[:], op0=ALU.mult,
                                               op1=ALU.mult), q)


SCAN = [[8, 9, 10, 11, 0, 1, 2, 3, 4, 5, 6, 7], [11, 10, 9, 8, 7, 6, 5, 4, 3, 2, 1, 0]]
STATE_BASE = [11, 0]
STATE_AFTER = [{n: STATE_BASE[d] + s for s, n in enumerate(SCAN[d][:11])} for d in range(2)]
STATE_BEFORE = [{n: (STATE_BASE[d] + s - 1 if s else None) for s, n in enumerate(SCAN[d])} for d in range(2)]
STATE_GROUPS = [(1, SCAN[1][0:6]), (1, SCAN[1][6:11]), (0, SCAN[0][0:6]), (0, SCAN[0][6:11])]
HID = [[0, 4, 8], [11, 15, 19]]
HI_SPLIT = [0, 16, 24, 34]
PAIRS = [0, 4, 8, 12]
SUMMED = [4, 8, 12, 16]
A_ORDER = {("prep", 0, 0): 0, ("out", 0): 1, ("prep", 0, 1): 2, ("prep", 1, 0): 3, ("out", 1): 4, ("prep", 1, 1): 5}


_INS = ["x", "c", "ctx", "c_ctx", "norm_mix_g", "norm_ffn_g", "w_mod", "b_mod", "gla_w_in", "gla_gate_w1",
        "gla_gate_w2", "gla_gate_b", "gla_head_norm_g", "gla_w_out", "lru_w_in", "lru_conv_w", "lru_conv_b",
        "lru_gate_a_w", "lru_gate_a_b", "lru_gate_x_w", "lru_gate_x_b", "lru_lambda", "lru_w_out", "ffn_w1",
        "ffn_w3", "ffn_w2", "final_norm_g"]


def kernel(**inputs):
    import numpy as _np
    import concourse.bacc as _bacc
    from concourse import mybir as _mybir
    from concourse.bass_utils import run_bass_kernel_spmd as _run

    nc = _bacc.Bacc("TRN2", target_bir_lowering=False, num_devices=1)
    arrays, args = {}, []
    for name in _INS:
        a = _np.ascontiguousarray(inputs[name])
        arrays[f"in_{name}_dram"] = a
        args.append(nc.dram_tensor(f"in_{name}_dram", a.shape, _mybir.dt.from_np(a.dtype), kind="ExternalInput").ap())
    args.append(nc.dram_tensor("out_dram", (1, LAT, D), _mybir.dt.float32, kind="ExternalOutput").ap())
    build(nc, *args)
    r = _run(nc, [arrays], core_ids=[0])
    return r.results[0]["out_dram"]
```
